# Optimizing a Trainium2 kernel written in Bass

```python
import jax, jax.numpy as jnp
from jax import lax
import numpy as np

D_MODEL = 2048
BATCH = 1
SEQ = 512
DEPTH = 1
DEC_BATCH = 8
DEC_SEQ = 8
PAST_LEN = 2048
PAGE_SIZE = 128

POOL_WIDTH = D_MODEL // 2
POOL_GROUPS = 4
POOL_GW = POOL_WIDTH // POOL_GROUPS
POOL_WINDOWS = (2, 4, 8, 16)
POOL_STATE = max(POOL_WINDOWS) - 1
HEAD_DIM = 128
N_HEADS = (D_MODEL - POOL_WIDTH) // HEAD_DIM
ATTN_WIDTH = N_HEADS * HEAD_DIM
IDX_HEADS = 16
IDX_DIM = 128
TOPK_MAX = 256
Q_BLOCK = 128
ROPE_THETA = 10000.0
D_FF = ((8 * D_MODEL // 3 + 255) // 256) * 256
EPS = 1e-6
NEG = -1e30
MIX_SPLITS = (POOL_WIDTH, ATTN_WIDTH, ATTN_WIDTH, ATTN_WIDTH, IDX_HEADS * IDX_DIM, IDX_DIM, IDX_HEADS)
D_IN = sum(MIX_SPLITS)

kernel_name = "hymba_pool_dsa_decoder_step"

def rmsnorm(x, g):
    xf = x.astype(jnp.float32)
    y = xf * lax.rsqrt(jnp.mean(xf * xf, axis=-1, keepdims=True) + EPS)
    return (y * g.astype(jnp.float32)).astype(x.dtype)

def rope(x, pos):
    half = x.shape[-1] // 2
    inv = ROPE_THETA ** (-jnp.arange(half, dtype=jnp.float32) / half)
    ang = pos.astype(jnp.float32)[:, None] * inv[None, :]
    cos = jnp.cos(ang)[None, :, None, :]
    sin = jnp.sin(ang)[None, :, None, :]
    xf = x.astype(jnp.float32)
    x1, x2 = xf[..., :half], xf[..., half:]
    return jnp.concatenate([x1 * cos - x2 * sin, x2 * cos + x1 * sin], axis=-1).astype(x.dtype)

def mix_inputs(h, w_in, pos):
    B, T = h.shape[0], h.shape[1]
    u = h @ w_in
    offs = [int(o) for o in np.cumsum(MIX_SPLITS)[:-1]]
    up, q, k, v, qi, ki, wi = jnp.split(u, offs, axis=-1)
    q = rope(q.reshape(B, T, N_HEADS, HEAD_DIM), pos)
    k = rope(k.reshape(B, T, N_HEADS, HEAD_DIM), pos)
    v = v.reshape(B, T, N_HEADS, HEAD_DIM)
    qi = rope(qi.reshape(B, T, IDX_HEADS, IDX_DIM), pos)
    ki = rope(ki[:, :, None, :], pos)[:, :, 0]
    wi = wi * (IDX_HEADS ** -0.5)
    return up, q, k, v, qi, ki, wi

def pool_mixer(up, prefix, pos, w_pool, s_pool):
    B, T = up.shape[0], up.shape[1]
    P = POOL_STATE
    ext = jnp.concatenate([prefix, up], axis=1)
    c = jnp.pad(jnp.cumsum(ext.astype(jnp.float32), axis=1), ((0, 0), (1, 0), (0, 0)))
    means = []
    for g, w in enumerate(POOL_WINDOWS):
        sl = slice(g * POOL_GW, (g + 1) * POOL_GW)
        s = c[:, P + 1:P + 1 + T, sl] - c[:, P + 1 - w:P + 1 - w + T, sl]
        cnt = jnp.minimum(w, pos + 1).astype(jnp.float32)[None, :, None]
        means.append(s / cnt)
    mean = jnp.stack(means, axis=2)
    d = (mean - up.astype(jnp.float32).reshape(B, T, POOL_GROUPS, POOL_GW)).astype(up.dtype)
    y = jnp.einsum('btgc,gcd->btgd', d, w_pool).reshape(B, T, POOL_WIDTH) * s_pool
    return y, ext[:, -P:]

def index_scores(qi, ki, wi):
    s = jnp.einsum('bqhe,bse->bqhs', qi, ki, preferred_element_type=jnp.float32) * (IDX_DIM ** -0.5)
    return jnp.einsum('bqhs,bqh->bqs', jax.nn.relu(s), wi.astype(jnp.float32))

def attend(q, kg, vg, valid):
    s = jnp.einsum('bqhd,bqkhd->bqhk', q, kg, preferred_element_type=jnp.float32) * (HEAD_DIM ** -0.5)
    s = jnp.where(valid[:, :, None, :], s, NEG)
    p = jax.nn.softmax(s, axis=-1).astype(vg.dtype)
    return jnp.einsum('bqhk,bqkhd->bqhd', p, vg)

def sparse_attn_prompt(q, k, v, qi, ki, wi):
    B, S = q.shape[0], q.shape[1]
    topk = min(TOPK_MAX, S // 4)
    nb = S // Q_BLOCK
    bi = jnp.arange(B)[:, None, None]
    key_pos = jnp.arange(S)

    def blk(args):
        qb, qib, wib, start = args
        qpos = start + jnp.arange(Q_BLOCK)
        sc = index_scores(qib, ki, wib)
        sc = jnp.where((key_pos[None, :] <= qpos[:, None])[None], sc, -jnp.inf)
        _, idx = lax.top_k(sc, topk)
        valid = idx <= qpos[None, :, None]
        return attend(qb, k[bi, idx], v[bi, idx], valid)

    def to_blocks(a):
        return jnp.moveaxis(a.reshape((B, nb, Q_BLOCK) + a.shape[2:]), 1, 0)

    starts = jnp.arange(nb) * Q_BLOCK
    out = lax.map(blk, (to_blocks(q), to_blocks(qi), to_blocks(wi), starts))
    return jnp.moveaxis(out, 0, 1).reshape(B, S, ATTN_WIDTH)

def sparse_attn_sample(q, k, v, qi, ki, wi, cache_k, cache_v, cache_idx_k, page_table, layer):
    B, T = q.shape[0], q.shape[1]
    n_pages = page_table.shape[1]
    past = n_pages * PAGE_SIZE
    L = past + T
    topk = min(TOPK_MAX, L // 4)
    bi = jnp.arange(B)[:, None, None]
    ik_past = cache_idx_k[layer, page_table].reshape(B, past, IDX_DIM)
    ik_all = jnp.concatenate([ik_past, ki], axis=1)
    qpos = past + jnp.arange(T)
    sc = index_scores(qi, ik_all, wi)
    sc = jnp.where((jnp.arange(L)[None, :] <= qpos[:, None])[None], sc, -jnp.inf)
    _, idx = lax.top_k(sc, topk)
    valid = idx <= qpos[None, :, None]
    in_past = (idx < past)[..., None, None]
    pidx = jnp.minimum(idx, past - 1)
    phys = page_table[bi, pidx // PAGE_SIZE]
    off = pidx % PAGE_SIZE
    nidx = jnp.clip(idx - past, 0, T - 1)
    kg = jnp.where(in_past, cache_k[layer, phys, off], k[bi, nidx])
    vg = jnp.where(in_past, cache_v[layer, phys, off], v[bi, nidx])
    return attend(q, kg, vg, valid).reshape(B, T, ATTN_WIDTH)

def block(x, pos, pool_prefix, attn_fn, g_mix, w_in, w_pool, s_pool, w_out, g_ffn, w_gate, w_up, w_down):
    h = rmsnorm(x, g_mix)
    up, q, k, v, qi, ki, wi = mix_inputs(h, w_in, pos)
    y_pool, pool_state = pool_mixer(up, pool_prefix, pos, w_pool, s_pool)
    y_attn = attn_fn(q, k, v, qi, ki, wi)
    x = x + jnp.concatenate([y_pool, y_attn], axis=-1) @ w_out
    h2 = rmsnorm(x, g_ffn)
    x = x + (jax.nn.silu(h2 @ w_gate) * (h2 @ w_up)) @ w_down
    return x, k, v, ki, pool_state

def setup_inputs(seed: int = 0) -> dict:
    key = jax.random.key(seed)
    ks = jax.random.split(key, 20)
    f32 = jnp.float32
    n_pages = PAST_LEN // PAGE_SIZE
    n_used = DEC_BATCH * n_pages
    n_phys = n_used + max(1, n_used // 4)
    nrm = lambda k, shape, scale=1.0: jax.random.normal(k, shape, f32) * scale
    page_table = jax.random.permutation(ks[6], n_phys)[:n_used].reshape(DEC_BATCH, n_pages).astype(jnp.int32)
    return {
        'x_prompt': nrm(ks[0], (BATCH, SEQ, D_MODEL)),
        'x_sample': nrm(ks[1], (DEC_BATCH, DEC_SEQ, D_MODEL)),
        'cache_k': nrm(ks[2], (DEPTH, n_phys, PAGE_SIZE, N_HEADS, HEAD_DIM)),
        'cache_v': nrm(ks[3], (DEPTH, n_phys, PAGE_SIZE, N_HEADS, HEAD_DIM)),
        'cache_idx_k': nrm(ks[4], (DEPTH, n_phys, PAGE_SIZE, IDX_DIM)),
        'state_pool': nrm(ks[5], (DEPTH, DEC_BATCH, POOL_STATE, POOL_WIDTH)),
        'page_table': page_table,
        'g_mix': 1.0 + nrm(ks[7], (DEPTH, D_MODEL), 0.02),
        'w_in': nrm(ks[8], (DEPTH, D_MODEL, D_IN), D_MODEL ** -0.5),
        'w_pool': nrm(ks[9], (DEPTH, POOL_GROUPS, POOL_GW, POOL_GW), POOL_GW ** -0.5),
        's_pool': 1.0 + nrm(ks[10], (DEPTH, POOL_WIDTH), 0.1),
        'w_out': nrm(ks[11], (DEPTH, D_MODEL, D_MODEL), D_MODEL ** -0.5),
        'g_ffn': 1.0 + nrm(ks[12], (DEPTH, D_MODEL), 0.02),
        'w_gate': nrm(ks[13], (DEPTH, D_MODEL, D_FF), D_MODEL ** -0.5),
        'w_up': nrm(ks[14], (DEPTH, D_MODEL, D_FF), D_MODEL ** -0.5),
        'w_down': nrm(ks[15], (DEPTH, D_FF, D_MODEL), D_FF ** -0.5),
        'g_final': 1.0 + nrm(ks[16], (D_MODEL,), 0.02),
    }

def reference(x_prompt, x_sample, cache_k, cache_v, cache_idx_k, state_pool, page_table,
              g_mix, w_in, w_pool, s_pool, w_out, g_ffn, w_gate, w_up, w_down, g_final):
    B, S = x_prompt.shape[0], x_prompt.shape[1]
    DB, T = x_sample.shape[0], x_sample.shape[1]
    past = page_table.shape[1] * PAGE_SIZE
    pos_p = jnp.arange(S)
    pos_s = past + jnp.arange(T)
    zero_prefix = jnp.zeros((B, POOL_STATE, POOL_WIDTH), x_prompt.dtype)

    xp, xs = x_prompt, x_sample
    kp_l, vp_l, ikp_l, pp_l = [], [], [], []
    ks_l, vs_l, iks_l, ps_l = [], [], [], []
    for l in range(DEPTH):
        lw = (g_mix[l], w_in[l], w_pool[l], s_pool[l], w_out[l], g_ffn[l], w_gate[l], w_up[l], w_down[l])
        xp, kp, vp, ikp, pp = block(xp, pos_p, zero_prefix, sparse_attn_prompt, *lw)

        def attn_s(q, k, v, qi, ki, wi, l=l):
            return sparse_attn_sample(q, k, v, qi, ki, wi, cache_k, cache_v, cache_idx_k, page_table, l)

        xs, ksm, vsm, iks, ps = block(xs, pos_s, state_pool[l], attn_s, *lw)
        kp_l.append(kp); vp_l.append(vp); ikp_l.append(ikp); pp_l.append(pp)
        ks_l.append(ksm); vs_l.append(vsm); iks_l.append(iks); ps_l.append(ps)

    y_prompt = rmsnorm(xp, g_final)
    y_sample = rmsnorm(xs, g_final)
    k_prompt = jnp.stack(kp_l); v_prompt = jnp.stack(vp_l)
    idx_k_prompt = jnp.stack(ikp_l); pool_prompt = jnp.stack(pp_l)
    k_sample = jnp.stack(ks_l); v_sample = jnp.stack(vs_l)
    idx_k_sample = jnp.stack(iks_l); pool_sample = jnp.stack(ps_l)
    return (y_prompt, y_sample, k_prompt, v_prompt, idx_k_prompt, pool_prompt, k_sample, v_sample, idx_k_sample, pool_sample)


_drawn_inputs = setup_inputs


def setup_inputs(seed=0):
    import zlib

    import numpy as np

    out = dict(_drawn_inputs(seed))
    spreads = {}
    factors = {'g_mix': 2.817, 'g_ffn': 4.476, 'g_final': 2.901}
    for name, (base, spread) in spreads.items():
        noise = np.random.default_rng([zlib.crc32(name.encode()), seed]).standard_normal(out[name].shape)
        drawn = base * np.exp(spread * noise) if base else spread * noise
        out[name] = __import__('jax').numpy.asarray(drawn.astype(out[name].dtype))
    for name, factor in factors.items():
        out[name] = (out[name] * factor).astype(out[name].dtype)
    return out
```

```python
from contextlib import ExitStack

import concourse.bass as bass
from concourse import mybir

F32 = mybir.dt.float32
F32R = mybir.dt.float32r
I32 = mybir.dt.int32
ALU = mybir.AluOpType
ACT = mybir.ActivationFunctionType
AX = mybir.AxisListType

P = 128
D = 2048
KT = D // P
SEQ = 512
DB = 8
DT = 8
NS = DB * DT
NT = SEQ + NS
HALF = NT // 2
PAGE = 128
NPG = 16
PAST = NPG * PAGE
NKEY = PAST + DT
POOL_W = 1024
NPOOL = POOL_W // P
WINDOWS = (2, 4, 8, 16)
STATE = 15
HD = 128
NH = 8
IH = 16
TOPK_P = 128
TOPK_S = 256
DFF = 5632
FT = 4
CHUNKS = DFF // (FT * P)
EPS = 1e-6
PAST_MASK = -3.0e38
TAKEN = -3.4e38
HIDE = -1.0e30
ATT_SCALE = float(HD) ** -0.5
IDX_SCALE = float(HD) ** -0.5 * float(IH) ** -0.5

C_UP, C_Q, C_K, C_V, C_QI, C_KI = 0, 1024, 2048, 3072, 4096, 6144
C_WI_TILE = C_KI + P + IH - P

S_KI, S_WI, S_QI = 0, 1, 2
S_K = S_QI + IH
S_V = S_K + NH
S_Q = S_V + NH
S_UP = S_Q + NH
S_POOL = S_UP + NPOOL
S_OUT = S_POOL + 1
S_FF = S_OUT + KT
PER_CHUNK = 3 * FT
N_SLOTS = S_FF + CHUNKS * PER_CHUNK
G_POOL = S_POOL
G_OUT = G_POOL + NPOOL
G_FF = G_OUT + KT
READ_CHUNK = FT + KT

BLOCKS = (1, 2, 3)
BLK_OFF = {1: 0, 2: 256, 3: 640}
BLK_W = 1152

K_IDENT, K_ONES, K_COS, K_SIN, K_REP, K_DIAG, K_TRI, K_NEW, K_CNT = 0, 128, 256, 832, 1408, 1536, 1600, 1728, 1736
K_ALL = K_CNT + 64


def constants():
    import numpy as np

    c = np.zeros((P, K_ALL), np.float32)
    c[:, K_IDENT:K_IDENT + P] = np.eye(P)
    c[:, K_ONES:K_ONES + P] = 1.0
    pos = np.concatenate([np.arange(SEQ), np.tile(PAST + np.arange(DT), DB)]).astype(np.float32)
    inv = (10000.0 ** (-(np.arange(HD // 2) / (HD // 2)))).astype(np.float32)
    ang = (pos[None, :] * inv[:, None]).astype(np.float32).astype(np.float64)
    c[:, K_COS:K_COS + NT] = np.tile(np.cos(ang), (2, 1))
    c[:, K_SIN:K_SIN + NT] = np.concatenate([np.sin(ang), -np.sin(ang)], 0)
    for h in range(IH):
        c[h, K_REP + h * DT:K_REP + (h + 1) * DT] = 1.0
    for p in range(P):
        c[p, K_DIAG + p % DT:K_DIAG + NS:DT] = 1.0
    c[:, K_TRI:K_TRI + P] = np.where(np.arange(P)[None, :] > np.arange(P)[:, None], PAST_MASK, 0.0)
    for r in range(NS):
        c[r, K_NEW:K_NEW + DT] = np.where(np.arange(DT) > r % DT, PAST_MASK, 0.0)
    for g, w in enumerate(WINDOWS):
        for t in range(STATE):
            c[:, K_CNT + g * 16 + t] = w / min(w, t + 1)
    return c


def build(nc, x_prompt, x_sample, cache_k, cache_v, cache_idx_k, state_pool, page_table, g_mix, w_in,
          w_pool, s_pool, w_out, g_ffn, w_gate, w_up, w_down, g_final, const, outs):
    (y_prompt, y_sample, k_prompt, v_prompt, idx_k_prompt, pool_prompt,
     k_sample, v_sample, idx_k_sample, pool_sample) = outs
    n_phys = cache_k.shape[1]
    ctx = ExitStack()
    with ctx:
        base = (nc.sbuf_base + 31) // 32 * 32
        OFF_A = base
        OFF_W = OFF_A + 2 * KT * NT * 4
        OFF_C = OFF_W + 6 * D * 4
        OFF_M = OFF_C + KT * NT * 4

        def at(name, offset, shape, dt=F32):
            return nc.alloc_sbuf_tensor_at(name, shape, dt, offset=offset)

        class Place:

            def __init__(self, offset):
                self.offset = offset

            def __call__(self, name, shape, dt=F32):
                size = 4
                for n in shape[1:]:
                    size *= n
                t = at(name, self.offset, shape, dt)
                self.offset += (size + 31) // 32 * 32
                return t

        in_a = Place(OFF_A)
        HH = in_a("HH", [P, KT, NT], F32R)
        HL = in_a("HL", [P, KT, NT], F32R)
        xin = at("xin", OFF_A, [P, 5, D])
        yrow = at("yrow", OFF_A, [P, 5, D])
        in_w = Place(OFF_W)
        raw = in_w("raw", [P, 2, D])
        wh = in_w("wh", [P, 2, D], F32R)
        wl = in_w("wl", [P, 2, D], F32R)
        in_w = Place(OFF_W)
        kpage = in_w("kpage", [P, 4, NH * HD])
        vpage = in_w("vpage", [P, 4, NH * HD])
        kturn = in_w("kturn", [P, 2, NH * HD])
        sx = in_w("sx", [P, (NPG + 1) * NS])
        vprompt = at("vprompt", OFF_W + 4 * NH * HD * 4, [P, 4, NH * HD])
        in_w = Place(OFF_W + 8 * NH * HD * 4)
        px = in_w("px", [P, 2, SEQ])
        pxt = in_w("pxt", [P, 2, SEQ])
        XT = at("XT", OFF_C, [P, KT, NT])
        qkT = at("qkT", OFF_C, [P, 2 * NH, NT])
        in_c = Place(OFF_C)
        ikraw = in_c("ikraw", [P, 4, 4 * HD])
        ikT = in_c("ikT", [P, 2, NKEY])
        irelu = in_c("irelu", [P, 3, 512])
        in_c = Place(OFF_C)
        DH = in_c("DH", [P, NPOOL, NT], F32R)
        DL = in_c("DL", [P, NPOOL, NT], F32R)
        in_m = Place(OFF_M)
        cst = in_m("cst", [P, K_ALL])
        gains = in_m("gains", [P, 4, KT])
        pages = in_m("pages", [1, DB * NPG], I32)
        ffn_from = in_m.offset
        T2 = in_m("T2", [P, 2, 16 + NT])
        rtmp = in_m("rtmp", [P, NT])
        kiT = in_m("kiT", [P, NT])
        wtok = in_m("wtok", [P, 4, IH])
        pscore = in_m("pscore", [P, BLK_W])
        sscore = in_m("sscore", [NS, NKEY])
        small = in_m("small", [P, 192])
        stage_at = in_m.offset
        stage = in_m("stage", [P, 2, 5, P])
        maskT = at("maskT", stage_at, [P, NPG + 1, NS])
        arena = in_m.offset
        in_m = Place(arena)
        sq = in_m("sq", [P, 2, NT])
        ss = in_m("ss", [P, NT])
        rstd = in_m("rstd", [P, NT])
        xn = in_m("xn", [P, 2, NT])
        grow = in_m("grow", [3 * KT + NPOOL, P])
        in_m = Place(arena)
        wiT = in_m("wiT", [IH, NT])
        wrow = in_m("wrow", [P, 576])
        pr = in_m("pr", [P, BLK_W])
        qis = in_m("qis", [P, DB, P])
        in_m = Place(arena)
        staterow = in_m("staterow", [DB * STATE, POOL_W])
        ust = in_m("ust", [NS, 2, P])
        upt = in_m("upt", [STATE, 2, P])
        ES = in_m("ES", [P, DB, STATE + DT + 1])
        win = in_m("win", [P, 2, 16 + SEQ])
        stateT = in_m("stateT", [P, NPOOL, DB * STATE])
        wins = in_m("wins", [P, 2, DB, STATE + DT + 1])
        in_m = Place(arena)
        qkb = in_m("qkb", [P, 2 * NH, DT])
        vnew = in_m("vnew", [DT, NH * HD])
        sm = in_m("sm", [P, 6, NS])
        dg = in_m("dg", [NS, NS])
        DF = in_m("DF", [P, 2, NT])
        in_m = Place(ffn_from)
        GH = in_m("GH", [P, FT, NT], F32R)
        GL = in_m("GL", [P, FT, NT], F32R)
        sg = in_m("sg", [P, 2, NT])
        hid = in_m("hid", [P, 2, NT])

        ident = cst[:, K_IDENT:K_IDENT + P]
        ones = cst[:, K_ONES:K_ONES + P]

        PS = ctx.enter_context(nc.psum_tensor("PS", [P, 8, 512], F32))

        def pair(g, rows=P):
            return PS[0:rows, 2 * (g % 2):2 * (g % 2) + 2, 0:HALF]

        def halves(ap):
            return ap.rearrange("p (a n) -> p a n", a=2)

        x_keep = nc.dram_tensor("x_keep", [P, KT * NT], F32, kind="Internal").ap()
        d_keep = nc.dram_tensor("d_keep", [P, NPOOL * NT], F32, kind="Internal").ap()

        def sem(name):
            return ctx.enter_context(nc.semaphore(name))

        const_in, pages_in, gain_in = sem("const_in"), sem("pages_in"), sem("gain_in")
        x_in = [sem(f"x_in{i}") for i in range(5)]
        raw_in = [sem(f"raw_in{i}") for i in range(2)]
        ik_in = [sem(f"ik_in{i}") for i in range(4)]
        k_in = [sem(f"k_in{i}") for i in range(4)]
        v_in = [sem(f"v_in{i}") for i in range(4)]
        vnew_in, vprompt_in, state_in = sem("vnew_in"), sem("vprompt_in"), sem("state_in")
        x_kept, x_back, d_kept = sem("x_kept"), sem("x_back"), sem("d_kept")
        d_back = [sem(f"d_back{i}") for i in range(2)]
        gains_turned, gains_ready = sem("gains_turned"), sem("gains_ready")
        high_ready, low_ready, slot_done = sem("high_ready"), sem("low_ready"), sem("slot_done")
        psum_read = sem("psum_read")
        x_turned, x_copied_act, x_copied_dve = sem("x_turned"), sem("x_copied_act"), sem("x_copied_dve")
        sq_ready, sq_added, ss_bcast, inv_ready, rstd_ready = (
            sem("sq_ready"), sem("sq_added"), sem("ss_bcast"), sem("inv_ready"), sem("rstd_ready"))
        xn_ready, norm_high, norm_low = sem("xn_ready"), sem("norm_high"), sem("norm_low")
        dve_seq, act_seq, pool_seq = sem("dve_seq"), sem("act_seq"), sem("pool_seq")
        roped, turned, turn_copied = sem("roped"), sem("turned"), sem("turn_copied")
        turn_out = [sem(f"turn_out{i}") for i in range(2)]
        k_kept = sem("k_kept")
        wi_ready, wi_turned, wrow_ready = sem("wi_ready"), sem("wi_turned"), sem("wrow_ready")
        idx_scored, idx_relu, idx_added, qis_copied = (
            sem("idx_scored"), sem("idx_relu"), sem("idx_added"), sem("qis_copied"))
        ik_turned, ik_copied, ik_new, is_scored, is_relu, is_summed = (
            sem("ik_turned"), sem("ik_copied"), sem("ik_new"), sem("is_scored"), sem("is_relu"), sem("is_summed"))
        ss_copied, bias_ready, bias_turned, maskT_ready = (
            sem("ss_copied"), sem("bias_ready"), sem("bias_turned"), sem("maskT_ready"))
        state_turned, state_copied, u_ready, u_turned, u_copied = (
            sem("state_turned"), sem("state_copied"), sem("u_ready"), sem("u_turned"), sem("u_copied"))
        d_ready = sem("d_ready")
        u_out = [sem(f"u_out{i}") for i in range(2)]
        df_high, df_low, pool_done, pool_high = sem("df_high"), sem("df_low"), sem("pool_done"), sem("pool_high")
        p_scored, p_max, p_exp, p_norm, p_turned, p_copied, p_out, p_high, p_low = (
            sem("p_scored"), sem("p_max"), sem("p_exp"), sem("p_norm"), sem("p_turned"), sem("p_copied"),
            sem("p_out"), sem("p_high"), sem("p_low"))
        qkb_ready, kt_turned, kt_act, kt_dve, k_scored, s_masked = (
            sem("qkb_ready"), sem("kt_turned"), sem("kt_act"), sem("kt_dve"), sem("k_scored"), sem("s_masked"))
        mx_ready, mx_turned, dg_ready, mx_bcast, sub_ready, s_exp, sum_ready, sum_bcast = (
            sem("mx_ready"), sem("mx_turned"), sem("dg_ready"), sem("mx_bcast"), sem("sub_ready"),
            sem("s_exp"), sem("sum_ready"), sem("sum_bcast"))
        v_used, s_out, sy_ready, sy_high, sy_low = (
            sem("v_used"), sem("s_out"), sem("sy_ready"), sem("sy_high"), sem("sy_low"))
        silu_done, hid_high, hid_low, down_done = (
            sem("silu_done"), sem("hid_high"), sem("hid_low"), sem("down_done"))
        y_ready, y_turned, y_copied_act, y_copied_dve = (
            sem("y_ready"), sem("y_turned"), sem("y_copied_act"), sem("y_copied_dve"))
        stored, state_out = sem("stored"), sem("state_out")

        class Chain:

            def __init__(self, eng, s):
                self.eng, self.s, self.n, self.more = eng, s, 0, 0

            def __call__(self, ins):
                self.n += 1
                ins.then_inc(self.s, 1)
                self.eng.wait_ge(self.s, self.n + self.more)

        def in_col(s):
            if s == S_KI:
                return C_KI
            if s == S_WI:
                return C_WI_TILE
            for first, col in ((S_UP, C_UP), (S_Q, C_Q), (S_V, C_V), (S_K, C_K), (S_QI, C_QI)):
                if s >= first:
                    return col + (s - first) * P

        rows_of = lambda w: w.rearrange("(k p) n -> p k n", p=P)
        win_v, wout_v = rows_of(w_in[0]), rows_of(w_out[0])
        wgate_v, wup_v, wdown_v = rows_of(w_gate[0]), rows_of(w_up[0]), rows_of(w_down[0])
        wpool_v = w_pool[0].rearrange("g (k p) m -> p (g k) m", p=P)
        x_rows = [x_prompt[0, t * P:(t + 1) * P, :] for t in range(4)] + [x_sample.rearrange("b t d -> (b t) d")]
        ROWS = [P] * 4 + [NS]

        def row_outputs(s):
            if s == S_KI:
                return (idx_k_prompt[0, 0].rearrange("(t p) d -> p t d", p=P),
                        idx_k_sample[0].rearrange("b t d -> (b t) d"))
            po, so, h = (k_prompt, k_sample, s - S_K) if s < S_V else (v_prompt, v_sample, s - S_V)
            return (po[0, 0, :, h, :].rearrange("(t p) d -> p t d", p=P),
                    so[0, :, :, h, :].rearrange("b t d -> (b t) d"))

        TURNS = [S_KI] + list(range(S_K, S_Q))
        block = ctx.enter_context(nc.Block())

        @block.sync
        def _(sp):
            sp.dma_start(cst[:, :], const).then_inc(const_in, 16)
            for t in range(5):
                sp.dma_start(xin[0:ROWS[t], t, :], x_rows[t]).then_inc(x_in[t], 16)
            for n, g in enumerate((g_mix[0], g_ffn[0], g_final)):
                sp.dma_start(grow[n * KT:(n + 1) * KT, :], g.rearrange("(k p) -> k p", p=P)).then_inc(gain_in, 16)
            sp.dma_start(grow[3 * KT:3 * KT + NPOOL, :], s_pool[0].rearrange("(k p) -> k p", p=P)).then_inc(gain_in, 16)
            sp.dma_start(pages[:, :], page_table.rearrange("(o b) n -> o (b n)", o=1)).then_inc(pages_in, 16)
            sp.dma_start(pool_sample[0, :, 0:STATE - DT, :], state_pool[0, :, DT:STATE, :]).then_inc(state_out, 16)

            def slot(s, parity, src, first=False):
                if not first:
                    sp.wait_ge(low_ready, s - 1)
                a, b = src.shape[1:]
                sp.dma_start(raw[:, parity, :].rearrange("p (a b) -> p a b", a=a), src).then_inc(raw_in[parity], 16)

            def columns(w, c):
                return w[:, :, c:c + P] if isinstance(c, int) else w[:, :, bass.ds(c, P)]

            for s in (S_KI, S_WI):
                slot(s, s % 2, columns(win_v, in_col(s)), first=True)
            sp.wait_ge(x_copied_act, 10)
            sp.wait_ge(x_copied_dve, 10)
            sp.dma_start(x_keep, XT[:, :, :].rearrange("p k n -> p (k n)")).then_inc(x_kept, 16)
            with sp.Fori(0, IH // 2) as i:
                for j in range(2):
                    slot(2 * i + (S_QI + j), j, columns(win_v, i * (2 * P) + (C_QI + j * P)))
            sp.wait_ge(x_kept, 16)
            sp.wait_ge(pages_in, 16)
            sp.wait_ge(norm_low, KT)
            for b in range(DB):
                if b == 1:
                    for s in (S_K, S_K + 1):
                        slot(s, s % 2, columns(win_v, in_col(s)))
                for c in range(2):
                    if b:
                        sp.wait_ge(ik_turned, 4 * (b - 1) + c + 1)
                    for j in range(4):
                        pg = sp.value_load(pages[0:1, b * NPG + 4 * c + j:b * NPG + 4 * c + j + 1], min_val=0,
                                           max_val=n_phys - 1)
                        sp.dma_start(ikraw[:, c, j * HD:(j + 1) * HD],
                                     cache_idx_k[0, bass.ds(pg, 1), :, :].rearrange("o p d -> p (o d)")
                                     ).then_inc(ik_in[c], 16)
            for first, col in ((S_K + 2, C_K + 2 * P), (S_Q, C_Q), (S_UP, C_UP)):
                n = {S_K + 2: S_Q - S_K - 2, S_Q: NH, S_UP: NPOOL}[first]
                if first == S_UP:
                    sp.wait_ge(is_summed, 5 * DB)
                    sp.dma_start(staterow[:, :], state_pool[0].rearrange("b t c -> (b t) c")).then_inc(state_in, 16)
                with sp.Fori(0, n // 2) as i:
                    for j in range(2):
                        slot(2 * i + (first + j), j, columns(win_v, i * (2 * P) + (col + j * P)))

            sp.wait_ge(slot_done, S_POOL)
            for t in range(2):
                sp.wait_ge(turn_out[t], 32 * len(TURNS[t::2]))
            sp.dma_start(vprompt[:, :, :], v_prompt[0, 0].rearrange("(t p) h d -> p t (h d)", p=P)
                         ).then_inc(vprompt_in, 16)

            def k_page(b, n, j, wait):
                if wait is not None:
                    sp.wait_ge(kt_turned, wait)
                pg = sp.value_load(pages[0:1, bass.ds(b * NPG + n, 1)], min_val=0, max_val=n_phys - 1)
                sp.dma_start(kpage[:, j, :], cache_k[0, bass.ds(pg, 1)].rearrange("o p h d -> p (o h d)")
                             ).then_inc(k_in[j], 16)

            for n in range(NPG):
                k_page(0, n, n % 4, n - 3 if n >= 4 else None)
            with sp.Fori(1, DB) as b:
                for n in range(NPG):
                    k_page(b, n, n % 4, b * NPG + (n - 3))

            sp.wait_ge(sy_low, DB)
            slot(S_POOL, 0, wpool_v)
            slot(S_OUT, 1, columns(wout_v, 0))
            sp.wait_ge(d_kept, 16 * NPOOL)
            for f in range(NPOOL):
                if f >= 2:
                    sp.wait_ge(df_low, f - 1)
                sp.dma_start(DF[:, f % 2, :], d_keep[:, f * NT:(f + 1) * NT]).then_inc(d_back[f % 2], 16)
            sp.wait_ge(slot_done, S_OUT)
            sp.dma_start(XT[:, :, :].rearrange("p k n -> p (k n)"), x_keep).then_inc(x_back, 16)
            with sp.Fori(0, (KT - 2) // 2) as i:
                for j in range(2):
                    slot(2 * i + (S_OUT + 1 + j), j, columns(wout_v, i * (2 * P) + (1 + j) * P))
            slot(S_FF - 1, (S_FF - 1) % 2, columns(wout_v, (KT - 1) * P))
            with sp.Fori(0, CHUNKS) as i:
                for j in range(2 * FT):
                    w = wup_v if j % 2 else wgate_v
                    slot(PER_CHUNK * i + (S_FF + j), (S_FF + j) % 2, columns(w, i * (FT * P) + (j // 2) * P))
                for j in range(FT):
                    slot(PER_CHUNK * i + (S_FF + 2 * FT + j), (S_FF + j) % 2,
                         wdown_v[:, bass.ds(i * FT, FT), j * 512:(j + 1) * 512])

            for q in range(4):
                sp.wait_ge(y_copied_act, 4 * q + 4)
                sp.wait_ge(y_copied_dve, 4 * q + 4)
                cols = slice(q * 512, (q + 1) * 512)
                sp.dma_start(y_prompt[0].rearrange("(t p) d -> p t d", p=P)[:, :, cols], yrow[:, 0:4, cols]
                             ).then_inc(stored, 16)
                sp.dma_start(y_sample.rearrange("b t d -> (b t) d")[:, cols], yrow[0:NS, 4, cols]
                             ).then_inc(stored, 16)
            sp.wait_ge(stored, 128)
            sp.wait_ge(state_out, 16)

        @block.gpsimd
        def _(pool):
            def low(s, parity):
                pool.wait_ge(high_ready, s + 1)
                nc.gpsimd.tensor_tensor(wl[:, parity, :], raw[:, parity, :], wh[:, parity, :].bitcast(F32),
                                        ALU.subtract).then_inc(low_ready, 1)

            low(0, 0)
            low(1, 1)
            with pool.Fori(0, IH // 2) as i:
                for j in range(2):
                    low(2 * i + (S_QI + j), j)
            pool.wait_ge(pages_in, 16)
            pool.wait_ge(x_kept, 16)
            pool.wait_ge(norm_low, KT)
            for b in range(DB):
                if b == 1:
                    low(S_K, 0)
                    low(S_K + 1, 1)
                for c in range(2, 4):
                    if b:
                        pool.wait_ge(ik_turned, 4 * (b - 1) + c + 1)
                    for j in range(4):
                        pg = pool.value_load(pages[0:1, b * NPG + 4 * c + j:b * NPG + 4 * c + j + 1], min_val=0,
                                             max_val=n_phys - 1)
                        pool.dma_start(ikraw[:, c, j * HD:(j + 1) * HD],
                                       cache_idx_k[0, bass.ds(pg, 1), :, :].rearrange("o p d -> p (o d)")
                                       ).then_inc(ik_in[c], 16)
            with pool.Fori(1, (S_POOL - S_K) // 2) as i:
                for j in range(2):
                    low(2 * i + (S_K + j), j)

            def v_page(b, n, j, wait):
                if wait is not None:
                    pool.wait_ge(v_used, wait)
                pg = pool.value_load(pages[0:1, bass.ds(b * NPG + n, 1)], min_val=0, max_val=n_phys - 1)
                pool.dma_start(vpage[:, j, :], cache_v[0, bass.ds(pg, 1)].rearrange("o p h d -> p (o h d)")
                               ).then_inc(v_in[j], 16)

            for t in range(2):
                pool.wait_ge(u_out[t], 16 * (DB + 1) * (NPOOL // 2))
            pool.wait_ge(p_out, 4 * NH)
            for n in range(NPG):
                if n == 4:
                    pool.dma_start(vnew[:, :], v_sample[0, 0].rearrange("t h d -> t (h d)")).then_inc(vnew_in, 16)
                v_page(0, n, n % 4, n - 3 if n >= 4 else None)
            with pool.Fori(1, DB) as b:
                for n in range(NPG):
                    if n == 4:
                        pool.wait_ge(s_out, b)
                        pool.dma_start(vnew[:, :], v_sample[0, bass.ds(b, 1)].rearrange("o t h d -> t (o h d)")
                                       ).then_inc(vnew_in, 16)
                    v_page(b, n, n % 4, b * NPG + (n - 3))

            low(S_POOL, 0)
            with pool.Fori(0, (N_SLOTS - S_OUT) // 2) as i:
                for j in range(2):
                    low(2 * i + (S_OUT + j), (S_OUT + j) % 2)

        @block.tensor
        def _(pe):
            def mm(s, g, parity, gate=None, cols=(0, P), rows=P, banks=None):
                pe.wait_ge(low_ready, s + 1)
                if not (isinstance(g, int) and g < 2):
                    pe.wait_ge(psum_read, g - 1)
                out = pair(parity if banks is None else banks, rows)
                for k in range(KT):
                    if gate is not None:
                        gate(k)
                    a, b = k * P + cols[0], k * P + cols[1]
                    for w, h in ((wh, HH), (wh, HL), (wl, HH)):
                        for n in range(2):
                            last = nc.tensor.matmul(out[:, n, :], w[:, parity, a:b],
                                                    h[:, k, n * HALF:(n + 1) * HALF],
                                                    start=(k == 0 and w is wh and h is HH),
                                                    stop=(k == KT - 1 and w is wl))
                last.then_inc(slot_done, 1)

            pe.wait_ge(const_in, 16)
            n = 0
            for t in range(5):
                pe.wait_ge(x_in[t], 16)
                for f in range(0, KT, 4):
                    if n >= 4:
                        pe.wait_ge(x_copied_dve if n % 2 else x_copied_act, (n - 4) // 2 + 1)
                    for j in range(4):
                        last = nc.tensor.transpose(PS[:, 4 + n % 4, j * P:j * P + ROWS[t]],
                                                   xin[0:ROWS[t], t, (f + j) * P:(f + j + 1) * P],
                                                   ident[0:ROWS[t], 0:ROWS[t]])
                    last.then_inc(x_turned, 1)
                    n += 1

            def sum_squares(m, bank=4):
                pe.wait_ge(sq_added, KT * (m + 1))
                for n in range(2):
                    last = nc.tensor.matmul(PS[:, bank + n, 0:HALF], ones, ss[:, n * HALF:(n + 1) * HALF],
                                            start=True, stop=True)
                last.then_inc(ss_bcast, 1)

            pe.wait_ge(gain_in, 64)
            nc.tensor.transpose(PS[:, 3, 0:3 * KT + NPOOL], grow[:, :], ident[0:3 * KT + NPOOL, 0:3 * KT + NPOOL]
                                ).then_inc(gains_turned, 1)
            sum_squares(0)

            def turn(t, src):
                b = 4 + 2 * (t % 2)
                if t >= 2:
                    pe.wait_ge(turn_copied, t - 1)
                for k in range(5):
                    last = nc.tensor.transpose(PS[0:ROWS[k], b + k // 4, (k % 4) * P:(k % 4 + 1) * P],
                                               src[:, k * P:k * P + ROWS[k]], ident)
                last.then_inc(turned, 1)

            def idx_prompt(h, j, first):
                for n, blk in enumerate(BLOCKS):
                    if first:
                        pe.wait_ge(turn_copied, 1)
                        pe.wait_ge(roped, 2)
                    else:
                        pe.wait_ge(idx_relu, 3 * h + (n - 2))
                    if n == 0 and not first:
                        pe.wait_ge(roped, h + 2)
                    last = nc.tensor.matmul(PS[:, 4 + n, 0:(blk + 1) * P], T2[:, j, 16 + blk * P:16 + (blk + 1) * P],
                                            kiT[:, 0:(blk + 1) * P], start=True, stop=True)
                    last.then_inc(idx_scored, 1)

            mm(S_KI, 0, 0, gate=lambda k: pe.wait_ge(norm_low, k + 1))
            mm(S_WI, 1, 1, cols=(P - IH, P), rows=IH)
            pe.wait_ge(roped, 1)
            turn(0, kiT[:, :])
            mm(S_QI, 2, 0)
            pe.wait_ge(psum_read, S_WI + 1)
            for blk in BLOCKS:
                nc.tensor.transpose(PS[:, 7, blk * IH:(blk + 1) * IH], wiT[:, blk * P:(blk + 1) * P], ident[0:IH, 0:IH])
            nc.tensor.matmul(PS[:, 7, 128:128 + NS], cst[0:IH, K_REP:K_REP + P], wiT[:, SEQ:NT],
                             start=True, stop=True).then_inc(wi_turned, 1)
            mm(S_QI + 1, 3, 1)
            idx_prompt(0, 0, True)
            with pe.Fori(1, IH // 2) as i:
                mm(2 * i + S_QI, 2 * i + S_QI, 0)
                idx_prompt(2 * i - 1, 1, False)
                mm(2 * i + (S_QI + 1), 2 * i + (S_QI + 1), 1)
                idx_prompt(2 * i, 0, False)
            idx_prompt(IH - 1, 1, False)

            CH = [(c * 512, 512) for c in range(4)] + [(PAST, DT)]

            def work(n):
                return 5 + n % 3

            def wait_work(n):
                m = n - 3
                if m < 0:
                    pe.wait_ge(idx_relu, 3 * IH)
                    pe.wait_ge(wrow_ready, 1)
                    return
                b, j = divmod(m, 9)
                if j < 4:
                    pe.wait_ge(ik_copied, 4 * b + j + 1)
                else:
                    pe.wait_ge(is_relu, 5 * b + j - 3)

            for b in range(DB):
                for c in range(4):
                    n = 9 * b + c
                    wait_work(n)
                    pe.wait_ge(ik_in[c], 64 * (b + 1))
                    for j in range(4):
                        last = nc.tensor.transpose(PS[:, work(n), j * P:(j + 1) * P],
                                                   ikraw[:, c, j * HD:(j + 1) * HD], ident)
                    last.then_inc(ik_turned, 1)

                def add_heads(c):
                    pe.wait_ge(is_relu, 5 * b + c + 1)
                    if b == 0 and c == 0:
                        pe.wait_ge(psum_read, S_K)
                    o, w = CH[c]
                    nc.tensor.matmul(PS[0:NS, c, 0:w], wrow[:, b * NS:(b + 1) * NS],
                                     irelu[:, (5 * b + c) % 3, 0:w], start=(b == 0), stop=(b == DB - 1)
                                     ).then_inc(is_summed, 1)

                for c, (o, w) in enumerate(CH):
                    n = 9 * b + 4 + c
                    wait_work(n)
                    if c < 4:
                        pe.wait_ge(ik_copied, 4 * b + c + 1)
                    else:
                        pe.wait_ge(ik_new, b + 1)
                    if b == 0 and c == 0:
                        pe.wait_ge(qis_copied, IH)
                    nc.tensor.matmul(PS[:, work(n), 0:w], qis[:, b, :], ikT[:, b % 2, o:o + w],
                                     start=True, stop=True).then_inc(is_scored, 1)
                    if c:
                        add_heads(c - 1)
                add_heads(4)

            pe.wait_ge(ss_copied, 1)
            mm(S_K, S_K, 0)
            mm(S_K + 1, S_K + 1, 1)

            def turn_head(s, j, t, rotated=True):
                if rotated:
                    pe.wait_ge(roped, s)
                else:
                    pe.wait_ge(psum_read, s + 1)
                b = 4 + 2 * ((j + 1) % 2)
                pe.wait_ge(turn_copied, t - 1)
                for k in range(5):
                    last = nc.tensor.transpose(PS[0:ROWS[k], b + k // 4, (k % 4) * P:(k % 4 + 1) * P],
                                               T2[:, j, 16 + k * P:16 + k * P + ROWS[k]], ident)
                last.then_inc(turned, 1)

            turn_head(S_K, 0, 1)
            with pe.Fori(1, NH // 2) as i:
                mm(2 * i + S_K, 2 * i + S_K, 0)
                turn_head(2 * i + (S_K - 1), 1, 2 * i)
                mm(2 * i + (S_K + 1), 2 * i + (S_K + 1), 1)
                turn_head(2 * i + S_K, 0, 2 * i + 1)
            mm(S_V, S_V, 0)
            turn_head(S_V - 1, 1, NH)
            mm(S_V + 1, S_V + 1, 1)
            turn_head(S_V, 0, NH + 1, False)
            with pe.Fori(NH // 2 + 1, NH) as i:
                mm(2 * i + S_K, 2 * i + S_K, 0)
                turn_head(2 * i + (S_K - 1), 1, 2 * i, False)
                mm(2 * i + (S_K + 1), 2 * i + (S_K + 1), 1)
                turn_head(2 * i + S_K, 0, 2 * i + 1, False)
            mm(S_Q, S_Q, 0)
            turn_head(S_Q - 1, 1, 2 * NH, False)
            mm(S_Q + 1, S_Q + 1, 1)
            with pe.Fori(1, NH // 2) as i:
                mm(2 * i + S_Q, 2 * i + S_Q, 0)
                mm(2 * i + (S_Q + 1), 2 * i + (S_Q + 1), 1)

            pe.wait_ge(state_in, 16)
            pe.wait_ge(turn_copied, 2 * NH + 1)

            for f in range(NPOOL):
                last = nc.tensor.transpose(PS[:, 6 + f // 4, (f % 4) * DB * STATE:(f % 4 + 1) * DB * STATE],
                                           staterow[:, f * P:(f + 1) * P], ident[0:DB * STATE, 0:DB * STATE])
            last.then_inc(state_turned, 1)

            def up_turn(f, j, free=None):
                pe.wait_ge(psum_read, f + (S_UP + 1))
                if free is not None:
                    pe.wait_ge(u_copied, free)
                nc.tensor.transpose(PS[0:STATE, 4 + j, 0:P], T2[:, j, 16 + SEQ - STATE:16 + SEQ], ident)
                nc.tensor.transpose(PS[0:NS, 4 + j, P:2 * P], T2[:, j, 16 + SEQ:16 + NT], ident).then_inc(u_turned, 1)

            mm(S_UP, S_UP, 0)
            mm(S_UP + 1, S_UP + 1, 1)
            up_turn(0, 0)
            with pe.Fori(1, NPOOL // 2) as i:
                mm(2 * i + S_UP, 2 * i + S_UP, 0)
                up_turn(2 * i - 1, 1, 2 * i - 1)
                mm(2 * i + (S_UP + 1), 2 * i + (S_UP + 1), 1)
                up_turn(2 * i, 0, 2 * i - 1)
            up_turn(NPOOL - 1, 1, NPOOL - 2)

            pe.wait_ge(psum_read, S_POOL)
            pe.wait_ge(bias_ready, 1)
            for n in range(NPG + 1):
                w = P if n < NPG else DT
                last = nc.tensor.transpose(PS[0:w, n // 8, (n % 8) * NS:(n % 8 + 1) * NS],
                                           sscore[:, n * P:n * P + w], ident[0:NS, 0:NS])
            last.then_inc(bias_turned, 1)

            UNITS = [(h, q) for h in range(NH) for q in range(4)]
            U = len(UNITS)
            for n in range(U + 2):
                if n < U:
                    h, q = UNITS[n]
                    if n == 0:
                        pe.wait_ge(maskT_ready, 1)
                        pe.wait_ge(u_copied, NPOOL)
                        pe.wait_ge(k_kept, NH)
                        pe.wait_ge(roped, S_UP - 1 - NH)
                    if n >= 2:
                        pe.wait_ge(p_max, n - 1)
                    nc.tensor.matmul(PS[:, n % 2, 0:(q + 1) * P], qkT[:, h, q * P:(q + 1) * P],
                                     qkT[:, NH + h, 0:(q + 1) * P], start=True, stop=True).then_inc(p_scored, 1)
                if 1 <= n <= U:
                    u = n - 1
                    h, q = UNITS[u]
                    pe.wait_ge(p_norm, u + 1)
                    if u >= 2:
                        pe.wait_ge(p_copied, u - 1)
                    for k in range(q + 1):
                        last = nc.tensor.transpose(PS[:, 2 + u % 2, k * P:(k + 1) * P], px[:, u % 2, k * P:(k + 1) * P],
                                                   ident)
                    last.then_inc(p_turned, 1)
                if n >= 2:
                    u = n - 2
                    h, q = UNITS[u]
                    pe.wait_ge(p_copied, u + 1)
                    if u == 0:
                        pe.wait_ge(vprompt_in, 16)
                    if u >= 2:
                        pe.wait_ge(p_low, u - 1)
                    for k in range(q + 1):
                        last = nc.tensor.matmul(PS[:, 4 + u % 2, 0:P], vprompt[:, k, h * HD:(h + 1) * HD],
                                                pxt[:, u % 2, k * P:(k + 1) * P], start=(k == 0), stop=(k == q))
                    last.then_inc(p_out, 1)

            pe.wait_ge(p_low, U)
            LAG = 4

            def k_turn(b, n):
                j = n % 2
                pe.wait_ge(k_in[n % 4], 64 * b + 16 * (n // 4 + 1))
                if not (isinstance(b, int) and n < 2):
                    pe.wait_ge(kt_act, b * NPG + (n - 1))
                    pe.wait_ge(kt_dve, b * NPG + (n - 1))
                for h in range(NH):
                    last = nc.tensor.transpose(PS[:, 2 * j + h // 4, (h % 4) * P:(h % 4 + 1) * P],
                                               kpage[:, n % 4, h * HD:(h + 1) * HD], ident)
                last.then_inc(kt_turned, 1)

            def k_score(b, n):
                if n == 0:
                    pe.wait_ge(qkb_ready, b + 1)
                    if not isinstance(b, int):
                        pe.wait_ge(mx_ready, b)
                pe.wait_ge(kt_act, b * NPG + (n + 1))
                pe.wait_ge(kt_dve, b * NPG + (n + 1))
                for h in range(NH):
                    last = nc.tensor.matmul(PS[:, 4 + n // 8, (n % 8) * NS + h * DT:(n % 8) * NS + (h + 1) * DT],
                                            kturn[:, n % 2, h * P:(h + 1) * P], qkb[:, h, :], start=True, stop=True,
                                            skip_group_check=True)
                last.then_inc(k_scored, 1)

            def k_new_score(b):
                pe.wait_ge(qkb_ready, b + 1)
                if not isinstance(b, int):
                    pe.wait_ge(mx_ready, b)
                for h in range(NH):
                    last = nc.tensor.matmul(PS[0:DT, 6, h * DT:(h + 1) * DT], qkb[:, NH + h, :], qkb[:, h, :],
                                            start=True, stop=True, skip_group_check=True)
                last.then_inc(k_scored, 1)

            def stats_max(b):
                pe.wait_ge(mx_ready, b)
                nc.tensor.matmul(PS[0:NS, 6, 64:64 + P], sm[:, 0, :], ident, start=True, stop=True,
                                 skip_group_check=True).then_inc(mx_turned, 1)

            def stats_bcast(b):
                pe.wait_ge(dg_ready, b)
                nc.tensor.matmul(PS[:, 6, 192:192 + NS], cst[0:NS, K_ONES:K_ONES + P], dg[:, :], start=True, stop=True,
                                 skip_group_check=True).then_inc(mx_bcast, 1)

            def stats_sum(b):
                pe.wait_ge(sum_ready, b)
                nc.tensor.matmul(PS[:, 6, 256:256 + NS], ones, sm[:, 2, :], start=True, stop=True,
                                 skip_group_check=True).then_inc(sum_bcast, 1)

            def pv(b, n):
                if n == 0:
                    pe.wait_ge(s_exp, b)
                if n < NPG:
                    pe.wait_ge(v_in[n % 4], 64 * b + (16 * (n // 4 + 1) - 64))
                else:
                    pe.wait_ge(vnew_in, 16 * b)
                for h in range(NH):
                    v = vpage[:, n % 4, h * HD:(h + 1) * HD] if n < NPG else vnew[:, h * HD:(h + 1) * HD]
                    rows = P if n < NPG else DT
                    last = nc.tensor.matmul(PS[:, 7, h * DT:(h + 1) * DT], v,
                                            sx[0:rows, n * NS + h * DT:n * NS + (h + 1) * DT],
                                            start=(n == 0 and h == 0), stop=(n == NPG), skip_group_check=True)
                last.then_inc(v_used if n < NPG else s_out, 1)

            def sequence(b, values):
                for n in range(NPG + 1):
                    if n < NPG:
                        k_turn(b, n)
                    if n == 0:
                        k_new_score(b)
                    if n == 0 and values:
                        stats_max(b)
                    if n == 2 and values:
                        stats_bcast(b)
                    if n:
                        k_score(b, n - 1)
                    if values and n >= LAG:
                        pv(b, n - LAG)
                    if n == 6 and values:
                        stats_sum(b)
                for n in range(NPG + 1 - LAG, NPG + 1):
                    if values:
                        pv(b, n)

            sequence(0, False)
            with pe.Fori(1, DB) as b:
                sequence(b, True)
            stats_max(DB)
            stats_bcast(DB)
            stats_sum(DB)
            for n in range(NPG + 1):
                pv(DB, n)

            pe.wait_ge(low_ready, S_OUT)
            pe.wait_ge(sy_ready, DB)
            for g in range(4):
                for m in range(2):
                    o = 2 * g + m
                    if o >= 2:
                        pe.wait_ge(psum_read, G_POOL + o - 1)
                    for k in range(2):
                        pe.wait_ge(df_low, 2 * g + k + 1)
                        a = (2 * g + k) * 256 + m * P
                        for w, d in ((wh, DH), (wh, DL), (wl, DH)):
                            for n in range(2):
                                last = nc.tensor.matmul(pair(o)[:, n, :], w[:, 0, a:a + P],
                                                        d[:, 2 * g + k, n * HALF:(n + 1) * HALF],
                                                        start=(k == 0 and w is wh and d is DH),
                                                        stop=(k == 1 and w is wl))
                    if o == NPOOL - 1:
                        last.then_inc(slot_done, 1)
                    else:
                        last.then_inc(pool_done, 1)

            pe.wait_ge(psum_read, G_OUT)
            with pe.Fori(0, KT // 2) as i:
                mm(2 * i + S_OUT, 2 * i + G_OUT, 1, banks=0)
                mm(2 * i + (S_OUT + 1), 2 * i + (G_OUT + 1), 0, banks=1)
            pe.wait_ge(psum_read, G_FF)
            sum_squares(1)

            pe.wait_ge(norm_low, 2 * KT)
            with pe.Fori(0, CHUNKS) as i:
                read0 = READ_CHUNK * i + G_FF
                for j in range(2 * FT):
                    s = PER_CHUNK * i + (S_FF + j)
                    parity = (S_FF + j) % 2
                    pe.wait_ge(low_ready, s + 1)
                    if j < 2:
                        pe.wait_ge(psum_read, read0 + (j - 1))
                    elif j % 2 == 0:
                        pe.wait_ge(silu_done, FT * i + j // 2)
                    else:
                        pe.wait_ge(psum_read, read0 + (j - 1) // 2)
                    for k in range(KT):
                        for w, h in ((wh, HH), (wh, HL), (wl, HH)):
                            for n in range(2):
                                last = nc.tensor.matmul(pair(j)[:, n, :], w[:, parity, k * P:(k + 1) * P],
                                                        h[:, k, n * HALF:(n + 1) * HALF],
                                                        start=(k == 0 and w is wh and h is HH),
                                                        stop=(k == KT - 1 and w is wl))
                    last.then_inc(slot_done, 1)
                for j in range(FT):
                    s = PER_CHUNK * i + (S_FF + 2 * FT + j)
                    parity = (S_FF + j) % 2
                    pe.wait_ge(low_ready, s + 1)
                    for m in range(4):
                        o = 4 * j + m
                        if o == 0:
                            pe.wait_ge(silu_done, FT * i + FT)
                        else:
                            pe.wait_ge(psum_read, read0 + (FT + o - 1))
                        for k in range(FT):
                            if o == 0:
                                pe.wait_ge(hid_low, FT * i + (k + 1))
                            a = k * 512 + m * P
                            for w, h in ((wh, GH), (wh, GL), (wl, GH)):
                                for n in range(2):
                                    last = nc.tensor.matmul(pair(o)[:, n, :], w[:, parity, a:a + P],
                                                            h[:, k, n * HALF:(n + 1) * HALF],
                                                            start=(k == 0 and w is wh and h is GH),
                                                            stop=(k == FT - 1 and w is wl))
                        if m == 3:
                            last.then_inc(slot_done, 1)
                        else:
                            last.then_inc(down_done, 1)
            sum_squares(2)

            for f in range(KT):
                pe.wait_ge(y_ready, f + 1)
                if f == 0:
                    pe.wait_ge(psum_read, G_FF + READ_CHUNK * CHUNKS)
                    pe.wait_ge(inv_ready, 3)
                if f >= 2:
                    pe.wait_ge(y_copied_act, f - 1)
                    pe.wait_ge(y_copied_dve, f - 1)
                for k in range(5):
                    last = nc.tensor.transpose(PS[0:ROWS[k], 2 * (f % 2) + k // 4, (k % 4) * P:(k % 4 + 1) * P],
                                               sq[:, f % 2, k * P:k * P + ROWS[k]], ident)
                last.then_inc(y_turned, 1)

        @block.scalar
        def _(act):
            def high(s, parity, wait=True):
                act.wait_ge(raw_in[parity], 16 * (s // 2 + 1))
                if wait:
                    act.wait_ge(slot_done, s - 1)
                nc.scalar.activation(wh[:, parity, :], raw[:, parity, :], ACT.Copy).then_inc(high_ready, 1)

            for n in range(0, 20, 2):
                t, f = n // 4, 4 * (n % 4)
                act.wait_ge(x_turned, n + 1)
                nc.scalar.activation(XT[:, f:f + 4, t * P:t * P + ROWS[t]],
                                     PS[:, 4 + n % 4, :].rearrange("p (j t) -> p j t", j=4)[:, :, 0:ROWS[t]],
                                     ACT.Copy).then_inc(x_copied_act, 1)
                if n == 8:
                    high(0, 0, wait=False)
                if n == 14:
                    high(1, 1, wait=False)

            def squares(m):
                for f in range(KT):
                    if f >= 2 or m:
                        act.wait_ge(sq_added, KT * m + f - 1)
                    nc.scalar.activation(sq[:, f % 2, :], XT[:, f, :], ACT.Square).then_inc(sq_ready, 1)

            def root(m):
                act.wait_ge(inv_ready, m + 1)
                nc.scalar.activation(rstd[:, :], rstd[:, :], ACT.Sqrt).then_inc(rstd_ready, 1)

            act.wait_ge(x_copied_act, 10)
            act.wait_ge(x_copied_dve, 10)
            squares(0)
            root(0)
            act.wait_ge(gains_ready, 1)
            for f in range(KT):
                act.wait_ge(xn_ready, f + 1)
                nc.scalar.activation(HH[:, f, :], xn[:, f % 2, :], ACT.Copy, scale=gains[:, 0, f:f + 1]
                                     ).then_inc(norm_high, 1)

            def rows_out(t):
                b, j = 4 + 2 * (t % 2), t % 2
                act.wait_ge(turned, t + 1)
                if t >= 2:
                    act.wait_ge(turn_out[j], 32 * (t // 2))
                nc.scalar.activation(stage[:, j, 0:4, :].rearrange("p a d -> p (a d)"), PS[:, b, :], ACT.Copy
                                     ).then_inc(act_seq, 1)
                nc.scalar.activation(stage[0:NS, j, 4, :], PS[0:NS, b + 1, 0:P], ACT.Copy).then_inc(turn_copied, 1)
                act.wait_ge(act_seq, t + 1)
                act.wait_ge(turn_copied, t + 1)
                dst_p, dst_s = row_outputs(TURNS[t])
                act.dma_start(dst_p, stage[:, j, 0:4, :]).then_inc(turn_out[j], 16)
                act.dma_start(dst_s, stage[0:NS, j, 4, :]).then_inc(turn_out[j], 16)

            for s in range(S_POOL):
                if s + 2 < S_POOL:
                    high(s + 2, s % 2)
                if s == S_WI:
                    rows_out(0)
                if S_QI < s < S_K:
                    h = s - 1 - S_QI
                    for n, blk in enumerate(BLOCKS):
                        o, w = BLK_OFF[blk], (blk + 1) * P
                        act.wait_ge(idx_scored, 3 * h + n + 1)
                        if h:
                            act.wait_ge(idx_added, 3 * (h - 1) + n + 1)
                        nc.scalar.activation(pr[:, o:o + w], PS[:, 4 + n, 0:w], ACT.Relu, scale=IDX_SCALE
                                             ).then_inc(idx_relu, 1)
                if S_QI <= s < S_K:
                    h = s - S_QI
                    act.wait_ge(roped, s)
                    nc.scalar.activation(
                        qis[:, :, h * DT:(h + 1) * DT],
                        T2[:, s % 2, 16 + SEQ:16 + NT].rearrange("p (b q) -> p b q", b=DB), ACT.Copy
                    ).then_inc(qis_copied, 1)
                if s == S_K - 1:
                    h = IH - 1
                    for n, blk in enumerate(BLOCKS):
                        o, w = BLK_OFF[blk], (blk + 1) * P
                        act.wait_ge(idx_scored, 3 * h + n + 1)
                        act.wait_ge(idx_added, 3 * (h - 1) + n + 1)
                        nc.scalar.activation(pr[:, o:o + w], PS[:, 4 + n, 0:w], ACT.Relu, scale=IDX_SCALE
                                             ).then_inc(idx_relu, 1)
                    for b in range(DB):
                        for c in range(5):
                            w = 512 if c < 4 else DT
                            n = 9 * b + 4 + c
                            m = 5 * b + c
                            act.wait_ge(is_scored, m + 1)
                            if m >= 3:
                                act.wait_ge(is_summed, m - 2)
                            nc.scalar.activation(irelu[:, m % 3, 0:w], PS[:, 5 + n % 3, 0:w], ACT.Relu,
                                                 scale=IDX_SCALE).then_inc(is_relu, 1)
                if S_K <= s < S_V:
                    act.wait_ge(roped, s)
                    nc.scalar.activation(qkT[:, NH + s - S_K, :], T2[:, s % 2, 16:16 + NT], ACT.Copy
                                         ).then_inc(k_kept, 1)
                if S_K < s <= S_Q:
                    rows_out(s - S_K)
                if s > S_UP:
                    act.wait_ge(d_ready, s - S_UP)
                    act.dma_start(d_keep[:, (s - 1 - S_UP) * NT:(s - S_UP) * NT], rtmp[:, :]).then_inc(d_kept, 16)
                if s > S_UP:
                    for f in ([s - 1 - S_UP] if s < S_POOL - 1 else [NPOOL - 2, NPOOL - 1]):
                        act.wait_ge(u_turned, f + 1)
                        if f >= 2:
                            act.wait_ge(u_out[f % 2], 16 * (DB + 1) * (f // 2))
                        nc.scalar.activation(upt[:, f % 2, :], PS[0:STATE, 4 + f % 2, 0:P], ACT.Copy
                                             ).then_inc(act_seq, 1)
                        nc.scalar.activation(ust[:, f % 2, :], PS[0:NS, 4 + f % 2, P:2 * P], ACT.Copy
                                             ).then_inc(u_copied, 1)
                        act.wait_ge(act_seq, 2 * NH + 1 + f + 1)
                        act.wait_ge(u_copied, f + 1)
                        act.dma_start(pool_prompt[0, 0, :, f * P:(f + 1) * P], upt[:, f % 2, :]
                                      ).then_inc(u_out[f % 2], 16)
                        for b in range(DB):
                            act.dma_start(pool_sample[0, b, STATE - DT:STATE, f * P:(f + 1) * P],
                                          ust[b * DT:(b + 1) * DT, f % 2, :]).then_inc(u_out[f % 2], 16)

            act.wait_ge(d_ready, NPOOL)
            act.dma_start(d_keep[:, (NPOOL - 1) * NT:], rtmp[:, :]).then_inc(d_kept, 16)

            UNITS = [(h, q) for h in range(NH) for q in range(4)]
            U = len(UNITS)
            act.wait_ge(slot_done, S_POOL)
            act.wait_ge(low_ready, S_POOL)
            for n in range(U + 2):
                if n < U:
                    w = (UNITS[n][1] + 1) * P
                    act.wait_ge(p_max, n + 1)
                    nc.scalar.activation(px[:, n % 2, 0:w], px[:, n % 2, 0:w], ACT.Exp, bias=small[:, 32 + n:33 + n],
                                         accum_out=small[:, 64 + n:65 + n]).then_inc(p_exp, 1)
                if 1 <= n <= U:
                    u = n - 1
                    w = (UNITS[u][1] + 1) * P
                    act.wait_ge(p_turned, u + 1)
                    if u >= 2:
                        act.wait_ge(p_out, u - 1)
                    nc.scalar.activation(pxt[:, u % 2, 0:w], PS[:, 2 + u % 2, 0:w], ACT.Copy).then_inc(p_copied, 1)
                if n >= 2:
                    u = n - 2
                    h, q = UNITS[u]
                    act.wait_ge(p_out, u + 1)
                    nc.scalar.activation(HH[:, NPOOL + h, q * P:(q + 1) * P], PS[:, 4 + u % 2, 0:P], ACT.Copy
                                         ).then_inc(p_high, 1)

            def kt_copy(b, n):
                act.wait_ge(kt_turned, b * NPG + (n + 1))
                if not (isinstance(b, int) and n < 2):
                    act.wait_ge(k_scored, b * (NPG + 1) + (n if n >= 2 else n - 1))
                nc.scalar.activation(kturn[:, n % 2, 0:512], PS[:, 2 * (n % 2), :], ACT.Copy).then_inc(kt_act, 1)

            def exponent(b):
                act.wait_ge(sub_ready, b)
                nc.scalar.activation(sx[:, :], sx[:, :], ACT.Exp).then_inc(s_exp, 1)

            def sample_high(b):
                act.wait_ge(sy_ready, b)
                nc.scalar.activation(HH[:, NPOOL:2 * NPOOL, bass.ds(b * DT + (SEQ - DT), DT)],
                                     sm[:, 3, :].rearrange("p (h q) -> p h q", h=NH), ACT.Copy).then_inc(sy_high, 1)

            for n in range(NPG):
                kt_copy(0, n)
            with act.Fori(1, DB) as b:
                for n in range(NPG):
                    kt_copy(b, n)
                    if n == 3:
                        exponent(b)
                sample_high(b)
            exponent(DB)
            act.wait_ge(sy_ready, DB)
            nc.scalar.activation(HH[:, NPOOL:2 * NPOOL, NT - DT:NT],
                                 sm[:, 3, :].rearrange("p (h q) -> p h q", h=NH), ACT.Copy).then_inc(sy_high, 1)

            high(S_POOL, 0)
            high(S_OUT, 1)
            for f in range(NPOOL):
                act.wait_ge(d_back[f % 2], 16 * (f // 2 + 1))
                nc.scalar.activation(DH[:, f, :], DF[:, f % 2, :], ACT.Copy).then_inc(df_high, 1)
            for o in range(NPOOL):
                act.wait_ge(pool_done, o + 1) if o < NPOOL - 1 else act.wait_ge(slot_done, S_OUT)
                nc.scalar.activation(halves(HH[:, o, :]), pair(o), ACT.Copy, scale=gains[:, 3, o:o + 1]
                                     ).then_inc(pool_high, 1)

            high(S_OUT + 1, 0)
            with act.Fori(0, KT // 2 - 1) as i:
                for j in range(2):
                    act.wait_ge(raw_in[1 - j], 16 * i + 16 * ((S_OUT + 2 + j) // 2 + 1))
                    act.wait_ge(slot_done, 2 * i + (S_OUT + 1 + j))
                    nc.scalar.activation(wh[:, 1 - j, :], raw[:, 1 - j, :], ACT.Copy).then_inc(high_ready, 1)
            for s in (S_FF, S_FF + 1):
                high(s, s % 2)
            act.wait_ge(psum_read, G_FF)
            squares(1)
            root(1)
            for f in range(KT):
                act.wait_ge(xn_ready, KT + f + 1)
                nc.scalar.activation(HH[:, f, :], xn[:, f % 2, :], ACT.Copy, scale=gains[:, 1, f:f + 1]
                                     ).then_inc(norm_high, 1)

            def ff_step(i, j, more):
                if more:
                    p = (S_FF + j) % 2
                    act.wait_ge(raw_in[p], 16 * (PER_CHUNK // 2) * i + 16 * ((S_FF + j + 2) // 2 + 1))
                    act.wait_ge(slot_done, PER_CHUNK * i + (S_FF + j + 1))
                    nc.scalar.activation(wh[:, p, :], raw[:, p, :], ACT.Copy).then_inc(high_ready, 1)
                if j >= 2 * FT:
                    return
                f = j // 2
                if j % 2 == 0:
                    act.wait_ge(slot_done, PER_CHUNK * i + (S_FF + j + 1))
                    act.wait_ge(psum_read, READ_CHUNK * i + G_FF + (f - 1 if f >= 2 else 0))
                    nc.scalar.activation(halves(sg[:, f % 2, :]), pair(j), ACT.Silu).then_inc(silu_done, 1)
                else:
                    act.wait_ge(psum_read, READ_CHUNK * i + (G_FF + f + 1))
                    nc.scalar.activation(GH[:, f, :], hid[:, f % 2, :], ACT.Copy).then_inc(hid_high, 1)

            with act.Fori(0, CHUNKS - 1) as i:
                for j in range(PER_CHUNK):
                    ff_step(i, j, True)
            for j in range(PER_CHUNK):
                ff_step(CHUNKS - 1, j, j + 2 < PER_CHUNK)

            act.wait_ge(psum_read, G_FF + READ_CHUNK * CHUNKS)
            squares(2)
            root(2)
            for f in range(KT + 1):
                if f < KT:
                    act.wait_ge(xn_ready, 2 * KT + f + 1)
                    if f >= 2:
                        act.wait_ge(y_turned, f - 1)
                    nc.scalar.activation(sq[:, f % 2, :], xn[:, f % 2, :], ACT.Copy, scale=gains[:, 2, f:f + 1]
                                         ).then_inc(y_ready, 1)
                if f:
                    g = f - 1
                    act.wait_ge(y_turned, g + 1)
                    nc.scalar.activation(yrow[:, 0:4, g * P:(g + 1) * P],
                                         PS[:, 2 * (g % 2), :].rearrange("p (a d) -> p a d", a=4), ACT.Copy
                                         ).then_inc(y_copied_act, 1)

            for t in range(2):
                act.wait_ge(turn_out[t], 32 * len(TURNS[t::2]))
                act.wait_ge(u_out[t], 16 * (DB + 1) * (NPOOL // 2))

        @block.vector
        def _(dve):
            link = Chain(dve, dve_seq)
            v = nc.vector
            link(v.memset(T2[:, :, 0:16], 0.0))
            for n in range(1, 20, 2):
                t, f = n // 4, 4 * (n % 4)
                dve.wait_ge(x_turned, n + 1)
                v.tensor_copy(XT[:, f:f + 4, t * P:t * P + ROWS[t]],
                              PS[:, 4 + n % 4, :].rearrange("p (j t) -> p j t", j=4)[:, :, 0:ROWS[t]]
                              ).then_inc(x_copied_dve, 1)

            def norm(m, low=True):
                for f in range(KT):
                    dve.wait_ge(sq_ready, KT * m + f + 1)
                    if f == 0:
                        v.tensor_copy(ss[:, :], sq[:, 0, :]).then_inc(sq_added, 1)
                    else:
                        dve.wait_ge(sq_added, KT * m + f)
                        v.tensor_tensor(ss[:, :], ss[:, :], sq[:, f % 2, :], ALU.add).then_inc(sq_added, 1)
                dve.wait_ge(ss_bcast, m + 1)
                link(v.tensor_scalar(halves(rstd[:, :]), PS[:, 4:6, 0:HALF], 1.0 / D, EPS, ALU.mult, ALU.add))
                v.reciprocal(rstd[:, :], rstd[:, :]).then_inc(inv_ready, 1)
                dve.wait_ge(rstd_ready, m + 1)

                def scaled(f):
                    if f >= 2:
                        dve.wait_ge(norm_high, KT * m + f - 1) if low else dve.wait_ge(y_ready, f - 1)
                        if low:
                            dve.wait_ge(norm_low, KT * m + f - 1)
                    v.tensor_tensor(xn[:, f % 2, :], XT[:, f, :], rstd[:, :], ALU.mult).then_inc(xn_ready, 1)

                scaled(0)
                for f in range(KT):
                    if f + 1 < KT:
                        scaled(f + 1)
                    if low:
                        dve.wait_ge(norm_high, KT * m + f + 1)
                        v.scalar_tensor_tensor(out=HL[:, f, :], in0=xn[:, f % 2, :], scalar=gains[:, m, f:f + 1],
                                               in1=HH[:, f, :].bitcast(F32), op0=ALU.mult, op1=ALU.subtract
                                               ).then_inc(norm_low, 1)
                    else:
                        dve.wait_ge(y_turned, f + 1)
                        v.tensor_copy(yrow[0:NS, 4, f * P:(f + 1) * P], PS[0:NS, 2 * (f % 2) + 1, 0:P]
                                      ).then_inc(y_copied_dve, 1)

            dve.wait_ge(x_copied_act, 10)
            dve.wait_ge(x_copied_dve, 10)
            dve.wait_ge(gains_turned, 1)
            v.tensor_copy(gains[:, :, :].rearrange("p n k -> p (n k)")[:, 0:3 * KT + NPOOL],
                          PS[:, 3, 0:3 * KT + NPOOL]).then_inc(gains_ready, 1)
            norm(0)

            cos, sin = cst[:, K_COS:K_COS + NT], cst[:, K_SIN:K_SIN + NT]

            link(v.memset(pscore[:, :], 0.0))
            for blk in BLOCKS:
                o = BLK_OFF[blk] + blk * P
                link(v.tensor_copy(pscore[:, o:o + P], cst[:, K_TRI:K_TRI + P]))

            def idx_add(h):
                for n, blk in enumerate(BLOCKS):
                    o, w = BLK_OFF[blk], (blk + 1) * P
                    dve.wait_ge(idx_relu, 3 * h + n + 1)
                    if h:
                        dve.wait_ge(idx_added, 3 * (h - 1) + n + 1)
                    v.scalar_tensor_tensor(out=pscore[:, o:o + w], in0=pr[:, o:o + w], scalar=wtok[:, blk, h:h + 1],
                                           in1=pscore[:, o:o + w], op0=ALU.mult, op1=ALU.add).then_inc(idx_added, 1)

            def sample_indexer():
                for b in range(DB):
                    for c in range(4):
                        n = 9 * b + c
                        dve.wait_ge(ik_turned, 4 * b + c + 1)
                        if b == 0 and c == 0:
                            dve.wait_ge(x_kept, 16)
                        if b >= 2:
                            dve.wait_ge(is_scored, 5 * (b - 1))
                        v.tensor_copy(ikT[:, b % 2, c * 512:(c + 1) * 512], PS[:, 5 + n % 3, :]).then_inc(ik_copied, 1)
                    v.tensor_copy(ikT[:, b % 2, PAST:NKEY], kiT[:, SEQ + b * DT:SEQ + (b + 1) * DT]
                                  ).then_inc(ik_new, 1)
                dve.wait_ge(is_summed, 5 * DB)
                v.tensor_copy(sscore[:, 0:PAST].rearrange("p (c n) -> p c n", c=4), PS[0:NS, 0:4, :])
                v.tensor_tensor(sscore[:, PAST:NKEY], PS[0:NS, 4, 0:DT], cst[0:NS, K_NEW:K_NEW + DT], ALU.add
                                ).then_inc(ss_copied, 1)
                dve.wait_ge(ss_copied, 1)

            def sample_round():
                link(v.max(small[0:NS, 0:8], sscore[:, :]))
                link(v.match_replace(sscore[:, :], small[0:NS, 0:8], sscore[:, :], TAKEN))

            def prompt_round():
                for n, blk in enumerate(BLOCKS):
                    o, w = BLK_OFF[blk], (blk + 1) * P
                    link(v.max(small[:, 8 + 8 * n:16 + 8 * n], pscore[:, o:o + w]))
                for n, blk in enumerate(BLOCKS):
                    o, w = BLK_OFF[blk], (blk + 1) * P
                    link(v.match_replace(pscore[:, o:o + w], small[:, 8 + 8 * n:16 + 8 * n], pscore[:, o:o + w],
                                         TAKEN))

            def pooled(f):
                g = f // 2
                e = T2[:, f % 2, :]
                if f:
                    dve.wait_ge(d_ready, f)
                v.tensor_copy(ES[:, :, 0:STATE], stateT[:, f, :].rearrange("p (b t) -> p b t", b=DB))
                link(v.tensor_copy(ES[:, :, STATE:STATE + DT], e[:, 16 + SEQ:16 + NT].rearrange("p (b t) -> p b t", b=DB)))
                cur_p, cur_s = e[:, 0:16 + SEQ], ES[:, :, :]
                for m in range(g + 1):
                    sh = 1 << m
                    o = (1 << (m + 1)) - 1
                    nxt_p, nxt_s = win[:, m % 2, :], wins[:, m % 2, :, :]
                    v.tensor_tensor(nxt_p[:, o:16 + SEQ], cur_p[:, o:16 + SEQ], cur_p[:, o - sh:16 + SEQ - sh], ALU.add)
                    link(v.tensor_tensor(nxt_s[:, :, o:STATE + DT], cur_s[:, :, o:STATE + DT],
                                         cur_s[:, :, o - sh:STATE + DT - sh], ALU.add))
                    cur_p, cur_s = nxt_p, nxt_s
                w = WINDOWS[g]
                link(v.tensor_tensor(cur_p[:, 16:16 + STATE], cur_p[:, 16:16 + STATE],
                                     cst[:, K_CNT + 16 * g:K_CNT + 16 * g + STATE], ALU.mult))
                if f:
                    dve.wait_ge(d_kept, 16 * f)
                dp = rtmp
                v.scalar_tensor_tensor(out=dp[:, 0:SEQ], in0=cur_p[:, 16:16 + SEQ], scalar=1.0 / w,
                                       in1=e[:, 16:16 + SEQ], op0=ALU.mult, op1=ALU.subtract)
                v.scalar_tensor_tensor(out=dp[:, SEQ:NT].rearrange("p (b t) -> p b t", b=DB),
                                       in0=cur_s[:, :, STATE:STATE + DT], scalar=1.0 / w,
                                       in1=ES[:, :, STATE:STATE + DT], op0=ALU.mult, op1=ALU.subtract
                                       ).then_inc(d_ready, 1)

            rounds = 0
            for s in range(S_POOL):
                dve.wait_ge(slot_done, s + 1)
                j = s % 2
                if s == S_KI:
                    dst = kiT[:, :]
                elif s >= S_UP or S_V <= s < S_Q or s == S_WI:
                    dst = None
                elif s >= S_Q:
                    dst = qkT[:, s - S_Q, :]
                else:
                    dst = T2[:, j, 16:16 + NT]
                if S_QI + 2 <= s < S_Q:
                    if s < S_K + 2:
                        dve.wait_ge(idx_scored, 3 * (min(s, S_K + 1) - 2 - S_QI + 1))
                        dve.wait_ge(qis_copied, min(s, S_K + 1) - 2 - S_QI + 1)
                    else:
                        dve.wait_ge(turned, s - S_K)
                        dve.wait_ge(k_kept, min(s - 1 - S_K, NH))
                if s == S_Q:
                    dve.wait_ge(is_summed, 5 * DB)
                if s == S_WI:
                    v.tensor_copy(halves(wiT[:, :]), pair(s, IH)).then_inc(psum_read, 1)
                elif dst is not None:
                    src = pair(s)
                    n_roped = s - NH if s >= S_Q else s if s else 1
                    if s:
                        dve.wait_ge(roped, n_roped - 1)
                    v.tensor_tensor(halves(rtmp[64:128, :]), src[0:64], halves(sin[0:64]), ALU.mult)
                    v.tensor_tensor(halves(rtmp[0:64, :]), src[64:128], halves(sin[64:128]), ALU.mult)
                    v.tensor_tensor(halves(dst), src, halves(cos), ALU.mult).then_inc(psum_read, 1)
                    dve.wait_ge(psum_read, s + 1)
                    v.tensor_tensor(dst, dst, rtmp[:, :], ALU.add).then_inc(roped, 1)
                elif s < S_Q:
                    v.tensor_copy(halves(T2[:, j, 16:16 + NT]), pair(s)).then_inc(psum_read, 1)
                else:
                    f = s - S_UP
                    if f >= 2:
                        dve.wait_ge(u_turned, f - 1)
                    else:
                        dve.wait_ge(turned, 2 * NH + 1)
                    v.tensor_copy(halves(T2[:, j, 16:16 + NT]), pair(s)).then_inc(psum_read, 1)
                    dve.wait_ge(psum_read, s + 1)
                    pooled(f)
                if s == S_UP - 1:
                    dve.wait_ge(state_turned, 1)
                    link(v.tensor_copy(stateT[:, :, :].rearrange("p (a f) r -> p a (f r)", a=2),
                                       PS[:, 6:8, 0:4 * DB * STATE]))
                if s == S_QI:
                    dve.wait_ge(wi_turned, 1)
                    v.memset(wrow[:, :], 0.0)
                    link(v.tensor_copy(wtok[:, 1:4, :], PS[:, 7, IH:4 * IH].rearrange("p (a h) -> p a h", a=3)))
                    v.tensor_tensor(wrow[:, :].rearrange("p (b x) -> p b x", b=DB)[:, :, 0:DT],
                                    PS[:, 7, 128:128 + NS].rearrange("p (b q) -> p b q", b=DB),
                                    cst[:, K_DIAG:K_DIAG + NS].rearrange("p (b q) -> p b q", b=DB), ALU.mult
                                    ).then_inc(wrow_ready, 1)
                if S_QI < s < S_K:
                    idx_add(s - 1 - S_QI)
                if s == S_K - 1:
                    idx_add(IH - 1)
                    sample_indexer()
                if S_K <= s < S_Q:
                    sample_round()
                    prompt_round()
                if S_Q <= s < S_UP:
                    sample_round()
                    sample_round()
            link(v.tensor_scalar(pscore[:, :], pscore[:, :], TAKEN, HIDE, ALU.not_equal, ALU.mult))
            v.tensor_scalar(sscore[:, :], sscore[:, :], TAKEN, HIDE, ALU.not_equal, ALU.mult).then_inc(bias_ready, 1)
            dve.wait_ge(bias_turned, 1)
            for t in range(2):
                dve.wait_ge(turn_out[t], 32 * len(TURNS[t::2]))
            link(v.tensor_copy(maskT[:, 0:NPG, :].rearrange("p n r -> p (n r)"),
                               PS[:, 0:2, :].rearrange("p a n -> p (a n)")))
            v.tensor_copy(maskT[0:DT, NPG, :], PS[0:DT, 2, 0:NS]).then_inc(maskT_ready, 1)

            UNITS = [(h, q) for h in range(NH) for q in range(4)]
            U = len(UNITS)
            dve.wait_ge(slot_done, S_POOL)
            dve.wait_ge(low_ready, S_POOL)
            for n in range(U + 2):
                if 1 <= n <= U:
                    u = n - 1
                    w = (UNITS[u][1] + 1) * P
                    dve.wait_ge(p_exp, u + 1)
                    link(v.reciprocal(small[:, 96 + u:97 + u], small[:, 64 + u:65 + u]))
                    v.tensor_scalar(px[:, u % 2, 0:w], px[:, u % 2, 0:w], small[:, 96 + u:97 + u], None, ALU.mult
                                    ).then_inc(p_norm, 1)
                if n < U:
                    h, q = UNITS[n]
                    w = (q + 1) * P
                    mask = pscore[:, BLK_OFF[q]:BLK_OFF[q] + w] if q else cst[:, K_TRI:K_TRI + P]
                    dve.wait_ge(p_scored, n + 1)
                    if n >= 2:
                        dve.wait_ge(p_turned, n - 1)
                    link(v.tensor_tensor_reduce(out=px[:, n % 2, 0:w], in0=PS[:, n % 2, 0:w], in1=mask,
                                                scale=ATT_SCALE, scalar=-3.0e38, op0=ALU.add, op1=ALU.max,
                                                accum_out=small[:, n:n + 1]))
                    v.tensor_scalar(small[:, 32 + n:33 + n], small[:, n:n + 1], -1.0, None, ALU.mult
                                    ).then_inc(p_max, 1)
                if n >= 2:
                    u = n - 2
                    h, q = UNITS[u]
                    dve.wait_ge(p_high, u + 1)
                    v.tensor_tensor(HL[:, NPOOL + h, q * P:(q + 1) * P], PS[:, 4 + u % 2, 0:P],
                                    HH[:, NPOOL + h, q * P:(q + 1) * P].bitcast(F32), ALU.subtract
                                    ).then_inc(p_low, 1)

            def heads(b):
                cols = slice(SEQ, SEQ + DT) if isinstance(b, int) else bass.ds(b * DT + SEQ, DT)
                v.tensor_scalar(qkb[:, 0:NH, :], qkT[:, 0:NH, cols], ATT_SCALE, None, ALU.mult)
                v.tensor_copy(qkb[:, NH:2 * NH, :], qkT[:, NH:2 * NH, cols]).then_inc(qkb_ready, 1)

            def kt_copy(b, n):
                dve.wait_ge(kt_turned, b * NPG + (n + 1))
                if not (isinstance(b, int) and n < 2):
                    dve.wait_ge(k_scored, b * (NPG + 1) + (n if n >= 2 else n - 1))
                v.tensor_copy(kturn[:, n % 2, 512:1024], PS[:, 2 * (n % 2) + 1, :]).then_inc(kt_dve, 1)

            def masked(b1):
                dve.wait_ge(k_scored, b1 * (NPG + 1))
                link(v.memset(sx[:, NPG * NS:], HIDE))
                c = bass.ds(b1 * DT - DT, DT) if not isinstance(b1, int) else slice((b1 - 1) * DT, b1 * DT)
                v.tensor_tensor(sx[:, 0:NPG * NS].rearrange("p (n h q) -> p n h q", n=NPG, h=NH),
                                PS[:, 4:6, :].rearrange("p a (n h q) -> p (a n) h q", n=8, h=NH),
                                maskT[:, 0:NPG, c].rearrange("p n (o q) -> p n o q", o=1).broadcast_to([P, NPG, NH, DT]),
                                ALU.add)
                link(v.tensor_tensor(sx[0:DT, NPG * NS:].rearrange("p (h q) -> p h q", h=NH),
                                     PS[0:DT, 6, 0:NS].rearrange("p (h q) -> p h q", h=NH),
                                     maskT[0:DT, NPG:NPG + 1, c].broadcast_to([DT, NH, DT]), ALU.add))
                v.tensor_reduce(sm[:, 0, :], sx[:, :].rearrange("p (n r) -> p r n", n=NPG + 1), AX.X, ALU.max
                                ).then_inc(mx_ready, 1)

            def diagonal(b1):
                dve.wait_ge(mx_turned, b1)
                link(v.tensor_reduce(small[0:NS, 140:141], PS[0:NS, 6, 64:64 + P], AX.X, ALU.max))
                v.tensor_scalar(dg[:, :], cst[0:NS, K_IDENT:K_IDENT + NS], small[0:NS, 140:141], None, ALU.mult
                                ).then_inc(dg_ready, 1)

            def subtract(b1):
                dve.wait_ge(mx_bcast, b1)
                link(v.tensor_copy(sm[:, 1, :], PS[:, 6, 192:192 + NS]))
                v.tensor_tensor(sx[:, :].rearrange("p (n r) -> p n r", n=NPG + 1),
                                sx[:, :].rearrange("p (n r) -> p n r", n=NPG + 1),
                                sm[:, 1:2, :].broadcast_to([P, NPG + 1, NS]), ALU.subtract).then_inc(sub_ready, 1)

            def totals(b1):
                dve.wait_ge(s_exp, b1)
                v.tensor_reduce(sm[:, 2, :], sx[:, :].rearrange("p (n r) -> p r n", n=NPG + 1), AX.X, ALU.add
                                ).then_inc(sum_ready, 1)

            def finish(b1):
                dve.wait_ge(sum_bcast, b1)
                link(v.reciprocal(sm[:, 4, :], PS[:, 6, 256:256 + NS]))
                dve.wait_ge(s_out, b1)
                v.tensor_tensor(sm[:, 3, :], PS[:, 7, 0:NS], sm[:, 4, :], ALU.mult).then_inc(sy_ready, 1)

            def sample_low(b1):
                dve.wait_ge(sy_high, b1)
                cols = slice(NT - DT, NT) if isinstance(b1, int) else bass.ds(b1 * DT + (SEQ - DT), DT)
                v.tensor_tensor(HL[:, NPOOL:2 * NPOOL, cols], sm[:, 3, :].rearrange("p (h q) -> p h q", h=NH),
                                HH[:, NPOOL:2 * NPOOL, cols].bitcast(F32), ALU.subtract).then_inc(sy_low, 1)

            dve.wait_ge(p_out, U)
            for t in range(2):
                dve.wait_ge(u_out[t], 16 * (DB + 1) * (NPOOL // 2))
            heads(0)
            for n in range(NPG):
                kt_copy(0, n)
            base_seq = link.n
            with dve.Fori(1, DB) as b:
                per = 5
                link.more = b * per - per
                masked(b)
                dve.wait_ge(k_scored, b * (NPG + 1))
                heads(b)
                for n in range(NPG):
                    kt_copy(b, n)
                    if n == 0:
                        diagonal(b)
                    if n == 2:
                        subtract(b)
                    if n == 5:
                        totals(b)
                finish(b)
                sample_low(b)
                link.more = 0
                used = link.n - base_seq
            per_turn = used
            link.n = base_seq + per_turn * (DB - 1)
            masked(DB)
            diagonal(DB)
            subtract(DB)
            totals(DB)
            finish(DB)
            sample_low(DB)
            assert per_turn == 5, per_turn

            for f in range(NPOOL):
                dve.wait_ge(df_high, f + 1)
                v.tensor_tensor(DL[:, f, :], DF[:, f % 2, :], DH[:, f, :].bitcast(F32), ALU.subtract).then_inc(df_low, 1)
            for o in range(NPOOL):
                dve.wait_ge(pool_high, o + 1)
                v.scalar_tensor_tensor(out=halves(HL[:, o, :]), in0=pair(o), scalar=gains[:, 3, o:o + 1],
                                       in1=halves(HH[:, o, :].bitcast(F32)), op0=ALU.mult, op1=ALU.subtract
                                       ).then_inc(psum_read, 1)

            dve.wait_ge(x_back, 16)
            for o in range(KT):
                dve.wait_ge(slot_done, S_OUT + o + 1)
                v.tensor_tensor(halves(XT[:, o, :]), halves(XT[:, o, :]), pair(G_OUT + o), ALU.add
                                ).then_inc(psum_read, 1)
            norm(1)

            with dve.Fori(0, CHUNKS) as i:
                for f in range(FT):
                    dve.wait_ge(slot_done, PER_CHUNK * i + (S_FF + 2 * f + 2))
                    dve.wait_ge(silu_done, FT * i + (f + 1))
                    if f >= 2:
                        dve.wait_ge(hid_low, FT * i + (f - 1))
                    v.tensor_tensor(halves(hid[:, f % 2, :]), halves(sg[:, f % 2, :]), pair(1), ALU.mult
                                    ).then_inc(psum_read, 1)
                    dve.wait_ge(hid_high, FT * i + (f + 1))
                    v.tensor_tensor(GL[:, f, :], hid[:, f % 2, :], GH[:, f, :].bitcast(F32), ALU.subtract
                                    ).then_inc(hid_low, 1)
                for o in range(KT):
                    if o % 4 == 3:
                        dve.wait_ge(slot_done, PER_CHUNK * i + (S_FF + 2 * FT + o // 4 + 1))
                    else:
                        dve.wait_ge(down_done, 12 * i + (3 * (o // 4) + o % 4 + 1))
                    v.tensor_tensor(halves(XT[:, o, :]), halves(XT[:, o, :]), pair(o), ALU.add).then_inc(psum_read, 1)
            norm(2, low=False)


_INS = ["x_prompt", "x_sample", "cache_k", "cache_v", "cache_idx_k", "state_pool", "page_table", "g_mix", "w_in",
        "w_pool", "s_pool", "w_out", "g_ffn", "w_gate", "w_up", "w_down", "g_final"]
_OUTS = [(1, SEQ, D), (DB, DT, D), (1, 1, SEQ, NH, HD), (1, 1, SEQ, NH, HD), (1, 1, SEQ, HD), (1, 1, STATE, POOL_W),
         (1, DB, DT, NH, HD), (1, DB, DT, NH, HD), (1, DB, DT, HD), (1, DB, STATE, POOL_W)]


def kernel(**inputs):
    import numpy as np
    import concourse.bacc as bacc
    from concourse.bass_utils import run_bass_kernel_spmd

    nc = bacc.Bacc("TRN2", target_bir_lowering=False, num_devices=1)
    arrays = {f"in_{n}": np.ascontiguousarray(inputs[n]) for n in _INS}
    arrays["in_const"] = constants()
    args = [nc.dram_tensor(n, a.shape, mybir.dt.from_np(a.dtype), kind="ExternalInput").ap()
            for n, a in arrays.items()]
    outs = [nc.dram_tensor(f"out_{i}", s, F32, kind="ExternalOutput").ap() for i, s in enumerate(_OUTS)]
    build(nc, *args, outs)
    r = run_bass_kernel_spmd(nc, [arrays], core_ids=[0])
    return tuple(r.results[0][f"out_{i}"] for i in range(len(_OUTS)))
```

```python
from contextlib import ExitStack

import concourse.bass as bass
from concourse import mybir

F32 = mybir.dt.float32
F32R = mybir.dt.float32r
I32 = mybir.dt.int32
ALU = mybir.AluOpType
ACT = mybir.ActivationFunctionType
AX = mybir.AxisListType

P = 128
D = 2048
KT = D // P
SEQ = 512
DB = 8
DT = 8
NS = DB * DT
NT = SEQ + NS
HALF = NT // 2
PAGE = 128
NPG = 16
PAST = NPG * PAGE
NKEY = PAST + DT
CHUNK = 2 * PAGE
NCH = PAST // CHUNK
GROUPS = ((0, 6), (6, 12), (12, NPG + 1))
POOL_W = 1024
NPOOL = POOL_W // P
WINDOWS = (2, 4, 8, 16)
STATE = 15
HD = 128
NH = 8
IH = 16
TOPK_P = 128
TOPK_S = 256
DFF = 5632
FT = 4
CHUNKS = DFF // (FT * P)
EPS = 1e-6
PAST_MASK = -3.0e38
TAKEN = -3.4e38
HIDE = -2.0 ** 100
ATT_SCALE = float(HD) ** -0.5
IDX_SCALE = float(HD) ** -0.5 * float(IH) ** -0.5

C_UP, C_Q, C_K, C_V, C_QI, C_KI = 0, 1024, 2048, 3072, 4096, 6144
C_WI_TILE = C_KI + P + IH - P

S_KI, S_WI, S_QI = 0, 1, 2
S_K = S_QI + IH
S_V = S_K + NH
S_Q = S_V + NH
S_UP = S_Q + NH
S_POOL = S_UP + NPOOL
S_OUT = S_POOL + 1
S_FF = S_OUT + KT
PER_CHUNK = 3 * FT
N_SLOTS = S_FF + CHUNKS * PER_CHUNK
G_POOL = S_POOL
G_OUT = G_POOL + NPOOL
G_FF = G_OUT + KT
READ_CHUNK = FT + KT

BLOCKS = (1, 2, 3)
BLK_OFF = {1: 0, 2: 256, 3: 640}
BLK_W = 1152

K_IDENT, K_ONES, K_COS, K_SIN, K_REP, K_DIAG, K_TRI, K_NEW, K_CNT = 0, 128, 256, 832, 1408, 1536, 1600, 1728, 1736
K_OTHER = K_CNT + 64
K_ALL = K_OTHER + NS


def constants():
    import numpy as np

    c = np.zeros((P, K_ALL), np.float32)
    c[:, K_IDENT:K_IDENT + P] = np.eye(P)
    c[:, K_ONES:K_ONES + P] = 1.0
    pos = np.concatenate([np.arange(SEQ), np.tile(PAST + np.arange(DT), DB)]).astype(np.float32)
    inv = (10000.0 ** (-(np.arange(HD // 2) / (HD // 2)))).astype(np.float32)
    ang = (pos[None, :] * inv[:, None]).astype(np.float32).astype(np.float64)
    c[:, K_COS:K_COS + NT] = np.tile(np.cos(ang), (2, 1))
    c[:, K_SIN:K_SIN + NT] = np.concatenate([np.sin(ang), -np.sin(ang)], 0)
    for h in range(IH):
        c[h, K_REP + h * DT:K_REP + (h + 1) * DT] = 1.0
    for p in range(P):
        c[p, K_DIAG + p % DT:K_DIAG + NS:DT] = 1.0
    c[:, K_TRI:K_TRI + P] = np.where(np.arange(P)[None, :] > np.arange(P)[:, None], PAST_MASK, 0.0)
    for r in range(NS):
        c[r, K_NEW:K_NEW + DT] = np.where(np.arange(DT) > r % DT, PAST_MASK, 0.0)
        c[r, K_OTHER:K_OTHER + NS] = np.where(np.arange(NS) // DT != r // DT, HIDE, 0.0)
    for g, w in enumerate(WINDOWS):
        for t in range(STATE):
            c[:, K_CNT + g * 16 + t] = w / min(w, t + 1)
    return c


def build(nc, x_prompt, x_sample, cache_k, cache_v, cache_idx_k, state_pool, page_table, g_mix, w_in,
          w_pool, s_pool, w_out, g_ffn, w_gate, w_up, w_down, g_final, const, outs):
    (y_prompt, y_sample, k_prompt, v_prompt, idx_k_prompt, pool_prompt,
     k_sample, v_sample, idx_k_sample, pool_sample) = outs
    n_phys = cache_k.shape[1]
    ctx = ExitStack()
    with ctx:
        base = (nc.sbuf_base + 31) // 32 * 32
        OFF_A = base
        OFF_W = OFF_A + 2 * KT * NT * 4
        OFF_C = OFF_W + 6 * D * 4
        OFF_M = OFF_C + KT * NT * 4

        def at(name, offset, shape, dt=F32):
            return nc.alloc_sbuf_tensor_at(name, shape, dt, offset=offset)

        class Place:

            def __init__(self, offset):
                self.offset = offset

            def __call__(self, name, shape, dt=F32):
                size = 4
                for n in shape[1:]:
                    size *= n
                t = at(name, self.offset, shape, dt)
                self.offset += (size + 31) // 32 * 32
                return t

        in_a = Place(OFF_A)
        HH = in_a("HH", [P, KT, NT], F32R)
        HL = in_a("HL", [P, KT, NT], F32R)
        xin = at("xin", OFF_A, [P, 5, D])
        yrow = at("yrow", OFF_A, [P, 5, D])
        in_a = Place(OFF_A)
        kth = in_a("kth", [P, 2, NH, CHUNK], F32R)
        knh = in_a("knh", [P, NH, NS], F32R)
        vraw = at("vraw", OFF_A, [NS, NH * HD])
        in_a = Place(OFF_A + KT * NT * 4)
        ktl = in_a("ktl", [P, 2, NH, CHUNK], F32R)
        knl = in_a("knl", [P, NH, NS], F32R)
        in_w = Place(OFF_W)
        raw = in_w("raw", [P, 2, D])
        wh = in_w("wh", [P, 2, D], F32R)
        wl = in_w("wl", [P, 2, D], F32R)
        in_w = Place(OFF_W)
        kpage = in_w("kpage", [P, 4, NH * HD])
        vpage = in_w("vpage", [P, 4, NH * HD])
        vhigh = in_w("vhigh", [P, 2, NH * HD], F32R)
        vlow = in_w("vlow", [P, 2, NH * HD], F32R)
        vprompt = at("vprompt", OFF_W + 4 * NH * HD * 4, [P, 4, NH * HD])
        in_w = Place(OFF_W + 8 * NH * HD * 4)
        px = in_w("px", [P, 3, SEQ])
        pxt = in_w("pxt", [P, 3, SEQ])
        XT = at("XT", OFF_C, [P, KT, NT])
        qkT = at("qkT", OFF_C, [P, 2 * NH, NT])
        in_c = Place(OFF_C)
        ikraw = in_c("ikraw", [P, 4, 4 * HD])
        ikT = in_c("ikT", [P, 2, NKEY])
        irelu = in_c("irelu", [P, 3, 512])
        in_c = Place(OFF_C)
        DH = in_c("DH", [P, NPOOL, NT], F32R)
        DL = in_c("DL", [P, NPOOL, NT], F32R)
        in_m = Place(OFF_M)
        cst = in_m("cst", [P, K_ALL])
        gains = in_m("gains", [P, 4, KT])
        pages = in_m("pages", [1, DB * NPG], I32)
        ffn_from = in_m.offset
        t2_at = in_m.offset
        T2 = in_m("T2", [P, 2, 16 + NT])
        rtmp = in_m("rtmp", [P, NT])
        kiT = in_m("kiT", [P, NT])
        wtok = in_m("wtok", [P, 4, IH])
        pscore = in_m("pscore", [P, BLK_W])
        sscore_at = in_m.offset
        sscore = in_m("sscore", [NS, NKEY])
        small = in_m("small", [P, 136])
        stage_at = in_m.offset
        stage = in_m("stage", [P, 2, 5, P])
        maskS = at("maskS", sscore_at, [NS, NKEY], F32R)
        pool_wl = at("pool_wl", t2_at, [P, D], F32R)
        dback = at("dback", OFF_A, [P, NPOOL, NT])
        in_m2 = Place(t2_at)
        prob = in_m2("prob", [NS, PAST + NS])
        qh = in_m2("qh", [P, NH * (NS + DT)], F32R)
        ql = in_m2("ql", [P, NH * (NS + DT)], F32R)
        assert in_m2.offset <= sscore_at
        in_m2 = Place(stage_at)
        ptl = in_m2("ptl", [P, NPG + 1, NS], F32R)
        pick = in_m2("pick", [NS, NS], F32R)
        maskN = in_m2("maskN", [NS, NS], F32R)
        assert in_m2.offset <= stage_at + 2 * 5 * P * 4
        arena = in_m.offset
        in_m = Place(arena)
        sq = in_m("sq", [P, 2, NT])
        ss = in_m("ss", [P, NT])
        rstd = in_m("rstd", [P, NT])
        xn = in_m("xn", [P, 2, NT])
        grow = in_m("grow", [3 * KT + NPOOL, P])
        in_m = Place(arena)
        wiT = in_m("wiT", [IH, NT])
        wrow = in_m("wrow", [P, 576])
        pr = in_m("pr", [P, BLK_W])
        qis = in_m("qis", [P, DB, P])
        in_m = Place(arena)
        staterow = in_m("staterow", [DB * STATE, POOL_W])
        ust = in_m("ust", [NS, 2, P])
        upt = in_m("upt", [STATE, 2, P])
        ES = in_m("ES", [P, DB, STATE + DT + 1])
        win = in_m("win", [P, 2, 16 + SEQ])
        stateT = in_m("stateT", [P, NPOOL, DB * STATE])
        wins = in_m("wins", [P, 2, DB, STATE + DT + 1])
        in_m = Place(arena)
        vnh = in_m("vnh", [NS, NH * HD], F32R)
        vnl = in_m("vnl", [NS, NH * HD], F32R)
        pth = in_m("pth", [P, NPG + 1, NS], F32R)
        orow = in_m("orow", [NS, NH * HD])
        in_m = Place(ffn_from)
        GH = in_m("GH", [P, FT, NT], F32R)
        GL = in_m("GL", [P, FT, NT], F32R)
        sg = in_m("sg", [P, 2, NT])
        hid = in_m("hid", [P, 2, NT])

        ident = cst[:, K_IDENT:K_IDENT + P]
        ones = cst[:, K_ONES:K_ONES + P]

        PS = ctx.enter_context(nc.psum_tensor("PS", [P, 8, 512], F32))

        def pair(g, rows=P):
            return PS[0:rows, 2 * (g % 2):2 * (g % 2) + 2, 0:HALF]

        def halves(ap):
            return ap.rearrange("p (a n) -> p a n", a=2)

        x_keep = nc.dram_tensor("x_keep", [P, KT * NT], F32, kind="Internal").ap()
        d_keep = nc.dram_tensor("d_keep", [P, NPOOL * NT], F32, kind="Internal").ap()

        def sem(name):
            return ctx.enter_context(nc.semaphore(name))

        const_in, pages_in, gain_in = sem("const_in"), sem("pages_in"), sem("gain_in")
        x_in = [sem(f"x_in{i}") for i in range(5)]
        raw_in = [sem(f"raw_in{i}") for i in range(2)]
        ik_in = [sem(f"ik_in{i}") for i in range(4)]
        k_in = [sem(f"k_in{i}") for i in range(4)]
        v_in = [sem(f"v_in{i}") for i in range(4)]
        vnew_in, vprompt_in, state_in = sem("vnew_in"), sem("vprompt_in"), sem("state_in")
        x_kept, x_back, d_kept = sem("x_kept"), [sem(f"x_back{i}") for i in range(4)], sem("d_kept")
        d_back = sem("d_back")
        gains_turned, gains_ready = sem("gains_turned"), sem("gains_ready")
        high_ready, low_ready, slot_done = sem("high_ready"), sem("low_ready"), sem("slot_done")
        psum_read = sem("psum_read")
        x_turned, x_copied_act, x_copied_dve = sem("x_turned"), sem("x_copied_act"), sem("x_copied_dve")
        sq_ready, sq_added, ss_bcast, inv_ready, rstd_ready = (
            sem("sq_ready"), sem("sq_added"), sem("ss_bcast"), sem("inv_ready"), sem("rstd_ready"))
        xn_ready, norm_high, norm_low = sem("xn_ready"), sem("norm_high"), sem("norm_low")
        dve_seq, act_seq, pool_seq = sem("dve_seq"), sem("act_seq"), sem("pool_seq")
        roped, turned, turn_copied = sem("roped"), sem("turned"), sem("turn_copied")
        turn_out = [sem(f"turn_out{i}") for i in range(2)]
        k_kept = sem("k_kept")
        wi_ready, wi_turned, wrow_ready = sem("wi_ready"), sem("wi_turned"), sem("wrow_ready")
        idx_scored, idx_relu, idx_added, qis_copied = (
            sem("idx_scored"), sem("idx_relu"), sem("idx_added"), sem("qis_copied"))
        ik_turned, ik_copied, ik_new, is_scored, is_relu, is_summed = (
            sem("ik_turned"), sem("ik_copied"), sem("ik_new"), sem("is_scored"), sem("is_relu"), sem("is_summed"))
        ss_copied, bias_ready, mask_ready = sem("ss_copied"), sem("bias_ready"), sem("mask_ready")
        state_turned, state_copied, u_ready, u_turned, u_copied = (
            sem("state_turned"), sem("state_copied"), sem("u_ready"), sem("u_turned"), sem("u_copied"))
        d_ready = sem("d_ready")
        u_out = [sem(f"u_out{i}") for i in range(2)]
        df_high, df_low, pool_done, pool_high = sem("df_high"), sem("df_low"), sem("pool_done"), sem("pool_high")
        p_scored, p_max, p_exp, p_norm, p_turned, p_copied, p_out, p_high, p_low = (
            sem("p_scored"), sem("p_max"), sem("p_exp"), sem("p_norm"), sem("p_turned"), sem("p_copied"),
            sem("p_out"), sem("p_high"), sem("p_low"))
        kn_high, kn_low, vn_high, vn_low = sem("kn_high"), sem("kn_low"), sem("vn_high"), sem("vn_low")
        q_high, q_low, pick_ready = sem("q_high"), sem("q_low"), sem("pick_ready")
        kt_turned, kt_high, kt_low, k_scored = sem("kt_turned"), sem("kt_high"), sem("kt_low"), sem("k_scored")
        part_max = sem("part_max")
        s_copied, s_max, s_exp, s_inv = sem("s_copied"), sem("s_max"), sem("s_exp"), sem("s_inv")
        pt_turned, pt_high, pt_low = sem("pt_turned"), sem("pt_high"), sem("pt_low")
        v_high, v_low, v_used, s_out = sem("v_high"), [sem(f"v_low{i}") for i in range(2)], sem("v_used"), sem("s_out")
        o_ready, o_turned, sy_high = sem("o_ready"), sem("o_turned"), sem("sy_high")
        out_read = sem("out_read")
        silu_done, hid_high, hid_low, down_done = (
            sem("silu_done"), sem("hid_high"), sem("hid_low"), sem("down_done"))
        y_ready, y_turned, y_copied_act, y_copied_dve = (
            sem("y_ready"), sem("y_turned"), sem("y_copied_act"), sem("y_copied_dve"))
        stored, state_out = sem("stored"), sem("state_out")

        class Chain:

            def __init__(self, eng, s):
                self.eng, self.s, self.n, self.more = eng, s, 0, 0

            def __call__(self, ins):
                self.n += 1
                ins.then_inc(self.s, 1)
                self.eng.wait_ge(self.s, self.n + self.more)

        def in_col(s):
            if s == S_KI:
                return C_KI
            if s == S_WI:
                return C_WI_TILE
            for first, col in ((S_UP, C_UP), (S_Q, C_Q), (S_V, C_V), (S_K, C_K), (S_QI, C_QI)):
                if s >= first:
                    return col + (s - first) * P

        rows_of = lambda w: w.rearrange("(k p) n -> p k n", p=P)
        win_v, wout_v = rows_of(w_in[0]), rows_of(w_out[0])
        wgate_v, wup_v, wdown_v = rows_of(w_gate[0]), rows_of(w_up[0]), rows_of(w_down[0])
        wpool_v = w_pool[0].rearrange("g (k p) m -> p (g k) m", p=P)
        x_rows = [x_prompt[0, t * P:(t + 1) * P, :] for t in range(4)] + [x_sample.rearrange("b t d -> (b t) d")]
        ROWS = [P] * 4 + [NS]

        def row_outputs(s):
            if s == S_KI:
                return (idx_k_prompt[0, 0].rearrange("(t p) d -> p t d", p=P),
                        idx_k_sample[0].rearrange("b t d -> (b t) d"))
            po, so, h = (k_prompt, k_sample, s - S_K) if s < S_V else (v_prompt, v_sample, s - S_V)
            return (po[0, 0, :, h, :].rearrange("(t p) d -> p t d", p=P),
                    so[0, :, :, h, :].rearrange("b t d -> (b t) d"))

        TURNS = [S_KI] + list(range(S_K, S_Q))
        block = ctx.enter_context(nc.Block())

        @block.sync
        def _(sp):
            sp.dma_start(cst[:, :], const).then_inc(const_in, 16)
            for t in range(5):
                sp.dma_start(xin[0:ROWS[t], t, :], x_rows[t]).then_inc(x_in[t], 16)
            for n, g in enumerate((g_mix[0], g_ffn[0], g_final)):
                sp.dma_start(grow[n * KT:(n + 1) * KT, :], g.rearrange("(k p) -> k p", p=P)).then_inc(gain_in, 16)
            sp.dma_start(grow[3 * KT:3 * KT + NPOOL, :], s_pool[0].rearrange("(k p) -> k p", p=P)).then_inc(gain_in, 16)
            sp.dma_start(pages[:, :], page_table.rearrange("(o b) n -> o (b n)", o=1)).then_inc(pages_in, 16)
            sp.dma_start(pool_sample[0, :, 0:STATE - DT, :], state_pool[0, :, DT:STATE, :]).then_inc(state_out, 16)

            def slot(s, parity, src, first=False):
                if not first:
                    sp.wait_ge(low_ready, s - 1)
                a, b = src.shape[1:]
                sp.dma_start(raw[:, parity, :].rearrange("p (a b) -> p a b", a=a), src).then_inc(raw_in[parity], 16)

            def columns(w, c):
                return w[:, :, c:c + P] if isinstance(c, int) else w[:, :, bass.ds(c, P)]

            for s in (S_KI, S_WI):
                slot(s, s % 2, columns(win_v, in_col(s)), first=True)
            sp.wait_ge(x_copied_act, 10)
            sp.wait_ge(x_copied_dve, 10)
            sp.dma_start(x_keep, XT[:, :, :].rearrange("p k n -> p (k n)")).then_inc(x_kept, 16)
            with sp.Fori(0, IH // 2) as i:
                for j in range(2):
                    slot(2 * i + (S_QI + j), j, columns(win_v, i * (2 * P) + (C_QI + j * P)))
            sp.wait_ge(x_kept, 16)
            sp.wait_ge(pages_in, 16)
            sp.wait_ge(norm_low, KT)
            for b in range(DB):
                if b == 1:
                    for s in (S_K, S_K + 1):
                        slot(s, s % 2, columns(win_v, in_col(s)))
                for c in range(2):
                    if b:
                        sp.wait_ge(ik_turned, 4 * (b - 1) + c + 1)
                    for j in range(4):
                        pg = sp.value_load(pages[0:1, b * NPG + 4 * c + j:b * NPG + 4 * c + j + 1], min_val=0,
                                           max_val=n_phys - 1)
                        sp.dma_start(ikraw[:, c, j * HD:(j + 1) * HD],
                                     cache_idx_k[0, bass.ds(pg, 1), :, :].rearrange("o p d -> p (o d)")
                                     ).then_inc(ik_in[c], 16)
            for first, col in ((S_K + 2, C_K + 2 * P), (S_Q, C_Q), (S_UP, C_UP)):
                n = {S_K + 2: S_Q - S_K - 2, S_Q: NH, S_UP: NPOOL}[first]
                if first == S_UP:
                    sp.wait_ge(is_summed, 5 * DB)
                    sp.dma_start(staterow[:, :], state_pool[0].rearrange("b t c -> (b t) c")).then_inc(state_in, 16)
                with sp.Fori(0, n // 2) as i:
                    for j in range(2):
                        slot(2 * i + (first + j), j, columns(win_v, i * (2 * P) + (col + j * P)))

            sp.wait_ge(slot_done, S_POOL)
            for t in range(2):
                sp.wait_ge(turn_out[t], 32 * len(TURNS[t::2]))
            sp.dma_start(vprompt[:, :, :], v_prompt[0, 0].rearrange("(t p) h d -> p t (h d)", p=P)
                         ).then_inc(vprompt_in, 16)

            for t in range(2):
                sp.wait_ge(turn_out[t], 32 * len(TURNS[t::2]))
            sp.dma_start(vraw[:, :], v_sample[0].rearrange("b t h d -> (b t) (h d)")).then_inc(vnew_in, 16)

            def page(b, n, ring, cache, arrived):
                pg = sp.value_load(pages[0:1, bass.ds(b * NPG + n, 1)], min_val=0, max_val=n_phys - 1)
                sp.dma_start(ring[:, n % 4, :], cache[0, bass.ds(pg, 1)].rearrange("o p h d -> p (o h d)")
                             ).then_inc(arrived[n % 4], 16)

            def k_page(b, n):
                if not (isinstance(b, int) and b == 0 and n < 4):
                    sp.wait_ge(kt_turned, b * NPG + (n - 3))
                page(b, n, kpage, cache_k, k_in)

            def v_page(b, n):
                if not (isinstance(b, int) and b == 1 and n < 4):
                    sp.wait_ge(v_low[n % 2], b * (NPG // 2) + (n // 2 - 1 - NPG // 2))
                page(b - 1, n, vpage, cache_v, v_in)

            def load_pages(b, keys, values):
                for c in range(-1, NCH):
                    for n in (2 * c + 2, 2 * c + 3):
                        if keys and n < NPG:
                            k_page(b, n)
                    for n in (2 * c, 2 * c + 1):
                        if values and n >= 0:
                            v_page(b, n)

            load_pages(0, True, False)
            load_pages(1, True, True)
            with sp.Fori(2, DB) as b:
                load_pages(b, True, True)
            for n in range(NPG):
                v_page(DB, n)
                if n == 3:
                    sp.wait_ge(kt_turned, DB * NPG)
                    slot(S_POOL, 0, wpool_v)
                if n in (5, 7):
                    sp.wait_ge(k_scored, DB * (NCH + 1))
                    sp.wait_ge(d_kept, 16 * NPOOL)
                    f = NPOOL // 2 * (n // 7)
                    sp.dma_start(dback[:, f:f + NPOOL // 2, :].rearrange("p f n -> p (f n)"),
                                 d_keep[:, f * NT:(f + NPOOL // 2) * NT]).then_inc(d_back, 16)
                if n == 9:
                    slot(S_OUT, 1, columns(wout_v, 0))

            slot(S_OUT + 1, 0, columns(wout_v, P))
            sp.wait_ge(slot_done, S_OUT)
            for o in range(4):
                sp.dma_start(XT[:, 4 * o:4 * o + 4, :].rearrange("p k n -> p (k n)"),
                             x_keep[:, 4 * o * NT:(4 * o + 4) * NT]).then_inc(x_back[o], 16)
                if o < 3:
                    slot(S_OUT + 2 + o, (S_OUT + 2 + o) % 2, columns(wout_v, (2 + o) * P))
            with sp.Fori(0, (KT - 6) // 2) as i:
                for j in range(2):
                    slot(2 * i + (S_OUT + 5 + j), j, columns(wout_v, i * (2 * P) + (5 + j) * P))
            slot(S_FF - 1, (S_FF - 1) % 2, columns(wout_v, (KT - 1) * P))
            with sp.Fori(0, CHUNKS) as i:
                for j in range(2 * FT):
                    w = wup_v if j % 2 else wgate_v
                    slot(PER_CHUNK * i + (S_FF + j), (S_FF + j) % 2, columns(w, i * (FT * P) + (j // 2) * P))
                for j in range(FT):
                    slot(PER_CHUNK * i + (S_FF + 2 * FT + j), (S_FF + j) % 2,
                         wdown_v[:, bass.ds(i * FT, FT), j * 512:(j + 1) * 512])

            for q in range(4):
                sp.wait_ge(y_copied_act, 4 * q + 4)
                sp.wait_ge(y_copied_dve, 4 * q + 4)
                cols = slice(q * 512, (q + 1) * 512)
                sp.dma_start(y_prompt[0].rearrange("(t p) d -> p t d", p=P)[:, :, cols], yrow[:, 0:4, cols]
                             ).then_inc(stored, 16)
                sp.dma_start(y_sample.rearrange("b t d -> (b t) d")[:, cols], yrow[0:NS, 4, cols]
                             ).then_inc(stored, 16)
            sp.wait_ge(stored, 128)
            sp.wait_ge(state_out, 16)

        @block.gpsimd
        def _(pool):
            def low(s, parity):
                pool.wait_ge(high_ready, s + 1)
                nc.gpsimd.tensor_tensor(wl[:, parity, :], raw[:, parity, :], wh[:, parity, :].bitcast(F32),
                                        ALU.subtract).then_inc(low_ready, 1)

            low(0, 0)
            low(1, 1)
            with pool.Fori(0, IH // 2) as i:
                for j in range(2):
                    low(2 * i + (S_QI + j), j)
            pool.wait_ge(pages_in, 16)
            pool.wait_ge(x_kept, 16)
            pool.wait_ge(norm_low, KT)
            for b in range(DB):
                if b == 1:
                    low(S_K, 0)
                    low(S_K + 1, 1)
                for c in range(2, 4):
                    if b:
                        pool.wait_ge(ik_turned, 4 * (b - 1) + c + 1)
                    for j in range(4):
                        pg = pool.value_load(pages[0:1, b * NPG + 4 * c + j:b * NPG + 4 * c + j + 1], min_val=0,
                                             max_val=n_phys - 1)
                        pool.dma_start(ikraw[:, c, j * HD:(j + 1) * HD],
                                       cache_idx_k[0, bass.ds(pg, 1), :, :].rearrange("o p d -> p (o d)")
                                       ).then_inc(ik_in[c], 16)
            with pool.Fori(1, (S_POOL - S_K) // 2) as i:
                for j in range(2):
                    low(2 * i + (S_K + j), j)

            def v_lows(b):
                for n in range(0, NPG, 2):
                    pool.wait_ge(v_high, b * NPG + (n + 1 - NPG))
                    nc.gpsimd.tensor_tensor(vlow[:, 0, :], vpage[:, n % 4, :], vhigh[:, 0, :].bitcast(F32),
                                            ALU.subtract).then_inc(v_low[0], 1)

            with pool.Fori(1, DB + 1) as b:
                v_lows(b)

            pool.wait_ge(high_ready, S_POOL + 1)
            pool.wait_ge(pt_turned, 3 * DB)
            nc.gpsimd.tensor_tensor(pool_wl[:, :], raw[:, 0, :], wh[:, 0, :].bitcast(F32),
                                    ALU.subtract).then_inc(low_ready, 1)
            pool.wait_ge(s_out, DB)
            with pool.Fori(0, (N_SLOTS - S_OUT) // 2) as i:
                for j in range(2):
                    low(2 * i + (S_OUT + j), (S_OUT + j) % 2)

        @block.tensor
        def _(pe):
            def mm(s, g, parity, gate=None, cols=(0, P), rows=P, banks=None):
                pe.wait_ge(low_ready, s + 1)
                if not (isinstance(g, int) and g < 2):
                    pe.wait_ge(psum_read, g - 1)
                out = pair(parity if banks is None else banks, rows)
                for k in range(KT):
                    if gate is not None:
                        gate(k)
                    a, b = k * P + cols[0], k * P + cols[1]
                    for w, h in ((wh, HH), (wh, HL), (wl, HH)):
                        for n in range(2):
                            last = nc.tensor.matmul(out[:, n, :], w[:, parity, a:b],
                                                    h[:, k, n * HALF:(n + 1) * HALF],
                                                    start=(k == 0 and w is wh and h is HH),
                                                    stop=(k == KT - 1 and w is wl))
                last.then_inc(slot_done, 1)

            pe.wait_ge(const_in, 16)
            n = 0
            for t in range(5):
                pe.wait_ge(x_in[t], 16)
                for f in range(0, KT, 4):
                    if n >= 4:
                        pe.wait_ge(x_copied_dve if n % 2 else x_copied_act, (n - 4) // 2 + 1)
                    for j in range(4):
                        last = nc.tensor.transpose(PS[:, 4 + n % 4, j * P:j * P + ROWS[t]],
                                                   xin[0:ROWS[t], t, (f + j) * P:(f + j + 1) * P],
                                                   ident[0:ROWS[t], 0:ROWS[t]])
                    last.then_inc(x_turned, 1)
                    n += 1

            def sum_squares(m, bank=4):
                pe.wait_ge(sq_added, KT * (m + 1))
                for n in range(2):
                    last = nc.tensor.matmul(PS[:, bank + n, 0:HALF], ones, ss[:, n * HALF:(n + 1) * HALF],
                                            start=True, stop=True)
                last.then_inc(ss_bcast, 1)

            pe.wait_ge(gain_in, 64)
            nc.tensor.transpose(PS[:, 3, 0:3 * KT + NPOOL], grow[:, :], ident[0:3 * KT + NPOOL, 0:3 * KT + NPOOL]
                                ).then_inc(gains_turned, 1)
            sum_squares(0)

            def turn(t, src):
                b = 4 + 2 * (t % 2)
                if t >= 2:
                    pe.wait_ge(turn_copied, t - 1)
                for k in range(5):
                    last = nc.tensor.transpose(PS[0:ROWS[k], b + k // 4, (k % 4) * P:(k % 4 + 1) * P],
                                               src[:, k * P:k * P + ROWS[k]], ident)
                last.then_inc(turned, 1)

            def idx_prompt(h, j, first):
                for n, blk in enumerate(BLOCKS):
                    if first:
                        pe.wait_ge(turn_copied, 1)
                        pe.wait_ge(roped, 2)
                    else:
                        pe.wait_ge(idx_relu, 3 * h + (n - 2))
                    if n == 0 and not first:
                        pe.wait_ge(roped, h + 2)
                    last = nc.tensor.matmul(PS[:, 4 + n, 0:(blk + 1) * P], T2[:, j, 16 + blk * P:16 + (blk + 1) * P],
                                            kiT[:, 0:(blk + 1) * P], start=True, stop=True)
                    last.then_inc(idx_scored, 1)

            mm(S_KI, 0, 0, gate=lambda k: pe.wait_ge(norm_low, k + 1))
            mm(S_WI, 1, 1, cols=(P - IH, P), rows=IH)
            pe.wait_ge(roped, 1)
            turn(0, kiT[:, :])
            mm(S_QI, 2, 0)
            pe.wait_ge(psum_read, S_WI + 1)
            for blk in BLOCKS:
                nc.tensor.transpose(PS[:, 7, blk * IH:(blk + 1) * IH], wiT[:, blk * P:(blk + 1) * P], ident[0:IH, 0:IH])
            nc.tensor.matmul(PS[:, 7, 128:128 + NS], cst[0:IH, K_REP:K_REP + P], wiT[:, SEQ:NT],
                             start=True, stop=True).then_inc(wi_turned, 1)
            mm(S_QI + 1, 3, 1)
            idx_prompt(0, 0, True)
            with pe.Fori(1, IH // 2) as i:
                mm(2 * i + S_QI, 2 * i + S_QI, 0)
                idx_prompt(2 * i - 1, 1, False)
                mm(2 * i + (S_QI + 1), 2 * i + (S_QI + 1), 1)
                idx_prompt(2 * i, 0, False)
            idx_prompt(IH - 1, 1, False)

            CH = [(c * 512, 512) for c in range(4)] + [(PAST, DT)]

            def work(n):
                return 5 + n % 3

            def wait_work(n):
                m = n - 3
                if m < 0:
                    pe.wait_ge(idx_relu, 3 * IH)
                    pe.wait_ge(wrow_ready, 1)
                    return
                b, j = divmod(m, 9)
                if j < 4:
                    pe.wait_ge(ik_copied, 4 * b + j + 1)
                else:
                    pe.wait_ge(is_relu, 5 * b + j - 3)

            for b in range(DB):
                for c in range(4):
                    n = 9 * b + c
                    wait_work(n)
                    pe.wait_ge(ik_in[c], 64 * (b + 1))
                    for j in range(4):
                        last = nc.tensor.transpose(PS[:, work(n), j * P:(j + 1) * P],
                                                   ikraw[:, c, j * HD:(j + 1) * HD], ident)
                    last.then_inc(ik_turned, 1)

                def add_heads(c):
                    pe.wait_ge(is_relu, 5 * b + c + 1)
                    if b == 0 and c == 0:
                        pe.wait_ge(psum_read, S_K)
                    o, w = CH[c]
                    nc.tensor.matmul(PS[0:NS, c, 0:w], wrow[:, b * NS:(b + 1) * NS],
                                     irelu[:, (5 * b + c) % 3, 0:w], start=(b == 0), stop=(b == DB - 1)
                                     ).then_inc(is_summed, 1)

                for c, (o, w) in enumerate(CH):
                    n = 9 * b + 4 + c
                    wait_work(n)
                    if c < 4:
                        pe.wait_ge(ik_copied, 4 * b + c + 1)
                    else:
                        pe.wait_ge(ik_new, b + 1)
                    if b == 0 and c == 0:
                        pe.wait_ge(qis_copied, IH)
                    nc.tensor.matmul(PS[:, work(n), 0:w], qis[:, b, :], ikT[:, b % 2, o:o + w],
                                     start=True, stop=True).then_inc(is_scored, 1)
                    if c:
                        add_heads(c - 1)
                add_heads(4)

            pe.wait_ge(ss_copied, 1)
            mm(S_K, S_K, 0)
            mm(S_K + 1, S_K + 1, 1)

            def turn_head(s, j, t, rotated=True):
                if rotated:
                    pe.wait_ge(roped, s)
                else:
                    pe.wait_ge(psum_read, s + 1)
                b = 4 + 2 * ((j + 1) % 2)
                pe.wait_ge(turn_copied, t - 1)
                for k in range(5):
                    last = nc.tensor.transpose(PS[0:ROWS[k], b + k // 4, (k % 4) * P:(k % 4 + 1) * P],
                                               T2[:, j, 16 + k * P:16 + k * P + ROWS[k]], ident)
                last.then_inc(turned, 1)

            turn_head(S_K, 0, 1)
            with pe.Fori(1, NH // 2) as i:
                mm(2 * i + S_K, 2 * i + S_K, 0)
                turn_head(2 * i + (S_K - 1), 1, 2 * i)
                mm(2 * i + (S_K + 1), 2 * i + (S_K + 1), 1)
                turn_head(2 * i + S_K, 0, 2 * i + 1)
            mm(S_V, S_V, 0)
            turn_head(S_V - 1, 1, NH)
            mm(S_V + 1, S_V + 1, 1)
            turn_head(S_V, 0, NH + 1, False)
            with pe.Fori(NH // 2 + 1, NH) as i:
                mm(2 * i + S_K, 2 * i + S_K, 0)
                turn_head(2 * i + (S_K - 1), 1, 2 * i, False)
                mm(2 * i + (S_K + 1), 2 * i + (S_K + 1), 1)
                turn_head(2 * i + S_K, 0, 2 * i + 1, False)
            mm(S_Q, S_Q, 0)
            turn_head(S_Q - 1, 1, 2 * NH, False)
            mm(S_Q + 1, S_Q + 1, 1)
            with pe.Fori(1, NH // 2) as i:
                mm(2 * i + S_Q, 2 * i + S_Q, 0)
                mm(2 * i + (S_Q + 1), 2 * i + (S_Q + 1), 1)

            pe.wait_ge(state_in, 16)
            pe.wait_ge(turn_copied, 2 * NH + 1)

            for f in range(NPOOL):
                last = nc.tensor.transpose(PS[:, 6 + f // 4, (f % 4) * DB * STATE:(f % 4 + 1) * DB * STATE],
                                           staterow[:, f * P:(f + 1) * P], ident[0:DB * STATE, 0:DB * STATE])
            last.then_inc(state_turned, 1)

            def up_turn(f, j, free=None):
                pe.wait_ge(psum_read, f + (S_UP + 1))
                if free is not None:
                    pe.wait_ge(u_copied, free)
                nc.tensor.transpose(PS[0:STATE, 4 + j, 0:P], T2[:, j, 16 + SEQ - STATE:16 + SEQ], ident)
                nc.tensor.transpose(PS[0:NS, 4 + j, P:2 * P], T2[:, j, 16 + SEQ:16 + NT], ident).then_inc(u_turned, 1)

            mm(S_UP, S_UP, 0)
            mm(S_UP + 1, S_UP + 1, 1)
            up_turn(0, 0)
            with pe.Fori(1, NPOOL // 2) as i:
                mm(2 * i + S_UP, 2 * i + S_UP, 0)
                up_turn(2 * i - 1, 1, 2 * i - 1)
                mm(2 * i + (S_UP + 1), 2 * i + (S_UP + 1), 1)
                up_turn(2 * i, 0, 2 * i - 1)
            up_turn(NPOOL - 1, 1, NPOOL - 2)

            pe.wait_ge(psum_read, S_POOL)
            pe.wait_ge(bias_ready, 1)

            UNITS = [(h, q) for h in range(NH) for q in range(4)]
            U = len(UNITS)
            for n in range(U + 3):
                if n < U:
                    h, q = UNITS[n]
                    if n == 0:
                        pe.wait_ge(u_copied, NPOOL)
                        pe.wait_ge(k_kept, NH)
                        pe.wait_ge(roped, S_UP - 1 - NH)
                    if n >= 3:
                        pe.wait_ge(p_max, n - 2)
                    nc.tensor.matmul(PS[:, n % 3, 0:(q + 1) * P], qkT[:, h, q * P:(q + 1) * P],
                                     qkT[:, NH + h, 0:(q + 1) * P], start=True, stop=True).then_inc(p_scored, 1)
                if 2 <= n < U + 2:
                    u = n - 2
                    h, q = UNITS[u]
                    pe.wait_ge(p_norm, u + 1)
                    if u >= 3:
                        pe.wait_ge(p_copied, u - 2)
                    for k in range(q + 1):
                        last = nc.tensor.transpose(PS[:, 3 + u % 3, k * P:(k + 1) * P], px[:, u % 3, k * P:(k + 1) * P],
                                                   ident)
                    last.then_inc(p_turned, 1)
                if n >= 3:
                    u = n - 3
                    h, q = UNITS[u]
                    pe.wait_ge(p_copied, u + 1)
                    if u == 0:
                        pe.wait_ge(vprompt_in, 16)
                    if u >= 2:
                        pe.wait_ge(p_low, u - 1)
                    for k in range(q + 1):
                        last = nc.tensor.matmul(PS[:, 6 + u % 2, 0:P], vprompt[:, k, h * HD:(h + 1) * HD],
                                                pxt[:, u % 3, k * P:(k + 1) * P], start=(k == 0), stop=(k == q))
                    last.then_inc(p_out, 1)

            pe.wait_ge(p_low, U)

            def k_turn(b, n):
                j = n % 2
                pe.wait_ge(k_in[n % 4], b * (4 * NPG) + 16 * (n // 4 + 1))
                if not (isinstance(b, int) and n < 2):
                    pe.wait_ge(kt_low, b * NPG + (n - 1))
                for h in range(NH):
                    last = nc.tensor.transpose(PS[:, 2 * j + h // 4, (h % 4) * P:(h % 4 + 1) * P],
                                               kpage[:, n % 4, h * HD:(h + 1) * HD], ident)
                last.then_inc(kt_turned, 1)

            def k_score(b, c):
                if c == 0:
                    pe.wait_ge(q_low, b + 1)
                    pe.wait_ge(pick_ready, b + 1)
                    pe.wait_ge(mask_ready, 1)
                if c < NCH:
                    pe.wait_ge(kt_low, b * NPG + (2 * c + 2))
                    w, mask = CHUNK, maskS[:, c * CHUNK:(c + 1) * CHUNK]
                    kh, kl = kth[:, c % 2], ktl[:, c % 2]
                else:
                    pe.wait_ge(kn_low, 1)
                    w, mask, kh, kl = NS, maskN[:, :], knh, knl
                if not (isinstance(b, int) and c == 0):
                    pe.wait_ge(s_copied, b * (NCH + 1) + c)
                out = PS[0:NS, 4, 0:w]
                for h in range(NH):
                    for q, k in ((qh, kh), (qh, kl), (ql, kh)):
                        nc.tensor.matmul(out, q[:, h * NS:(h + 1) * NS], k[:, h, :],
                                         start=(h == 0 and q is qh and k is kh), stop=False)
                nc.tensor.matmul(out, pick[:, :], mask, start=False, stop=True).then_inc(k_scored, 1)

            def turn_rows(waits, out, rows):
                if waits:
                    return nc.tensor.matmul(out, rows, ident[0:NS, 0:NS], start=True, stop=True)
                return nc.tensor.transpose(out, rows, ident[0:NS, 0:NS])

            def p_turn(b, g):
                if g == 0:
                    pe.wait_ge(s_exp, b)
                    pe.wait_ge(out_read, b)
                else:
                    pe.wait_ge(pt_low, b * 3 + (g - 3))
                n0, n1 = GROUPS[g]
                for n in range(n0, n1):
                    w = PAGE if n < NPG else NS
                    last = turn_rows(n == n0, PS[0:w, 5, (n - n0) * NS:(n - n0 + 1) * NS],
                                     prob[:, n * PAGE:n * PAGE + w])
                last.then_inc(pt_turned, 1)

            def pv(b, n):
                for g in range(3):
                    if n == GROUPS[g][0]:
                        pe.wait_ge(pt_low, b * 3 + (g - 2))
                if n == 0:
                    pe.wait_ge(out_read, b)
                if n < NPG:
                    pe.wait_ge(v_low[n % 2], b * (NPG // 2) + (n // 2 + 1 - NPG // 2))
                    rows, vh, vl = PAGE, vhigh[:, n % 2], vlow[:, n % 2]
                else:
                    pe.wait_ge(vn_low, 1)
                    rows, vh, vl = NS, vnh, vnl
                for a in range(2):
                    for p, v in ((pth, vh), (pth, vl), (ptl, vh)):
                        last = nc.tensor.matmul(PS[0:NS, 6 + a, :], p[0:rows, n, :], v[:, a * 512:(a + 1) * 512],
                                                start=(n == 0 and p is pth and v is vh),
                                                stop=(n == NPG and p is ptl))
                last.then_inc(v_used if n < NPG else s_out, 1)

            def o_turn(b):
                pe.wait_ge(o_ready, b)
                pe.wait_ge(pt_low, b * 3)
                for h in range(NH):
                    last = turn_rows(h == 0, PS[:, 5, h * NS:(h + 1) * NS], orow[:, h * HD:(h + 1) * HD])
                last.then_inc(o_turned, 1)

            def sequence(b, keys, values):
                for c in range(NCH + 1):
                    if keys and c < NCH:
                        k_turn(b, 2 * c)
                        k_turn(b, 2 * c + 1)
                    if values and c == 2:
                        p_turn(b, 1)
                    if c and keys:
                        k_score(b, c - 1)
                    if values and c == 1:
                        p_turn(b, 0)
                    if values and c >= 2:
                        pv(b, 2 * c - 4)
                        pv(b, 2 * c - 3)
                    if values and c == 3:
                        p_turn(b, 2)
                if values:
                    for n in range(2 * NCH - 2, NPG + 1):
                        pv(b, n)
                if keys:
                    k_score(b, NCH)
                if values:
                    o_turn(b)

            sequence(0, True, False)
            with pe.Fori(1, DB) as b:
                sequence(b, True, True)
            sequence(DB, False, True)

            pe.wait_ge(low_ready, S_OUT)
            pe.wait_ge(o_ready, DB)
            for g in range(4):
                for m in range(2):
                    o = 2 * g + m
                    if o >= 2:
                        pe.wait_ge(psum_read, G_POOL + o - 1)
                    if o == 0:
                        pe.wait_ge(df_low, NPOOL)
                    for k in range(2):
                        a = (2 * g + k) * 256 + m * P
                        for w, d in ((wh[:, 0], DH), (wh[:, 0], DL), (pool_wl, DH)):
                            for n in range(2):
                                last = nc.tensor.matmul(pair(o)[:, n, :], w[:, a:a + P],
                                                        d[:, 2 * g + k, n * HALF:(n + 1) * HALF],
                                                        start=(k == 0 and w is not pool_wl and d is DH),
                                                        stop=(k == 1 and w is pool_wl))
                    if o == NPOOL - 1:
                        last.then_inc(slot_done, 1)
                    else:
                        last.then_inc(pool_done, 1)

            pe.wait_ge(psum_read, G_OUT)
            with pe.Fori(0, KT // 2) as i:
                mm(2 * i + S_OUT, 2 * i + G_OUT, 1, banks=0)
                mm(2 * i + (S_OUT + 1), 2 * i + (G_OUT + 1), 0, banks=1)
            pe.wait_ge(psum_read, G_FF)
            sum_squares(1)

            pe.wait_ge(norm_low, 2 * KT)
            with pe.Fori(0, CHUNKS) as i:
                read0 = READ_CHUNK * i + G_FF
                for j in range(2 * FT):
                    s = PER_CHUNK * i + (S_FF + j)
                    parity = (S_FF + j) % 2
                    pe.wait_ge(low_ready, s + 1)
                    if j < 2:
                        pe.wait_ge(psum_read, read0 + (j - 1))
                    elif j % 2 == 0:
                        pe.wait_ge(silu_done, FT * i + j // 2)
                    else:
                        pe.wait_ge(psum_read, read0 + (j - 1) // 2)
                    for k in range(KT):
                        for w, h in ((wh, HH), (wh, HL), (wl, HH)):
                            for n in range(2):
                                last = nc.tensor.matmul(pair(j)[:, n, :], w[:, parity, k * P:(k + 1) * P],
                                                        h[:, k, n * HALF:(n + 1) * HALF],
                                                        start=(k == 0 and w is wh and h is HH),
                                                        stop=(k == KT - 1 and w is wl))
                    last.then_inc(slot_done, 1)
                for j in range(FT):
                    s = PER_CHUNK * i + (S_FF + 2 * FT + j)
                    parity = (S_FF + j) % 2
                    pe.wait_ge(low_ready, s + 1)
                    for m in range(4):
                        o = 4 * j + m
                        if o == 0:
                            pe.wait_ge(silu_done, FT * i + FT)
                        else:
                            pe.wait_ge(psum_read, read0 + (FT + o - 1))
                        for k in range(FT):
                            if o == 0:
                                pe.wait_ge(hid_low, FT * i + (k + 1))
                            a = k * 512 + m * P
                            for w, h in ((wh, GH), (wh, GL), (wl, GH)):
                                for n in range(2):
                                    last = nc.tensor.matmul(pair(o)[:, n, :], w[:, parity, a:a + P],
                                                            h[:, k, n * HALF:(n + 1) * HALF],
                                                            start=(k == 0 and w is wh and h is GH),
                                                            stop=(k == FT - 1 and w is wl))
                        if m == 3:
                            last.then_inc(slot_done, 1)
                        else:
                            last.then_inc(down_done, 1)
            sum_squares(2)

            for f in range(KT):
                pe.wait_ge(y_ready, f + 1)
                if f == 0:
                    pe.wait_ge(psum_read, G_FF + READ_CHUNK * CHUNKS)
                    pe.wait_ge(inv_ready, 3)
                if f >= 2:
                    pe.wait_ge(y_copied_act, f - 1)
                    pe.wait_ge(y_copied_dve, f - 1)
                for k in range(5):
                    last = nc.tensor.transpose(PS[0:ROWS[k], 2 * (f % 2) + k // 4, (k % 4) * P:(k % 4 + 1) * P],
                                               sq[:, f % 2, k * P:k * P + ROWS[k]], ident)
                last.then_inc(y_turned, 1)

        @block.scalar
        def _(act):
            def high(s, parity, wait=True):
                act.wait_ge(raw_in[parity], 16 * (s // 2 + 1))
                if wait:
                    act.wait_ge(slot_done, s - 1)
                nc.scalar.activation(wh[:, parity, :], raw[:, parity, :], ACT.Copy).then_inc(high_ready, 1)

            for n in range(0, 20, 2):
                t, f = n // 4, 4 * (n % 4)
                act.wait_ge(x_turned, n + 1)
                nc.scalar.activation(XT[:, f:f + 4, t * P:t * P + ROWS[t]],
                                     PS[:, 4 + n % 4, :].rearrange("p (j t) -> p j t", j=4)[:, :, 0:ROWS[t]],
                                     ACT.Copy).then_inc(x_copied_act, 1)
                if n == 8:
                    high(0, 0, wait=False)
                if n == 14:
                    high(1, 1, wait=False)

            def squares(m):
                for f in range(KT):
                    if f >= 2 or m:
                        act.wait_ge(sq_added, KT * m + f - 1)
                    nc.scalar.activation(sq[:, f % 2, :], XT[:, f, :], ACT.Square).then_inc(sq_ready, 1)

            def root(m):
                act.wait_ge(inv_ready, m + 1)
                nc.scalar.activation(rstd[:, :], rstd[:, :], ACT.Sqrt).then_inc(rstd_ready, 1)

            act.wait_ge(x_copied_act, 10)
            act.wait_ge(x_copied_dve, 10)
            squares(0)
            root(0)
            act.wait_ge(gains_ready, 1)
            for f in range(KT):
                act.wait_ge(xn_ready, f + 1)
                nc.scalar.activation(HH[:, f, :], xn[:, f % 2, :], ACT.Copy, scale=gains[:, 0, f:f + 1]
                                     ).then_inc(norm_high, 1)

            def rows_out(t):
                b, j = 4 + 2 * (t % 2), t % 2
                act.wait_ge(turned, t + 1)
                if t >= 2:
                    act.wait_ge(turn_out[j], 32 * (t // 2))
                nc.scalar.activation(stage[:, j, 0:4, :].rearrange("p a d -> p (a d)"), PS[:, b, :], ACT.Copy
                                     ).then_inc(act_seq, 1)
                nc.scalar.activation(stage[0:NS, j, 4, :], PS[0:NS, b + 1, 0:P], ACT.Copy).then_inc(turn_copied, 1)
                act.wait_ge(act_seq, t + 1)
                act.wait_ge(turn_copied, t + 1)
                dst_p, dst_s = row_outputs(TURNS[t])
                act.dma_start(dst_p, stage[:, j, 0:4, :]).then_inc(turn_out[j], 16)
                act.dma_start(dst_s, stage[0:NS, j, 4, :]).then_inc(turn_out[j], 16)

            for s in range(S_POOL):
                if s + 2 < S_POOL:
                    high(s + 2, s % 2)
                if s == S_WI:
                    rows_out(0)
                if S_QI < s < S_K:
                    h = s - 1 - S_QI
                    for n, blk in enumerate(BLOCKS):
                        o, w = BLK_OFF[blk], (blk + 1) * P
                        act.wait_ge(idx_scored, 3 * h + n + 1)
                        if h:
                            act.wait_ge(idx_added, 3 * (h - 1) + n + 1)
                        nc.scalar.activation(pr[:, o:o + w], PS[:, 4 + n, 0:w], ACT.Relu, scale=IDX_SCALE
                                             ).then_inc(idx_relu, 1)
                if S_QI <= s < S_K:
                    h = s - S_QI
                    act.wait_ge(roped, s)
                    nc.scalar.activation(
                        qis[:, :, h * DT:(h + 1) * DT],
                        T2[:, s % 2, 16 + SEQ:16 + NT].rearrange("p (b q) -> p b q", b=DB), ACT.Copy
                    ).then_inc(qis_copied, 1)
                if s == S_K - 1:
                    h = IH - 1
                    for n, blk in enumerate(BLOCKS):
                        o, w = BLK_OFF[blk], (blk + 1) * P
                        act.wait_ge(idx_scored, 3 * h + n + 1)
                        act.wait_ge(idx_added, 3 * (h - 1) + n + 1)
                        nc.scalar.activation(pr[:, o:o + w], PS[:, 4 + n, 0:w], ACT.Relu, scale=IDX_SCALE
                                             ).then_inc(idx_relu, 1)
                    for b in range(DB):
                        for c in range(5):
                            w = 512 if c < 4 else DT
                            n = 9 * b + 4 + c
                            m = 5 * b + c
                            act.wait_ge(is_scored, m + 1)
                            if m >= 3:
                                act.wait_ge(is_summed, m - 2)
                            nc.scalar.activation(irelu[:, m % 3, 0:w], PS[:, 5 + n % 3, 0:w], ACT.Relu,
                                                 scale=IDX_SCALE).then_inc(is_relu, 1)
                if S_K <= s < S_V:
                    act.wait_ge(roped, s)
                    nc.scalar.activation(qkT[:, NH + s - S_K, :], T2[:, s % 2, 16:16 + NT], ACT.Copy
                                         ).then_inc(k_kept, 1)
                if S_K < s <= S_Q:
                    rows_out(s - S_K)
                if s > S_UP:
                    act.wait_ge(d_ready, s - S_UP)
                    act.dma_start(d_keep[:, (s - 1 - S_UP) * NT:(s - S_UP) * NT], rtmp[:, :]).then_inc(d_kept, 16)
                if s > S_UP:
                    for f in ([s - 1 - S_UP] if s < S_POOL - 1 else [NPOOL - 2, NPOOL - 1]):
                        act.wait_ge(u_turned, f + 1)
                        if f >= 2:
                            act.wait_ge(u_out[f % 2], 16 * (DB + 1) * (f // 2))
                        nc.scalar.activation(upt[:, f % 2, :], PS[0:STATE, 4 + f % 2, 0:P], ACT.Copy
                                             ).then_inc(act_seq, 1)
                        nc.scalar.activation(ust[:, f % 2, :], PS[0:NS, 4 + f % 2, P:2 * P], ACT.Copy
                                             ).then_inc(u_copied, 1)
                        act.wait_ge(act_seq, 2 * NH + 1 + f + 1)
                        act.wait_ge(u_copied, f + 1)
                        act.dma_start(pool_prompt[0, 0, :, f * P:(f + 1) * P], upt[:, f % 2, :]
                                      ).then_inc(u_out[f % 2], 16)
                        for b in range(DB):
                            act.dma_start(pool_sample[0, b, STATE - DT:STATE, f * P:(f + 1) * P],
                                          ust[b * DT:(b + 1) * DT, f % 2, :]).then_inc(u_out[f % 2], 16)

            act.wait_ge(d_ready, NPOOL)
            act.dma_start(d_keep[:, (NPOOL - 1) * NT:], rtmp[:, :]).then_inc(d_kept, 16)

            UNITS = [(h, q) for h in range(NH) for q in range(4)]
            U = len(UNITS)
            act.wait_ge(slot_done, S_POOL)
            act.wait_ge(low_ready, S_POOL)
            for n in range(U + 3):
                if n < U:
                    w = (UNITS[n][1] + 1) * P
                    act.wait_ge(p_max, n + 1)
                    nc.scalar.activation(px[:, n % 3, 0:w], px[:, n % 3, 0:w], ACT.Exp, bias=small[:, 32 + n:33 + n],
                                         accum_out=small[:, 64 + n:65 + n]).then_inc(p_exp, 1)
                if 2 <= n < U + 2:
                    u = n - 2
                    w = (UNITS[u][1] + 1) * P
                    act.wait_ge(p_turned, u + 1)
                    if u >= 3:
                        act.wait_ge(p_out, u - 2)
                    nc.scalar.activation(pxt[:, u % 3, 0:w], PS[:, 3 + u % 3, 0:w], ACT.Copy).then_inc(p_copied, 1)
                if n >= 3:
                    u = n - 3
                    h, q = UNITS[u]
                    act.wait_ge(p_out, u + 1)
                    nc.scalar.activation(HH[:, NPOOL + h, q * P:(q + 1) * P], PS[:, 6 + u % 2, 0:P], ACT.Copy
                                         ).then_inc(p_high, 1)

            def diagonal(q, n=NH):
                return q.rearrange("p (h x) -> p h x", h=n)[:, :, 0:DT]

            turned_out = PS[:, :, :].rearrange("p b n -> p (b n)")[:, 5 * 512:5 * 512 + NH * (NS + DT)]

            def query_high(b):
                act.wait_ge(out_read, 1)
                if not isinstance(b, int):
                    act.wait_ge(k_scored, b * (NCH + 1))
                cols = slice(SEQ, SEQ + DT) if isinstance(b, int) else bass.ds(b * DT + SEQ, DT)
                nc.scalar.activation(diagonal(qh[:, :]), qkT[:, 0:NH, cols], ACT.Copy, scale=ATT_SCALE
                                     ).then_inc(q_high, 1)

            def key_high(b, n):
                c = n // 2
                act.wait_ge(kt_turned, b * NPG + (n + 1))
                if not (isinstance(b, int) and c < 2):
                    act.wait_ge(k_scored, b * (NCH + 1) + (c - 1 if c >= 2 else c - 2))
                nc.scalar.activation(kth[:, c % 2, :, (n % 2) * PAGE:(n % 2 + 1) * PAGE],
                                     PS[:, 2 * (n % 2):2 * (n % 2) + 2, :].rearrange("p a (h k) -> p (a h) k", h=4),
                                     ACT.Copy).then_inc(kt_high, 1)

            def value_high(b, n):
                act.wait_ge(v_in[n % 4], b * (4 * NPG) + (16 * (n // 4 + 1) - 4 * NPG))
                if n < 2:
                    act.wait_ge(out_read, b)
                else:
                    act.wait_ge(v_used, b * NPG + (n - 1 - NPG))
                nc.scalar.activation(vhigh[:, n % 2, :], vpage[:, n % 4, :], ACT.Copy).then_inc(v_high, 1)

            def exponent(b):
                act.wait_ge(s_max, b)
                nc.scalar.activation(prob[:, :], prob[:, :], ACT.Exp, bias=small[0:NS, 129:130],
                                     accum_out=small[0:NS, 130:131]).then_inc(s_exp, 1)

            def prob_high(b, g):
                act.wait_ge(pt_turned, b * 3 + (g - 2))
                if g == 0:
                    act.wait_ge(out_read, b)
                n0, n1 = GROUPS[g]
                nc.scalar.activation(pth[:, n0:n1, :].rearrange("p n r -> p (n r)"),
                                     PS[:, 5, 0:(n1 - n0) * NS], ACT.Copy).then_inc(pt_high, 1)

            def sequence(b, keys, values):
                if keys:
                    query_high(b)
                for c in range(NCH + 1):
                    if values and c == 1:
                        exponent(b)
                    for n in (2 * c, 2 * c + 1):
                        if keys and c < NCH:
                            key_high(b, n)
                    if values and c in (1, 2):
                        prob_high(b, c - 1)
                    if values and c >= 1:
                        value_high(b, 2 * c - 2)
                        value_high(b, 2 * c - 1)
                    if values and c == 3:
                        prob_high(b, 2)
                    if not keys and c >= NCH // 2:
                        for f in ((2 * c - NCH, 2 * c - NCH + 1) if c < NCH else ()):
                            if f == 0 or f == NPOOL // 2:
                                act.wait_ge(d_back, 16 * (1 + f // 4))
                            nc.scalar.activation(DH[:, f, :], dback[:, f, :], ACT.Copy).then_inc(df_high, 1)
                if not keys:
                    for i in range(2):
                        act.wait_ge(v_low[i], DB * NPG // 2)
                    high(S_POOL, 0)
                    high(S_OUT, 1)
                if values:
                    act.wait_ge(o_turned, b)
                    cols = slice(NT - DT, NT) if isinstance(b, int) else bass.ds(b * DT + (SEQ - DT), DT)
                    nc.scalar.activation(HH[:, NPOOL:2 * NPOOL, cols], diagonal(turned_out), ACT.Copy
                                         ).then_inc(sy_high, 1)

            nc.scalar.activation(knh[:, :, :], qkT[:, NH:2 * NH, SEQ:NT], ACT.Copy).then_inc(kn_high, 1)
            act.wait_ge(vnew_in, 16)
            act.wait_ge(out_read, 1)
            nc.scalar.activation(vnh[:, :], vraw[:, :], ACT.Copy).then_inc(vn_high, 1)
            act.wait_ge(vn_low, 1)
            sequence(0, True, False)
            with act.Fori(1, DB) as b:
                sequence(b, True, True)
            sequence(DB, False, True)

            act.wait_ge(df_low, NPOOL)
            for o in range(NPOOL):
                act.wait_ge(pool_done, o + 1) if o < NPOOL - 1 else act.wait_ge(slot_done, S_OUT)
                nc.scalar.activation(halves(HH[:, o, :]), pair(o), ACT.Copy, scale=gains[:, 3, o:o + 1]
                                     ).then_inc(pool_high, 1)

            high(S_OUT + 1, 0)
            with act.Fori(0, KT // 2 - 1) as i:
                for j in range(2):
                    act.wait_ge(raw_in[1 - j], 16 * i + 16 * ((S_OUT + 2 + j) // 2 + 1))
                    act.wait_ge(slot_done, 2 * i + (S_OUT + 1 + j))
                    nc.scalar.activation(wh[:, 1 - j, :], raw[:, 1 - j, :], ACT.Copy).then_inc(high_ready, 1)
            for s in (S_FF, S_FF + 1):
                high(s, s % 2)
            act.wait_ge(psum_read, G_FF)
            squares(1)
            root(1)
            for f in range(KT):
                act.wait_ge(xn_ready, KT + f + 1)
                nc.scalar.activation(HH[:, f, :], xn[:, f % 2, :], ACT.Copy, scale=gains[:, 1, f:f + 1]
                                     ).then_inc(norm_high, 1)

            def ff_step(i, j, more):
                if more:
                    p = (S_FF + j) % 2
                    act.wait_ge(raw_in[p], 16 * (PER_CHUNK // 2) * i + 16 * ((S_FF + j + 2) // 2 + 1))
                    act.wait_ge(slot_done, PER_CHUNK * i + (S_FF + j + 1))
                    nc.scalar.activation(wh[:, p, :], raw[:, p, :], ACT.Copy).then_inc(high_ready, 1)
                if j >= 2 * FT:
                    return
                f = j // 2
                if j % 2 == 0:
                    act.wait_ge(slot_done, PER_CHUNK * i + (S_FF + j + 1))
                    act.wait_ge(psum_read, READ_CHUNK * i + G_FF + (f - 1 if f >= 2 else 0))
                    nc.scalar.activation(halves(sg[:, f % 2, :]), pair(j), ACT.Silu).then_inc(silu_done, 1)
                else:
                    act.wait_ge(psum_read, READ_CHUNK * i + (G_FF + f + 1))
                    nc.scalar.activation(GH[:, f, :], hid[:, f % 2, :], ACT.Copy).then_inc(hid_high, 1)

            with act.Fori(0, CHUNKS - 1) as i:
                for j in range(PER_CHUNK):
                    ff_step(i, j, True)
            for j in range(PER_CHUNK):
                ff_step(CHUNKS - 1, j, j + 2 < PER_CHUNK)

            act.wait_ge(psum_read, G_FF + READ_CHUNK * CHUNKS)
            squares(2)
            root(2)
            for f in range(KT + 1):
                if f < KT:
                    act.wait_ge(xn_ready, 2 * KT + f + 1)
                    if f >= 2:
                        act.wait_ge(y_turned, f - 1)
                    nc.scalar.activation(sq[:, f % 2, :], xn[:, f % 2, :], ACT.Copy, scale=gains[:, 2, f:f + 1]
                                         ).then_inc(y_ready, 1)
                if f:
                    g = f - 1
                    act.wait_ge(y_turned, g + 1)
                    nc.scalar.activation(yrow[:, 0:4, g * P:(g + 1) * P],
                                         PS[:, 2 * (g % 2), :].rearrange("p (a d) -> p a d", a=4), ACT.Copy
                                         ).then_inc(y_copied_act, 1)

            for t in range(2):
                act.wait_ge(turn_out[t], 32 * len(TURNS[t::2]))
                act.wait_ge(u_out[t], 16 * (DB + 1) * (NPOOL // 2))

        @block.vector
        def _(dve):
            link = Chain(dve, dve_seq)
            v = nc.vector
            link(v.memset(T2[:, :, 0:16], 0.0))
            for n in range(1, 20, 2):
                t, f = n // 4, 4 * (n % 4)
                dve.wait_ge(x_turned, n + 1)
                v.tensor_copy(XT[:, f:f + 4, t * P:t * P + ROWS[t]],
                              PS[:, 4 + n % 4, :].rearrange("p (j t) -> p j t", j=4)[:, :, 0:ROWS[t]]
                              ).then_inc(x_copied_dve, 1)

            def norm(m, low=True):
                for f in range(KT):
                    dve.wait_ge(sq_ready, KT * m + f + 1)
                    if f == 0:
                        v.tensor_copy(ss[:, :], sq[:, 0, :]).then_inc(sq_added, 1)
                    else:
                        dve.wait_ge(sq_added, KT * m + f)
                        v.tensor_tensor(ss[:, :], ss[:, :], sq[:, f % 2, :], ALU.add).then_inc(sq_added, 1)
                dve.wait_ge(ss_bcast, m + 1)
                link(v.tensor_scalar(halves(rstd[:, :]), PS[:, 4:6, 0:HALF], 1.0 / D, EPS, ALU.mult, ALU.add))
                v.reciprocal(rstd[:, :], rstd[:, :]).then_inc(inv_ready, 1)
                dve.wait_ge(rstd_ready, m + 1)

                def scaled(f):
                    if f >= 2:
                        dve.wait_ge(norm_high, KT * m + f - 1) if low else dve.wait_ge(y_ready, f - 1)
                        if low:
                            dve.wait_ge(norm_low, KT * m + f - 1)
                    v.tensor_tensor(xn[:, f % 2, :], XT[:, f, :], rstd[:, :], ALU.mult).then_inc(xn_ready, 1)

                scaled(0)
                for f in range(KT):
                    if f + 1 < KT:
                        scaled(f + 1)
                    if low:
                        dve.wait_ge(norm_high, KT * m + f + 1)
                        v.scalar_tensor_tensor(out=HL[:, f, :], in0=xn[:, f % 2, :], scalar=gains[:, m, f:f + 1],
                                               in1=HH[:, f, :].bitcast(F32), op0=ALU.mult, op1=ALU.subtract
                                               ).then_inc(norm_low, 1)
                    else:
                        dve.wait_ge(y_turned, f + 1)
                        v.tensor_copy(yrow[0:NS, 4, f * P:(f + 1) * P], PS[0:NS, 2 * (f % 2) + 1, 0:P]
                                      ).then_inc(y_copied_dve, 1)

            dve.wait_ge(x_copied_act, 10)
            dve.wait_ge(x_copied_dve, 10)
            dve.wait_ge(gains_turned, 1)
            v.tensor_copy(gains[:, :, :].rearrange("p n k -> p (n k)")[:, 0:3 * KT + NPOOL],
                          PS[:, 3, 0:3 * KT + NPOOL]).then_inc(gains_ready, 1)
            norm(0)

            cos, sin = cst[:, K_COS:K_COS + NT], cst[:, K_SIN:K_SIN + NT]

            link(v.memset(pscore[:, :], 0.0))
            for blk in BLOCKS:
                o = BLK_OFF[blk] + blk * P
                link(v.tensor_copy(pscore[:, o:o + P], cst[:, K_TRI:K_TRI + P]))

            def idx_add(h):
                for n, blk in enumerate(BLOCKS):
                    o, w = BLK_OFF[blk], (blk + 1) * P
                    dve.wait_ge(idx_relu, 3 * h + n + 1)
                    if h:
                        dve.wait_ge(idx_added, 3 * (h - 1) + n + 1)
                    v.scalar_tensor_tensor(out=pscore[:, o:o + w], in0=pr[:, o:o + w], scalar=wtok[:, blk, h:h + 1],
                                           in1=pscore[:, o:o + w], op0=ALU.mult, op1=ALU.add).then_inc(idx_added, 1)

            def sample_indexer():
                for b in range(DB):
                    for c in range(4):
                        n = 9 * b + c
                        dve.wait_ge(ik_turned, 4 * b + c + 1)
                        if b == 0 and c == 0:
                            dve.wait_ge(x_kept, 16)
                        if b >= 2:
                            dve.wait_ge(is_scored, 5 * (b - 1))
                        v.tensor_copy(ikT[:, b % 2, c * 512:(c + 1) * 512], PS[:, 5 + n % 3, :]).then_inc(ik_copied, 1)
                    v.tensor_copy(ikT[:, b % 2, PAST:NKEY], kiT[:, SEQ + b * DT:SEQ + (b + 1) * DT]
                                  ).then_inc(ik_new, 1)
                dve.wait_ge(is_summed, 5 * DB)
                v.tensor_copy(sscore[:, 0:PAST].rearrange("p (c n) -> p c n", c=4), PS[0:NS, 0:4, :])
                v.tensor_tensor(sscore[:, PAST:NKEY], PS[0:NS, 4, 0:DT], cst[0:NS, K_NEW:K_NEW + DT], ALU.add
                                ).then_inc(ss_copied, 1)
                dve.wait_ge(ss_copied, 1)

            def sample_round():
                link(v.max(small[0:NS, 0:8], sscore[:, :]))
                link(v.match_replace(sscore[:, :], small[0:NS, 0:8], sscore[:, :], TAKEN))

            def prompt_round():
                for n, blk in enumerate(BLOCKS):
                    o, w = BLK_OFF[blk], (blk + 1) * P
                    link(v.max(small[:, 8 + 8 * n:16 + 8 * n], pscore[:, o:o + w]))
                for n, blk in enumerate(BLOCKS):
                    o, w = BLK_OFF[blk], (blk + 1) * P
                    link(v.match_replace(pscore[:, o:o + w], small[:, 8 + 8 * n:16 + 8 * n], pscore[:, o:o + w],
                                         TAKEN))

            def pooled(f):
                g = f // 2
                e = T2[:, f % 2, :]
                if f:
                    dve.wait_ge(d_ready, f)
                v.tensor_copy(ES[:, :, 0:STATE], stateT[:, f, :].rearrange("p (b t) -> p b t", b=DB))
                link(v.tensor_copy(ES[:, :, STATE:STATE + DT], e[:, 16 + SEQ:16 + NT].rearrange("p (b t) -> p b t", b=DB)))
                cur_p, cur_s = e[:, 0:16 + SEQ], ES[:, :, :]
                for m in range(g + 1):
                    sh = 1 << m
                    o = (1 << (m + 1)) - 1
                    nxt_p, nxt_s = win[:, m % 2, :], wins[:, m % 2, :, :]
                    v.tensor_tensor(nxt_p[:, o:16 + SEQ], cur_p[:, o:16 + SEQ], cur_p[:, o - sh:16 + SEQ - sh], ALU.add)
                    link(v.tensor_tensor(nxt_s[:, :, o:STATE + DT], cur_s[:, :, o:STATE + DT],
                                         cur_s[:, :, o - sh:STATE + DT - sh], ALU.add))
                    cur_p, cur_s = nxt_p, nxt_s
                w = WINDOWS[g]
                link(v.tensor_tensor(cur_p[:, 16:16 + STATE], cur_p[:, 16:16 + STATE],
                                     cst[:, K_CNT + 16 * g:K_CNT + 16 * g + STATE], ALU.mult))
                if f:
                    dve.wait_ge(d_kept, 16 * f)
                dp = rtmp
                v.scalar_tensor_tensor(out=dp[:, 0:SEQ], in0=cur_p[:, 16:16 + SEQ], scalar=1.0 / w,
                                       in1=e[:, 16:16 + SEQ], op0=ALU.mult, op1=ALU.subtract)
                v.scalar_tensor_tensor(out=dp[:, SEQ:NT].rearrange("p (b t) -> p b t", b=DB),
                                       in0=cur_s[:, :, STATE:STATE + DT], scalar=1.0 / w,
                                       in1=ES[:, :, STATE:STATE + DT], op0=ALU.mult, op1=ALU.subtract
                                       ).then_inc(d_ready, 1)

            rounds = 0
            for s in range(S_POOL):
                dve.wait_ge(slot_done, s + 1)
                j = s % 2
                if s == S_KI:
                    dst = kiT[:, :]
                elif s >= S_UP or S_V <= s < S_Q or s == S_WI:
                    dst = None
                elif s >= S_Q:
                    dst = qkT[:, s - S_Q, :]
                else:
                    dst = T2[:, j, 16:16 + NT]
                if S_QI + 2 <= s < S_Q:
                    if s < S_K + 2:
                        dve.wait_ge(idx_scored, 3 * (min(s, S_K + 1) - 2 - S_QI + 1))
                        dve.wait_ge(qis_copied, min(s, S_K + 1) - 2 - S_QI + 1)
                    else:
                        dve.wait_ge(turned, s - S_K)
                        dve.wait_ge(k_kept, min(s - 1 - S_K, NH))
                if s == S_Q:
                    dve.wait_ge(is_summed, 5 * DB)
                if s == S_WI:
                    v.tensor_copy(halves(wiT[:, :]), pair(s, IH)).then_inc(psum_read, 1)
                elif dst is not None:
                    src = pair(s)
                    n_roped = s - NH if s >= S_Q else s if s else 1
                    if s:
                        dve.wait_ge(roped, n_roped - 1)
                    v.tensor_tensor(halves(rtmp[64:128, :]), src[0:64], halves(sin[0:64]), ALU.mult)
                    v.tensor_tensor(halves(rtmp[0:64, :]), src[64:128], halves(sin[64:128]), ALU.mult)
                    v.tensor_tensor(halves(dst), src, halves(cos), ALU.mult).then_inc(psum_read, 1)
                    dve.wait_ge(psum_read, s + 1)
                    v.tensor_tensor(dst, dst, rtmp[:, :], ALU.add).then_inc(roped, 1)
                elif s < S_Q:
                    v.tensor_copy(halves(T2[:, j, 16:16 + NT]), pair(s)).then_inc(psum_read, 1)
                else:
                    f = s - S_UP
                    if f >= 2:
                        dve.wait_ge(u_turned, f - 1)
                    else:
                        dve.wait_ge(turned, 2 * NH + 1)
                    v.tensor_copy(halves(T2[:, j, 16:16 + NT]), pair(s)).then_inc(psum_read, 1)
                    dve.wait_ge(psum_read, s + 1)
                    pooled(f)
                if s == S_UP - 1:
                    dve.wait_ge(state_turned, 1)
                    link(v.tensor_copy(stateT[:, :, :].rearrange("p (a f) r -> p a (f r)", a=2),
                                       PS[:, 6:8, 0:4 * DB * STATE]))
                if s == S_QI:
                    dve.wait_ge(wi_turned, 1)
                    v.memset(wrow[:, :], 0.0)
                    link(v.tensor_copy(wtok[:, 1:4, :], PS[:, 7, IH:4 * IH].rearrange("p (a h) -> p a h", a=3)))
                    v.tensor_tensor(wrow[:, :].rearrange("p (b x) -> p b x", b=DB)[:, :, 0:DT],
                                    PS[:, 7, 128:128 + NS].rearrange("p (b q) -> p b q", b=DB),
                                    cst[:, K_DIAG:K_DIAG + NS].rearrange("p (b q) -> p b q", b=DB), ALU.mult
                                    ).then_inc(wrow_ready, 1)
                if S_QI < s < S_K:
                    idx_add(s - 1 - S_QI)
                if s == S_K - 1:
                    idx_add(IH - 1)
                    sample_indexer()
                if S_K <= s < S_Q:
                    sample_round()
                    prompt_round()
                if S_Q <= s < S_UP:
                    sample_round()
                    sample_round()
            link(v.tensor_scalar(pscore[:, :], pscore[:, :], TAKEN, HIDE, ALU.not_equal, ALU.mult))
            for t in range(2):
                dve.wait_ge(turn_out[t], 32 * len(TURNS[t::2]))
            v.tensor_scalar(maskS[:, :], sscore[:, :], TAKEN, HIDE, ALU.not_equal, ALU.mult).then_inc(bias_ready, 1)
            dve.wait_ge(bias_ready, 1)
            v.tensor_tensor(maskN[:, :].rearrange("r (b t) -> r b t", b=DB),
                            maskS[:, PAST:NKEY].bitcast(F32).rearrange("r (o t) -> r o t", o=1
                                                                      ).broadcast_to([NS, DB, DT]),
                            cst[0:NS, K_OTHER:K_OTHER + NS].rearrange("r (b t) -> r b t", b=DB), ALU.add
                            ).then_inc(mask_ready, 1)

            UNITS = [(h, q) for h in range(NH) for q in range(4)]
            U = len(UNITS)
            dve.wait_ge(slot_done, S_POOL)
            dve.wait_ge(low_ready, S_POOL)
            for n in range(U + 4):
                if n < U:
                    h, q = UNITS[n]
                    w = (q + 1) * P
                    mask = pscore[:, BLK_OFF[q]:BLK_OFF[q] + w] if q else cst[:, K_TRI:K_TRI + P]
                    dve.wait_ge(p_scored, n + 1)
                    if n >= 3:
                        dve.wait_ge(p_turned, n - 2)
                    link(v.tensor_tensor_reduce(out=px[:, n % 3, 0:w], in0=PS[:, n % 3, 0:w], in1=mask,
                                                scale=ATT_SCALE, scalar=-3.0e38, op0=ALU.add, op1=ALU.max,
                                                accum_out=small[:, n:n + 1]))
                    v.tensor_scalar(small[:, 32 + n:33 + n], small[:, n:n + 1], -1.0, None, ALU.mult
                                    ).then_inc(p_max, 1)
                if 1 <= n <= U:
                    u = n - 1
                    w = (UNITS[u][1] + 1) * P
                    dve.wait_ge(p_exp, u + 1)
                    link(v.reciprocal(small[:, 96 + u:97 + u], small[:, 64 + u:65 + u]))
                    v.tensor_scalar(px[:, u % 3, 0:w], px[:, u % 3, 0:w], small[:, 96 + u:97 + u], None, ALU.mult
                                    ).then_inc(p_norm, 1)
                if n >= 4:
                    u = n - 4
                    h, q = UNITS[u]
                    dve.wait_ge(p_high, u + 1)
                    v.tensor_tensor(HL[:, NPOOL + h, q * P:(q + 1) * P], PS[:, 6 + u % 2, 0:P],
                                    HH[:, NPOOL + h, q * P:(q + 1) * P].bitcast(F32), ALU.subtract
                                    ).then_inc(p_low, 1)

            def diagonal(q):
                return q.rearrange("p (h x) -> p h x", h=NH)[:, :, 0:DT]

            turned_out = PS[:, :, :].rearrange("p b n -> p (b n)")[:, 5 * 512:5 * 512 + NH * (NS + DT)]

            def query_low(b):
                dve.wait_ge(q_high, b + 1)
                cols = slice(SEQ, SEQ + DT) if isinstance(b, int) else bass.ds(b * DT + SEQ, DT)
                v.scalar_tensor_tensor(out=diagonal(ql[:, :]), in0=qkT[:, 0:NH, cols], scalar=ATT_SCALE,
                                       in1=diagonal(qh[:, :].bitcast(F32)), op0=ALU.mult, op1=ALU.subtract
                                       ).then_inc(q_low, 1)
                own = slice(0, DT) if isinstance(b, int) else bass.ds(b * DT, DT)
                v.tensor_copy(pick[:, :].rearrange("r (h q) -> r h q", h=NH),
                              cst[0:NS, own].rearrange("r (o q) -> r o q", o=1).broadcast_to([NS, NH, DT])
                              ).then_inc(pick_ready, 1)

            def key_low(b, n):
                c = n // 2
                dve.wait_ge(kt_high, b * NPG + (n + 1))
                place = (slice(None), c % 2, slice(None), slice((n % 2) * PAGE, (n % 2 + 1) * PAGE))
                v.tensor_tensor(ktl[place], PS[:, 2 * (n % 2):2 * (n % 2) + 2, :].rearrange(
                    "p a (h k) -> p (a h) k", h=4), kth[place].bitcast(F32), ALU.subtract).then_inc(kt_low, 1)

            def value_low(b, n):
                dve.wait_ge(v_high, b * NPG + (n + 1 - NPG))
                v.tensor_tensor(vlow[:, 1, :], vpage[:, n % 4, :], vhigh[:, 1, :].bitcast(F32), ALU.subtract
                                ).then_inc(v_low[1], 1)

            def scores(b, c):
                dve.wait_ge(k_scored, b * (NCH + 1) + (c + 1))
                if not isinstance(b, int):
                    dve.wait_ge(pt_turned, b * 3 + (c // 3 - 2))
                w = CHUNK if c < NCH else NS
                v.tensor_copy(prob[:, c * CHUNK:c * CHUNK + w], PS[0:NS, 4, 0:w]).then_inc(s_copied, 1)
                dve.wait_ge(s_copied, b * (NCH + 1) + (c + 1))
                v.tensor_reduce(small[0:NS, c:c + 1], prob[:, c * CHUNK:c * CHUNK + w], AX.X, ALU.max
                                ).then_inc(part_max, 1)

            def maxima(b):
                dve.wait_ge(part_max, b * (NCH + 1))
                link(v.tensor_reduce(small[0:NS, 128:129], small[0:NS, 0:NCH + 1], AX.X, ALU.max))
                v.tensor_scalar(small[0:NS, 129:130], small[0:NS, 128:129], -1.0, None, ALU.mult).then_inc(s_max, 1)

            def prob_low(b, g):
                dve.wait_ge(pt_high, b * 3 + (g - 2))
                n0, n1 = GROUPS[g]
                v.tensor_tensor(ptl[:, n0:n1, :].rearrange("p n r -> p (n r)"), PS[:, 5, 0:(n1 - n0) * NS],
                                pth[:, n0:n1, :].bitcast(F32).rearrange("p n r -> p (n r)"), ALU.subtract
                                ).then_inc(pt_low, 1)

            def sequence(b, keys, values):
                if values:
                    maxima(b)
                if keys:
                    query_low(b)
                for c in range(NCH + 1):
                    for n in (2 * c, 2 * c + 1):
                        if keys and c < NCH:
                            key_low(b, n)
                    if values and c in (1, 2):
                        prob_low(b, c - 1)
                    if keys and c:
                        scores(b, c - 1)
                    if values and c:
                        value_low(b, 2 * c - 1)
                    if values and c == 3:
                        prob_low(b, 2)
                    if not keys and NCH // 2 <= c < NCH:
                        for f in (2 * c - NCH, 2 * c - NCH + 1):
                            dve.wait_ge(df_high, f + 1)
                            v.tensor_tensor(DL[:, f, :], dback[:, f, :], DH[:, f, :].bitcast(F32), ALU.subtract
                                            ).then_inc(df_low, 1)
                if values:
                    dve.wait_ge(s_exp, b)
                    v.reciprocal(small[0:NS, 131:132], small[0:NS, 130:131]).then_inc(s_inv, 1)
                    dve.wait_ge(s_inv, b)
                    dve.wait_ge(s_out, b)
                    v.tensor_scalar(orow[:, :], PS[0:NS, 6:8, :].rearrange("p a n -> p (a n)"),
                                    small[0:NS, 131:132], None, ALU.mult).then_inc(o_ready, 1)
                if keys:
                    scores(b, NCH)
                if values:
                    dve.wait_ge(sy_high, b)
                    cols = slice(NT - DT, NT) if isinstance(b, int) else bass.ds(b * DT + (SEQ - DT), DT)
                    v.tensor_tensor(HL[:, NPOOL:2 * NPOOL, cols], diagonal(turned_out),
                                    HH[:, NPOOL:2 * NPOOL, cols].bitcast(F32), ALU.subtract).then_inc(out_read, 1)

            dve.wait_ge(p_low, U)
            dve.wait_ge(d_kept, 16 * NPOOL)
            for t in range(2):
                dve.wait_ge(u_out[t], 16 * (DB + 1) * (NPOOL // 2))
            v.memset(ql[:, :].bitcast(F32), 0.0)
            v.memset(qh[:, :].bitcast(F32), 0.0).then_inc(out_read, 1)
            dve.wait_ge(kn_high, 1)
            v.tensor_tensor(knl[:, :, :], qkT[:, NH:2 * NH, SEQ:NT], knh[:, :, :].bitcast(F32), ALU.subtract
                            ).then_inc(kn_low, 1)
            dve.wait_ge(vn_high, 1)
            v.tensor_tensor(vnl[:, :], vraw[:, :], vnh[:, :].bitcast(F32), ALU.subtract).then_inc(vn_low, 1)
            sequence(0, True, False)
            before = link.n
            with dve.Fori(1, DB) as b:
                link.more = b - 1
                sequence(b, True, True)
            link.more = 0
            assert link.n == before + 1
            link.n = before + DB - 1
            sequence(DB, False, True)

            for o in range(NPOOL):
                dve.wait_ge(pool_high, o + 1)
                v.scalar_tensor_tensor(out=halves(HL[:, o, :]), in0=pair(o), scalar=gains[:, 3, o:o + 1],
                                       in1=halves(HH[:, o, :].bitcast(F32)), op0=ALU.mult, op1=ALU.subtract
                                       ).then_inc(psum_read, 1)

            for o in range(KT):
                if o % 4 == 0:
                    dve.wait_ge(x_back[o // 4], 16)
                dve.wait_ge(slot_done, S_OUT + o + 1)
                v.tensor_tensor(halves(XT[:, o, :]), halves(XT[:, o, :]), pair(G_OUT + o), ALU.add
                                ).then_inc(psum_read, 1)
            norm(1)

            with dve.Fori(0, CHUNKS) as i:
                for f in range(FT):
                    dve.wait_ge(slot_done, PER_CHUNK * i + (S_FF + 2 * f + 2))
                    dve.wait_ge(silu_done, FT * i + (f + 1))
                    if f >= 2:
                        dve.wait_ge(hid_low, FT * i + (f - 1))
                    v.tensor_tensor(halves(hid[:, f % 2, :]), halves(sg[:, f % 2, :]), pair(1), ALU.mult
                                    ).then_inc(psum_read, 1)
                    dve.wait_ge(hid_high, FT * i + (f + 1))
                    v.tensor_tensor(GL[:, f, :], hid[:, f % 2, :], GH[:, f, :].bitcast(F32), ALU.subtract
                                    ).then_inc(hid_low, 1)
                for o in range(KT):
                    if o % 4 == 3:
                        dve.wait_ge(slot_done, PER_CHUNK * i + (S_FF + 2 * FT + o // 4 + 1))
                    else:
                        dve.wait_ge(down_done, 12 * i + (3 * (o // 4) + o % 4 + 1))
                    v.tensor_tensor(halves(XT[:, o, :]), halves(XT[:, o, :]), pair(o), ALU.add).then_inc(psum_read, 1)
            norm(2, low=False)


_INS = ["x_prompt", "x_sample", "cache_k", "cache_v", "cache_idx_k", "state_pool", "page_table", "g_mix", "w_in",
        "w_pool", "s_pool", "w_out", "g_ffn", "w_gate", "w_up", "w_down", "g_final"]
_OUTS = [(1, SEQ, D), (DB, DT, D), (1, 1, SEQ, NH, HD), (1, 1, SEQ, NH, HD), (1, 1, SEQ, HD), (1, 1, STATE, POOL_W),
         (1, DB, DT, NH, HD), (1, DB, DT, NH, HD), (1, DB, DT, HD), (1, DB, STATE, POOL_W)]


def kernel(**inputs):
    import numpy as np
    import concourse.bacc as bacc
    from concourse.bass_utils import run_bass_kernel_spmd

    nc = bacc.Bacc("TRN2", target_bir_lowering=False, num_devices=1)
    arrays = {f"in_{n}": np.ascontiguousarray(inputs[n]) for n in _INS}
    arrays["in_const"] = constants()
    args = [nc.dram_tensor(n, a.shape, mybir.dt.from_np(a.dtype), kind="ExternalInput").ap()
            for n, a in arrays.items()]
    outs = [nc.dram_tensor(f"out_{i}", s, F32, kind="ExternalOutput").ap() for i, s in enumerate(_OUTS)]
    build(nc, *args, outs)
    r = run_bass_kernel_spmd(nc, [arrays], core_ids=[0])
    return tuple(r.results[0][f"out_{i}"] for i in range(len(_OUTS)))
```

```python
from contextlib import ExitStack

import concourse.bass as bass
from concourse import mybir

F32 = mybir.dt.float32
F32R = mybir.dt.float32r
I32 = mybir.dt.int32
ALU = mybir.AluOpType
ACT = mybir.ActivationFunctionType
AX = mybir.AxisListType

P = 128
D = 2048
KT = D // P
SEQ = 512
DB = 8
DT = 8
NS = DB * DT
NT = SEQ + NS
HALF = NT // 2
PAGE = 128
NPG = 16
PAST = NPG * PAGE
NKEY = PAST + DT
CHUNK = 2 * PAGE
NCH = PAST // CHUNK
GROUPS = ((0, 6), (6, 12), (12, NPG + 1))
POOL_W = 1024
NPOOL = POOL_W // P
WINDOWS = (2, 4, 8, 16)
STATE = 15
HD = 128
NH = 8
IH = 16
TOPK_P = 128
TOPK_S = 256
DFF = 5632
FT = 4
CHUNKS = DFF // (FT * P)
EPS = 1e-6
PAST_MASK = -3.0e38
TAKEN = -3.4e38
HIDE = -2.0 ** 100
ATT_SCALE = float(HD) ** -0.5
IDX_SCALE = float(HD) ** -0.5 * float(IH) ** -0.5

C_UP, C_Q, C_K, C_V, C_QI, C_KI = 0, 1024, 2048, 3072, 4096, 6144
C_WI_TILE = C_KI + P + IH - P

S_KI, S_WI, S_QI = 0, 1, 2
S_K = S_QI + IH
S_V = S_K + NH
S_Q = S_V + NH
S_UP = S_Q + NH
S_POOL = S_UP + NPOOL
S_OUT = S_POOL + 1
S_FF = S_OUT + KT
PER_CHUNK = 3 * FT
N_SLOTS = S_FF + CHUNKS * PER_CHUNK
G_POOL = S_POOL
G_OUT = G_POOL + NPOOL
G_FF = G_OUT + KT
READ_CHUNK = FT + KT

BLOCKS = (1, 2, 3)
BLK_OFF = {1: 0, 2: 256, 3: 640}
BLK_W = 1152

K_IDENT, K_ONES, K_COS, K_SIN, K_REP, K_DIAG, K_TRI, K_NEW, K_CNT = 0, 128, 256, 832, 1408, 1536, 1600, 1728, 1736
K_OTHER = K_CNT + 64
K_ALL = K_OTHER + NS


def constants():
    import numpy as np

    c = np.zeros((P, K_ALL), np.float32)
    c[:, K_IDENT:K_IDENT + P] = np.eye(P)
    c[:, K_ONES:K_ONES + P] = 1.0
    pos = np.concatenate([np.arange(SEQ), np.tile(PAST + np.arange(DT), DB)]).astype(np.float32)
    inv = (10000.0 ** (-(np.arange(HD // 2) / (HD // 2)))).astype(np.float32)
    ang = (pos[None, :] * inv[:, None]).astype(np.float32).astype(np.float64)
    c[:, K_COS:K_COS + NT] = np.tile(np.cos(ang), (2, 1))
    c[:, K_SIN:K_SIN + NT] = np.concatenate([np.sin(ang), -np.sin(ang)], 0)
    for h in range(IH):
        c[h, K_REP + h * DT:K_REP + (h + 1) * DT] = 1.0
    for p in range(P):
        c[p, K_DIAG + p % DT:K_DIAG + NS:DT] = 1.0
    c[:, K_TRI:K_TRI + P] = np.where(np.arange(P)[None, :] > np.arange(P)[:, None], PAST_MASK, 0.0)
    for r in range(NS):
        c[r, K_NEW:K_NEW + DT] = np.where(np.arange(DT) > r % DT, PAST_MASK, 0.0)
        c[r, K_OTHER:K_OTHER + NS] = np.where(np.arange(NS) // DT != r // DT, HIDE, 0.0)
    for g, w in enumerate(WINDOWS):
        for t in range(STATE):
            c[:, K_CNT + g * 16 + t] = w / min(w, t + 1)
    return c


def build(nc, x_prompt, x_sample, cache_k, cache_v, cache_idx_k, state_pool, page_table, g_mix, w_in,
          w_pool, s_pool, w_out, g_ffn, w_gate, w_up, w_down, g_final, const, outs):
    (y_prompt, y_sample, k_prompt, v_prompt, idx_k_prompt, pool_prompt,
     k_sample, v_sample, idx_k_sample, pool_sample) = outs
    n_phys = cache_k.shape[1]
    ctx = ExitStack()
    with ctx:
        base = (nc.sbuf_base + 31) // 32 * 32
        OFF_A = base
        OFF_W = OFF_A + 2 * KT * NT * 4
        OFF_C = OFF_W + 6 * D * 4
        OFF_M = OFF_C + KT * NT * 4

        def at(name, offset, shape, dt=F32):
            return nc.alloc_sbuf_tensor_at(name, shape, dt, offset=offset)

        class Place:

            def __init__(self, offset):
                self.offset = offset

            def __call__(self, name, shape, dt=F32):
                size = 4
                for n in shape[1:]:
                    size *= n
                t = at(name, self.offset, shape, dt)
                self.offset += (size + 31) // 32 * 32
                return t

        in_a = Place(OFF_A)
        HH = in_a("HH", [P, KT, NT], F32R)
        HL = in_a("HL", [P, KT, NT], F32R)
        xin = at("xin", OFF_A, [P, 5, D])
        yrow = at("yrow", OFF_A, [P, 5, D])
        in_a = Place(OFF_A)
        kth = in_a("kth", [P, 2, NH, CHUNK], F32R)
        knh = in_a("knh", [P, NH, NS], F32R)
        vraw = at("vraw", OFF_A, [NS, NH * HD])
        in_a = Place(OFF_A + KT * NT * 4)
        ktl = in_a("ktl", [P, 2, NH, CHUNK], F32R)
        knl = in_a("knl", [P, NH, NS], F32R)
        in_w = Place(OFF_W)
        raw = in_w("raw", [P, 2, D])
        wh = in_w("wh", [P, 2, D], F32R)
        wl = in_w("wl", [P, 2, D], F32R)
        in_w = Place(OFF_W)
        kpage = in_w("kpage", [P, 4, NH * HD])
        vpage = in_w("vpage", [P, 4, NH * HD])
        vhigh = in_w("vhigh", [P, 2, NH * HD], F32R)
        vlow = in_w("vlow", [P, 2, NH * HD], F32R)
        in_a = Place(OFF_A + KT * NT * 4)
        vhigh2 = in_a("vhigh2", [P, 2, NH * HD], F32R)
        vlow2 = in_a("vlow2", [P, 2, NH * HD], F32R)

        def is_number(b, number):
            return isinstance(b, int) and b == number

        def tokens(b, first):
            return slice(first + b * DT, first + (b + 1) * DT) if isinstance(b, int) else bass.ds(b * DT + first, DT)

        def diagonal(q):
            return q.rearrange("p (h x) -> p h x", h=NH)[:, :, 0:DT]

        def value_halves(n, last):
            if last and n % 4 >= 2:
                return vhigh2[:, n % 2, :], vlow2[:, n % 2, :]
            return vhigh[:, n % 2, :], vlow[:, n % 2, :]

        vprompt = at("vprompt", OFF_W + 4 * NH * HD * 4, [P, 4, NH * HD])
        in_w = Place(OFF_W + 8 * NH * HD * 4)
        px = in_w("px", [P, 3, SEQ])
        pxt = in_w("pxt", [P, 3, SEQ])
        XT = at("XT", OFF_C, [P, KT, NT])
        qkT = at("qkT", OFF_C, [P, 2 * NH, NT])
        in_c = Place(OFF_C)
        ikraw = in_c("ikraw", [P, 4, 4 * HD])
        ikT = in_c("ikT", [P, 2, NKEY])
        irelu = in_c("irelu", [P, 3, 512])
        in_c = Place(OFF_C)
        DH = in_c("DH", [P, NPOOL, NT], F32R)
        DL = in_c("DL", [P, NPOOL, NT], F32R)
        in_m = Place(OFF_M)
        cst = in_m("cst", [P, K_ALL])
        gains = in_m("gains", [P, 4, KT])
        pages = in_m("pages", [1, DB * NPG], I32)
        stats = in_m("stats", [P, 8])
        ffn_from = in_m.offset
        t2_at = in_m.offset
        T2 = in_m("T2", [P, 2, 16 + NT])
        rtmp = in_m("rtmp", [P, NT])
        kiT = in_m("kiT", [P, NT])
        wtok = in_m("wtok", [P, 4, IH])
        pscore = in_m("pscore", [P, BLK_W])
        sscore_at = in_m.offset
        sscore = in_m("sscore", [NS, NKEY])
        small = in_m("small", [P, 136])
        stage_at = in_m.offset
        stage = in_m("stage", [P, 2, 5, P])
        spread = at("spread", sscore_at, [P, 5, P])
        maskS = at("maskS", sscore_at, [NS, NKEY], F32R)
        pool_wl = at("pool_wl", t2_at, [P, D], F32R)
        dback = at("dback", OFF_A, [P, NPOOL, NT])
        more = Place(t2_at)
        prob = more("prob", [NS, PAST + NS])
        qhl = more("qhl", [P, NS + NH * (2 * NS + DT)], F32R)
        ptn = more("ptn", [NS, 2 * NS], F32R)
        assert more.offset <= sscore_at
        more = Place(stage_at)
        orow = more("orow", [NS, NH * HD])
        pick = more("pick", [NS, NS], F32R)
        maskN = more("maskN", [NS, NS], F32R)
        assert more.offset <= stage_at + 2 * 5 * P * 4
        arena = in_m.offset
        in_m = Place(arena)
        sq = in_m("sq", [P, 2, NT])
        ss = in_m("ss", [P, NT])
        xn = in_m("xn", [P, 4, NT])
        grow = in_m("grow", [3 * KT + NPOOL, P])
        in_m = Place(arena)
        wiT = in_m("wiT", [IH, NT])
        wrow = in_m("wrow", [P, 576])
        pr = in_m("pr", [P, BLK_W])
        qis = in_m("qis", [P, DB, P])
        in_m = Place(arena)
        staterow = in_m("staterow", [DB * STATE, POOL_W])
        ust = in_m("ust", [NS, 2, P])
        upt = in_m("upt", [STATE, 2, P])
        ES = in_m("ES", [P, DB, STATE + DT + 1])
        win = in_m("win", [P, 2, 16 + SEQ])
        stateT = in_m("stateT", [P, NPOOL, DB * STATE])
        wins = in_m("wins", [P, 2, DB, STATE + DT + 1])
        in_m = Place(arena)
        vnh = in_m("vnh", [NS, NH * HD], F32R)
        vnl = in_m("vnl", [NS, NH * HD], F32R)
        pt = in_m("pt", [P, NPG, 2 * NS], F32R)
        in_m = Place(ffn_from)
        GH = in_m("GH", [P, FT, NT], F32R)
        GL = in_m("GL", [P, FT, NT], F32R)
        sg = in_m("sg", [P, 2, NT])
        hid = in_m("hid", [P, 2, NT])

        ident = cst[:, K_IDENT:K_IDENT + P]
        ones = cst[:, K_ONES:K_ONES + P]

        PS = ctx.enter_context(nc.psum_tensor("PS", [P, 8, 512], F32))

        def pair(g, rows=P):
            return PS[0:rows, 2 * (g % 2):2 * (g % 2) + 2, 0:HALF]

        turned_out = PS[:, :, :].rearrange("p b n -> p (b n)")[:, 5 * 512:5 * 512 + NH * (NS + DT)]

        def halves(ap):
            return ap.rearrange("p (a n) -> p a n", a=2)

        x_keep = nc.dram_tensor("x_keep", [P, KT * NT], F32, kind="Internal").ap()
        d_keep = nc.dram_tensor("d_keep", [P, NPOOL * NT], F32, kind="Internal").ap()

        def sem(name):
            return ctx.enter_context(nc.semaphore(name))

        ident_in, const_in, pages_in, gain_in = sem("ident_in"), sem("const_in"), sem("pages_in"), sem("gain_in")
        x_in = [sem(f"x_in{i}") for i in range(5)]
        raw_in = [sem(f"raw_in{i}") for i in range(2)]
        ik_in = [sem(f"ik_in{i}") for i in range(4)]
        k_in = [sem(f"k_in{i}") for i in range(4)]
        v_in = [sem(f"v_in{i}") for i in range(4)]
        vnew_in, vprompt_in, state_in = sem("vnew_in"), sem("vprompt_in"), sem("state_in")
        x_kept, x_back, d_kept = sem("x_kept"), [sem(f"x_back{i}") for i in range(4)], sem("d_kept")
        d_back = sem("d_back")
        gains_turned, gains_ready = sem("gains_turned"), sem("gains_ready")
        high_ready, low_ready, slot_done = sem("high_ready"), sem("low_ready"), sem("slot_done")
        psum_read = sem("psum_read")
        x_turned, x_copied_act, x_copied_dve = sem("x_turned"), sem("x_copied_act"), sem("x_copied_dve")
        row_squared, sq_ready, sq_added, col_summed = (
            sem("row_squared"), sem("sq_ready"), sem("sq_added"), sem("col_summed"))
        inv_ready, rstd_ready, spread_ready, rstd_bcast = (
            sem("inv_ready"), sem("rstd_ready"), sem("spread_ready"), sem("rstd_bcast"))
        xn_ready, norm_high = sem("xn_ready"), sem("norm_high")
        norm_low = [sem("norm_low_pool"), sem("norm_low_dve")]
        dve_seq, act_seq = sem("dve_seq"), sem("act_seq")
        roped, turned, turn_copied = sem("roped"), sem("turned"), sem("turn_copied")
        turn_out = [sem(f"turn_out{i}") for i in range(2)]
        k_kept = sem("k_kept")
        wi_turned, wrow_ready = sem("wi_turned"), sem("wrow_ready")
        idx_scored, idx_relu, idx_added, qis_copied = (
            sem("idx_scored"), sem("idx_relu"), sem("idx_added"), sem("qis_copied"))
        ik_turned, ik_copied, ik_new, is_scored, is_relu, is_summed = (
            sem("ik_turned"), sem("ik_copied"), sem("ik_new"), sem("is_scored"), sem("is_relu"), sem("is_summed"))
        ss_copied, bias_ready, mask_ready = sem("ss_copied"), sem("bias_ready"), sem("mask_ready")
        state_turned, u_turned, u_copied = sem("state_turned"), sem("u_turned"), sem("u_copied")
        d_ready = sem("d_ready")
        u_out = [sem(f"u_out{i}") for i in range(2)]
        df_high, df_low, pool_done, pool_high = sem("df_high"), sem("df_low"), sem("pool_done"), sem("pool_high")
        p_scored, p_max, p_exp, p_norm, p_turned, p_copied, p_out, p_high, p_low = (
            sem("p_scored"), sem("p_max"), sem("p_exp"), sem("p_norm"), sem("p_turned"), sem("p_copied"),
            sem("p_out"), sem("p_high"), sem("p_low"))
        kn_high, kn_low, vn_high, vn_low = sem("kn_high"), sem("kn_low"), sem("vn_high"), sem("vn_low")
        q_high, q_low, pick_ready = sem("q_high"), sem("q_low"), sem("pick_ready")
        kt_turned, kt_high, kt_low, k_scored = sem("kt_turned"), sem("kt_high"), sem("kt_low"), sem("k_scored")
        part_max, s_low_copied = sem("part_max"), sem("s_low_copied")
        s_copied, s_max, s_exp, s_inv = sem("s_copied"), sem("s_max"), sem("s_exp"), sem("s_inv")
        pt_turned, pt_high, pt_low = sem("pt_turned"), sem("pt_high"), sem("pt_low")
        ptn_high, ptn_low, low_out = sem("ptn_high"), sem("ptn_low"), sem("low_out")
        v_high, v_low, v_used, s_out = sem("v_high"), [sem(f"v_low{i}") for i in range(2)], sem("v_used"), sem("s_out")
        o_ready, o_turned, sy_high = sem("o_ready"), sem("o_turned"), sem("sy_high")
        out_read = sem("out_read")
        silu_done, hid_high, hid_low, down_done = (
            sem("silu_done"), sem("hid_high"), sem("hid_low"), sem("down_done"))
        y_turned, y_copied_act, y_copied_dve = sem("y_turned"), sem("y_copied_act"), sem("y_copied_dve")
        stored, state_out = sem("stored"), sem("state_out")

        def by_dve(f):
            return f % 4 == 0

        def low_of(m, f):
            return (norm_low[1], KT // 4 * m + f // 4 + 1) if by_dve(f) else (
                norm_low[0], 3 * KT // 4 * m + f - f // 4)

        rstd = PS[:, 6:8, :].rearrange("p a n -> p (a n)")[:, 0:NT]

        class Chain:

            def __init__(self, eng, s):
                self.eng, self.s, self.n, self.more = eng, s, 0, 0

            def __call__(self, ins):
                self.n += 1
                ins.then_inc(self.s, 1)
                self.eng.wait_ge(self.s, self.n + self.more)

        def in_col(s):
            if s == S_KI:
                return C_KI
            if s == S_WI:
                return C_WI_TILE
            for first, col in ((S_UP, C_UP), (S_Q, C_Q), (S_V, C_V), (S_K, C_K), (S_QI, C_QI)):
                if s >= first:
                    return col + (s - first) * P

        rows_of = lambda w: w.rearrange("(k p) n -> p k n", p=P)
        win_v, wout_v = rows_of(w_in[0]), rows_of(w_out[0])
        wgate_v, wup_v, wdown_v = rows_of(w_gate[0]), rows_of(w_up[0]), rows_of(w_down[0])
        wpool_v = w_pool[0].rearrange("g (k p) m -> p (g k) m", p=P)
        x_rows = [x_prompt[0, t * P:(t + 1) * P, :] for t in range(4)] + [x_sample.rearrange("b t d -> (b t) d")]
        ROWS = [P] * 4 + [NS]

        def row_outputs(s):
            if s == S_KI:
                return (idx_k_prompt[0, 0].rearrange("(t p) d -> p t d", p=P),
                        idx_k_sample[0].rearrange("b t d -> (b t) d"))
            po, so, h = (k_prompt, k_sample, s - S_K) if s < S_V else (v_prompt, v_sample, s - S_V)
            return (po[0, 0, :, h, :].rearrange("(t p) d -> p t d", p=P),
                    so[0, :, :, h, :].rearrange("b t d -> (b t) d"))

        def store_last_rows(eng, f):
            eng.wait_ge(act_seq, 2 * NH + 1 + f + 1)
            eng.wait_ge(u_copied, f + 1)
            eng.dma_start(pool_prompt[0, 0, :, f * P:(f + 1) * P], upt[:, f % 2, :]).then_inc(u_out[f % 2], 16)
            for b in range(DB):
                eng.dma_start(pool_sample[0, b, STATE - DT:STATE, f * P:(f + 1) * P],
                              ust[b * DT:(b + 1) * DT, f % 2, :]).then_inc(u_out[f % 2], 16)

        TURNS = [S_KI] + list(range(S_K, S_Q))
        block = ctx.enter_context(nc.Block())

        @block.sync
        def _(sp):
            sp.dma_start(cst[:, 0:K_COS], const[:, 0:K_COS]).then_inc(ident_in, 16)
            for t in range(5):
                sp.dma_start(xin[0:ROWS[t], t, :], x_rows[t]).then_inc(x_in[t], 16)
            sp.dma_start(cst[:, K_COS:], const[:, K_COS:]).then_inc(const_in, 16)
            for n, g in enumerate((g_mix[0], g_ffn[0], g_final)):
                sp.dma_start(grow[n * KT:(n + 1) * KT, :], g.rearrange("(k p) -> k p", p=P)).then_inc(gain_in, 16)
            sp.dma_start(grow[3 * KT:3 * KT + NPOOL, :], s_pool[0].rearrange("(k p) -> k p", p=P)).then_inc(gain_in, 16)
            sp.dma_start(pages[:, :], page_table.rearrange("(o b) n -> o (b n)", o=1)).then_inc(pages_in, 16)
            sp.dma_start(pool_sample[0, :, 0:STATE - DT, :], state_pool[0, :, DT:STATE, :]).then_inc(state_out, 16)

            def slot(s, parity, src, first=False):
                if not first:
                    sp.wait_ge(low_ready, s - 1)
                a, b = src.shape[1:]
                sp.dma_start(raw[:, parity, :].rearrange("p (a b) -> p a b", a=a), src).then_inc(raw_in[parity], 16)

            def columns(w, c):
                return w[:, :, c:c + P] if isinstance(c, int) else w[:, :, bass.ds(c, P)]

            for s in (S_KI, S_WI):
                slot(s, s % 2, columns(win_v, in_col(s)), first=True)
            sp.wait_ge(x_copied_act, 10)
            sp.wait_ge(x_copied_dve, 10)
            sp.dma_start(x_keep, XT[:, :, :].rearrange("p k n -> p (k n)")).then_inc(x_kept, 16)
            with sp.Fori(0, IH // 2) as i:
                for j in range(2):
                    slot(2 * i + (S_QI + j), j, columns(win_v, i * (2 * P) + (C_QI + j * P)))
            sp.wait_ge(x_kept, 16)
            sp.wait_ge(pages_in, 16)
            for f in (KT - 4, KT - 1):
                sp.wait_ge(*low_of(0, f))
            for b in range(DB):
                if b == 1:
                    for s in (S_K, S_K + 1):
                        slot(s, s % 2, columns(win_v, in_col(s)))
                for c in range(2):
                    if b:
                        sp.wait_ge(ik_turned, 4 * (b - 1) + c + 1)
                    for j in range(4):
                        pg = sp.value_load(pages[0:1, b * NPG + 4 * c + j:b * NPG + 4 * c + j + 1], min_val=0,
                                           max_val=n_phys - 1)
                        sp.dma_start(ikraw[:, c, j * HD:(j + 1) * HD],
                                     cache_idx_k[0, bass.ds(pg, 1), :, :].rearrange("o p d -> p (o d)")
                                     ).then_inc(ik_in[c], 16)
            for first, col in ((S_K + 2, C_K + 2 * P), (S_Q, C_Q), (S_UP, C_UP)):
                n = {S_K + 2: S_Q - S_K - 2, S_Q: NH, S_UP: NPOOL}[first]
                if first == S_UP:
                    sp.wait_ge(is_summed, 5 * DB)
                    sp.dma_start(staterow[:, :], state_pool[0].rearrange("b t c -> (b t) c")).then_inc(state_in, 16)
                with sp.Fori(0, n // 2) as i:
                    for j in range(2):
                        slot(2 * i + (first + j), j, columns(win_v, i * (2 * P) + (col + j * P)))

            sp.wait_ge(slot_done, S_POOL)
            for t in range(2):
                sp.wait_ge(turn_out[t], 32 * len(TURNS[t::2]))
            sp.dma_start(vprompt[:, :, :], v_prompt[0, 0].rearrange("(t p) h d -> p t (h d)", p=P)
                         ).then_inc(vprompt_in, 16)

            for t in range(2):
                sp.wait_ge(turn_out[t], 32 * len(TURNS[t::2]))
            sp.wait_ge(d_ready, NPOOL)
            sp.dma_start(d_keep[:, (NPOOL - 1) * NT:], rtmp[:, :]).then_inc(d_kept, 16)
            for f in (NPOOL - 2, NPOOL - 1):
                store_last_rows(sp, f)
            sp.dma_start(vraw[:, :], v_sample[0].rearrange("b t h d -> (b t) (h d)")).then_inc(vnew_in, 16)

            def page(b, n, ring, cache, arrived):
                pg = sp.value_load(pages[0:1, bass.ds(b * NPG + n, 1)], min_val=0, max_val=n_phys - 1)
                sp.dma_start(ring[:, n % 4, :], cache[0, bass.ds(pg, 1)].rearrange("o p h d -> p (o h d)")
                             ).then_inc(arrived[n % 4], 16)

            def k_page(b, n):
                if not (isinstance(b, int) and b == 0 and n < 4):
                    sp.wait_ge(kt_turned, b * NPG + (n - 3))
                page(b, n, kpage, cache_k, k_in)

            def v_page(b, n):
                if not (isinstance(b, int) and b == 1 and n < 4):
                    sp.wait_ge(v_low[n % 2], b * (NPG // 2) + (n // 2 - 1 - NPG // 2))
                page(b - 1, n, vpage, cache_v, v_in)

            def load_pages(b, keys, values, ahead):
                for c in range(NCH):
                    for n in (2 * c + 2, 2 * c + 3):
                        if keys and (n < NPG or ahead):
                            k_page(b, n)
                    for n in (2 * c, 2 * c + 1):
                        if values and n >= 0:
                            v_page(b, n)

            k_page(0, 0)
            k_page(0, 1)
            load_pages(0, True, False, True)
            load_pages(1, True, True, True)
            with sp.Fori(2, DB - 1) as b:
                load_pages(b, True, True, True)
            load_pages(DB - 1, True, True, False)
            for n in range(NPG):
                v_page(DB, n)
                if n == 3:
                    sp.wait_ge(kt_turned, DB * NPG)
                    slot(S_POOL, 0, wpool_v)
                if n in (5, 7):
                    sp.wait_ge(k_scored, DB * (NCH + 1))
                    sp.wait_ge(d_kept, 16 * NPOOL)
                    f = NPOOL // 2 * (n // 7)
                    sp.dma_start(dback[:, f:f + NPOOL // 2, :].rearrange("p f n -> p (f n)"),
                                 d_keep[:, f * NT:(f + NPOOL // 2) * NT]).then_inc(d_back, 16)
                if n == 9:
                    slot(S_OUT, 1, columns(wout_v, 0))

            slot(S_OUT + 1, 0, columns(wout_v, P))
            sp.wait_ge(slot_done, S_OUT)
            for o in range(4):
                sp.dma_start(XT[:, 4 * o:4 * o + 4, :].rearrange("p k n -> p (k n)"),
                             x_keep[:, 4 * o * NT:(4 * o + 4) * NT]).then_inc(x_back[o], 16)
                if o < 3:
                    slot(S_OUT + 2 + o, (S_OUT + 2 + o) % 2, columns(wout_v, (2 + o) * P))
            with sp.Fori(0, (KT - 6) // 2) as i:
                for j in range(2):
                    slot(2 * i + (S_OUT + 5 + j), j, columns(wout_v, i * (2 * P) + (5 + j) * P))
            slot(S_FF - 1, (S_FF - 1) % 2, columns(wout_v, (KT - 1) * P))
            with sp.Fori(0, CHUNKS) as i:
                for j in range(2 * FT):
                    w = wup_v if j % 2 else wgate_v
                    slot(PER_CHUNK * i + (S_FF + j), (S_FF + j) % 2, columns(w, i * (FT * P) + (j // 2) * P))
                for j in range(FT):
                    slot(PER_CHUNK * i + (S_FF + 2 * FT + j), (S_FF + j) % 2,
                         wdown_v[:, bass.ds(i * FT, FT), j * 512:(j + 1) * 512])

            for q in range(4):
                sp.wait_ge(y_copied_act, 4 * q + 4)
                sp.wait_ge(y_copied_dve, 4 * q + 4)
                cols = slice(q * 512, (q + 1) * 512)
                sp.dma_start(y_prompt[0].rearrange("(t p) d -> p t d", p=P)[:, :, cols], yrow[:, 0:4, cols]
                             ).then_inc(stored, 16)
                sp.dma_start(y_sample.rearrange("b t d -> (b t) d")[:, cols], yrow[0:NS, 4, cols]
                             ).then_inc(stored, 16)
            sp.wait_ge(stored, 128)
            sp.wait_ge(state_out, 16)

        @block.gpsimd
        def _(pool):
            def low(s, parity):
                pool.wait_ge(high_ready, s + 1)
                nc.gpsimd.tensor_tensor(wl[:, parity, :], raw[:, parity, :], wh[:, parity, :].bitcast(F32),
                                        ALU.subtract).then_inc(low_ready, 1)

            def norm_lows(m):
                for f in range(KT):
                    if not by_dve(f):
                        pool.wait_ge(norm_high, KT * m + f + 1)
                        nc.gpsimd.tensor_tensor(HL[:, f, :], xn[:, f % 4, :], HH[:, f, :].bitcast(F32), ALU.subtract
                                                ).then_inc(norm_low[0], 1)

            low(0, 0)
            norm_lows(0)
            low(1, 1)
            with pool.Fori(0, IH // 2) as i:
                for j in range(2):
                    low(2 * i + (S_QI + j), j)
            pool.wait_ge(pages_in, 16)
            pool.wait_ge(x_kept, 16)
            for f in (KT - 4, KT - 1):
                pool.wait_ge(*low_of(0, f))
            for b in range(DB):
                if b == 1:
                    low(S_K, 0)
                    low(S_K + 1, 1)
                for c in range(2, 4):
                    if b:
                        pool.wait_ge(ik_turned, 4 * (b - 1) + c + 1)
                    for j in range(4):
                        pg = pool.value_load(pages[0:1, b * NPG + 4 * c + j:b * NPG + 4 * c + j + 1], min_val=0,
                                             max_val=n_phys - 1)
                        pool.dma_start(ikraw[:, c, j * HD:(j + 1) * HD],
                                       cache_idx_k[0, bass.ds(pg, 1), :, :].rearrange("o p d -> p (o d)")
                                       ).then_inc(ik_in[c], 16)
            with pool.Fori(1, (S_POOL - S_K) // 2) as i:
                for j in range(2):
                    low(2 * i + (S_K + j), j)

            def v_lows(b):
                for n in range(0, NPG, 2):
                    pool.wait_ge(v_high, b * NPG + (n + 1 - NPG))
                    high, low = value_halves(n, is_number(b, DB))
                    nc.gpsimd.tensor_tensor(low, vpage[:, n % 4, :], high.bitcast(F32), ALU.subtract
                                            ).then_inc(v_low[0], 1)

            with pool.Fori(1, DB) as b:
                v_lows(b)
            v_lows(DB)

            pool.wait_ge(high_ready, S_POOL + 1)
            pool.wait_ge(pt_turned, 3 * DB)
            nc.gpsimd.tensor_tensor(pool_wl[:, :], raw[:, 0, :], wh[:, 0, :].bitcast(F32),
                                    ALU.subtract).then_inc(low_ready, 1)
            pool.wait_ge(s_out, DB)
            with pool.Fori(0, (S_FF + 2 - S_OUT) // 2) as i:
                for j in range(2):
                    low(2 * i + (S_OUT + j), (S_OUT + j) % 2)
            norm_lows(1)
            with pool.Fori(0, (N_SLOTS - S_FF - 2) // 2) as i:
                for j in range(2):
                    low(2 * i + (S_FF + 2 + j), (S_FF + j) % 2)

        @block.tensor
        def _(pe):
            def mm(s, g, parity, gate=None, cols=(0, P), rows=P, banks=None):
                pe.wait_ge(low_ready, s + 1)
                if not (isinstance(g, int) and g < 2):
                    pe.wait_ge(psum_read, g - 1)
                out = pair(parity if banks is None else banks, rows)
                for k in range(KT):
                    if gate is not None:
                        gate(k)
                    a, b = k * P + cols[0], k * P + cols[1]
                    for w, h in ((wh, HH), (wh, HL), (wl, HH)):
                        for n in range(2):
                            last = nc.tensor.matmul(out[:, n, :], w[:, parity, a:b],
                                                    h[:, k, n * HALF:(n + 1) * HALF],
                                                    start=(k == 0 and w is wh and h is HH),
                                                    stop=(k == KT - 1 and w is wl))
                last.then_inc(slot_done, 1)

            pe.wait_ge(ident_in, 16)
            n = 0
            for t in range(5):
                pe.wait_ge(x_in[t], 16)
                for f in range(0, KT, 4):
                    if n >= 4:
                        pe.wait_ge(x_copied_dve if n % 2 else x_copied_act, (n - 4) // 2 + 1)
                    for j in range(4):
                        last = nc.tensor.transpose(PS[:, 4 + n % 4, j * P:j * P + ROWS[t]],
                                                   xin[0:ROWS[t], t, (f + j) * P:(f + j + 1) * P],
                                                   ident[0:ROWS[t], 0:ROWS[t]])
                    last.then_inc(x_turned, 1)
                    n += 1

            def column_sums(m):
                pe.wait_ge(sq_added, KT * m)
                for t in range(5):
                    last = nc.tensor.matmul(PS[0:ROWS[t], 4, t:t + 1], ss[:, t * P:t * P + ROWS[t]], ones[:, 0:1],
                                            start=True, stop=True)
                last.then_inc(col_summed, 1)

            def spread_rstd(m):
                for t in range(5):
                    pe.wait_ge(spread_ready, 5 * m + t + 1)
                    last = nc.tensor.matmul(rstd[:, t * P:t * P + ROWS[t]], ones[0:ROWS[t], :],
                                            spread[0:ROWS[t], t, 0:ROWS[t]], start=True, stop=True)
                last.then_inc(rstd_bcast, 1)

            pe.wait_ge(gain_in, 64)
            pe.wait_ge(row_squared, 5)
            nc.tensor.transpose(PS[:, 3, 0:3 * KT + NPOOL], grow[:, :], ident[0:3 * KT + NPOOL, 0:3 * KT + NPOOL]
                                ).then_inc(gains_turned, 1)
            pe.wait_ge(x_copied_act, 10)
            pe.wait_ge(x_copied_dve, 10)
            spread_rstd(0)

            def turn(t, src):
                b = 4 + 2 * (t % 2)
                if t >= 2:
                    pe.wait_ge(turn_copied, t - 1)
                for k in range(5):
                    last = nc.tensor.transpose(PS[0:ROWS[k], b + k // 4, (k % 4) * P:(k % 4 + 1) * P],
                                               src[:, k * P:k * P + ROWS[k]], ident)
                last.then_inc(turned, 1)

            def idx_prompt(h, j, first):
                for n, blk in enumerate(BLOCKS):
                    if first:
                        pe.wait_ge(turn_copied, 1)
                        pe.wait_ge(roped, 2)
                    else:
                        pe.wait_ge(idx_relu, 3 * h + (n - 2))
                    if n == 0 and not first:
                        pe.wait_ge(roped, h + 2)
                    last = nc.tensor.matmul(PS[:, 4 + n, 0:(blk + 1) * P], T2[:, j, 16 + blk * P:16 + (blk + 1) * P],
                                            kiT[:, 0:(blk + 1) * P], start=True, stop=True)
                    last.then_inc(idx_scored, 1)

            mm(S_KI, 0, 0, gate=lambda k: pe.wait_ge(*low_of(0, k)))
            mm(S_WI, 1, 1, cols=(P - IH, P), rows=IH)
            pe.wait_ge(roped, 1)
            turn(0, kiT[:, :])
            mm(S_QI, 2, 0)
            pe.wait_ge(psum_read, S_WI + 1)
            for blk in BLOCKS:
                nc.tensor.transpose(PS[:, 7, blk * IH:(blk + 1) * IH], wiT[:, blk * P:(blk + 1) * P], ident[0:IH, 0:IH])
            pe.wait_ge(const_in, 16)
            nc.tensor.matmul(PS[:, 7, 128:128 + NS], cst[0:IH, K_REP:K_REP + P], wiT[:, SEQ:NT],
                             start=True, stop=True).then_inc(wi_turned, 1)
            mm(S_QI + 1, 3, 1)
            idx_prompt(0, 0, True)
            with pe.Fori(1, IH // 2) as i:
                mm(2 * i + S_QI, 2 * i + S_QI, 0)
                idx_prompt(2 * i - 1, 1, False)
                mm(2 * i + (S_QI + 1), 2 * i + (S_QI + 1), 1)
                idx_prompt(2 * i, 0, False)
            idx_prompt(IH - 1, 1, False)

            CH = [(c * 512, 512) for c in range(4)] + [(PAST, DT)]

            def work(n):
                return 5 + n % 3

            def wait_work(n):
                m = n - 3
                if m < 0:
                    pe.wait_ge(idx_relu, 3 * IH)
                    pe.wait_ge(wrow_ready, 1)
                    return
                b, j = divmod(m, 9)
                if j < 4:
                    pe.wait_ge(ik_copied, 4 * b + j + 1)
                else:
                    pe.wait_ge(is_relu, 5 * b + j - 3)

            for b in range(DB):
                for c in range(4):
                    n = 9 * b + c
                    wait_work(n)
                    pe.wait_ge(ik_in[c], 64 * (b + 1))
                    for j in range(4):
                        last = nc.tensor.transpose(PS[:, work(n), j * P:(j + 1) * P],
                                                   ikraw[:, c, j * HD:(j + 1) * HD], ident)
                    last.then_inc(ik_turned, 1)

                def add_heads(c):
                    pe.wait_ge(is_relu, 5 * b + c + 1)
                    if b == 0 and c == 0:
                        pe.wait_ge(psum_read, S_K)
                    o, w = CH[c]
                    nc.tensor.matmul(PS[0:NS, c, 0:w], wrow[:, b * NS:(b + 1) * NS],
                                     irelu[:, (5 * b + c) % 3, 0:w], start=(b == 0), stop=(b == DB - 1)
                                     ).then_inc(is_summed, 1)

                for c, (o, w) in enumerate(CH):
                    n = 9 * b + 4 + c
                    wait_work(n)
                    if c < 4:
                        pe.wait_ge(ik_copied, 4 * b + c + 1)
                    else:
                        pe.wait_ge(ik_new, b + 1)
                    if b == 0 and c == 0:
                        pe.wait_ge(qis_copied, IH)
                    nc.tensor.matmul(PS[:, work(n), 0:w], qis[:, b, :], ikT[:, b % 2, o:o + w],
                                     start=True, stop=True).then_inc(is_scored, 1)
                    if c:
                        add_heads(c - 1)
                add_heads(4)

            pe.wait_ge(ss_copied, 1)
            mm(S_K, S_K, 0)
            mm(S_K + 1, S_K + 1, 1)

            def turn_head(s, j, t, rotated=True):
                if rotated:
                    pe.wait_ge(roped, s)
                else:
                    pe.wait_ge(psum_read, s + 1)
                b = 4 + 2 * ((j + 1) % 2)
                pe.wait_ge(turn_copied, t - 1)
                for k in range(5):
                    last = nc.tensor.transpose(PS[0:ROWS[k], b + k // 4, (k % 4) * P:(k % 4 + 1) * P],
                                               T2[:, j, 16 + k * P:16 + k * P + ROWS[k]], ident)
                last.then_inc(turned, 1)

            turn_head(S_K, 0, 1)
            with pe.Fori(1, NH // 2) as i:
                mm(2 * i + S_K, 2 * i + S_K, 0)
                turn_head(2 * i + (S_K - 1), 1, 2 * i)
                mm(2 * i + (S_K + 1), 2 * i + (S_K + 1), 1)
                turn_head(2 * i + S_K, 0, 2 * i + 1)
            mm(S_V, S_V, 0)
            turn_head(S_V - 1, 1, NH)
            mm(S_V + 1, S_V + 1, 1)
            turn_head(S_V, 0, NH + 1, False)
            with pe.Fori(NH // 2 + 1, NH) as i:
                mm(2 * i + S_K, 2 * i + S_K, 0)
                turn_head(2 * i + (S_K - 1), 1, 2 * i, False)
                mm(2 * i + (S_K + 1), 2 * i + (S_K + 1), 1)
                turn_head(2 * i + S_K, 0, 2 * i + 1, False)
            mm(S_Q, S_Q, 0)
            turn_head(S_Q - 1, 1, 2 * NH, False)
            mm(S_Q + 1, S_Q + 1, 1)
            with pe.Fori(1, NH // 2) as i:
                mm(2 * i + S_Q, 2 * i + S_Q, 0)
                mm(2 * i + (S_Q + 1), 2 * i + (S_Q + 1), 1)

            pe.wait_ge(state_in, 16)
            pe.wait_ge(turn_copied, 2 * NH + 1)

            for f in range(NPOOL):
                last = nc.tensor.transpose(PS[:, 6 + f // 4, (f % 4) * DB * STATE:(f % 4 + 1) * DB * STATE],
                                           staterow[:, f * P:(f + 1) * P], ident[0:DB * STATE, 0:DB * STATE])
            last.then_inc(state_turned, 1)

            def up_turn(f, j, free=None):
                pe.wait_ge(psum_read, f + (S_UP + 1))
                if free is not None:
                    pe.wait_ge(u_copied, free)
                nc.tensor.transpose(PS[0:STATE, 4 + j, 0:P], T2[:, j, 16 + SEQ - STATE:16 + SEQ], ident)
                nc.tensor.transpose(PS[0:NS, 4 + j, P:2 * P], T2[:, j, 16 + SEQ:16 + NT], ident).then_inc(u_turned, 1)

            mm(S_UP, S_UP, 0)
            mm(S_UP + 1, S_UP + 1, 1)
            up_turn(0, 0)
            with pe.Fori(1, NPOOL // 2) as i:
                mm(2 * i + S_UP, 2 * i + S_UP, 0)
                up_turn(2 * i - 1, 1, 2 * i - 1)
                mm(2 * i + (S_UP + 1), 2 * i + (S_UP + 1), 1)
                up_turn(2 * i, 0, 2 * i - 1)
            up_turn(NPOOL - 1, 1, NPOOL - 2)

            pe.wait_ge(psum_read, S_POOL)

            UNITS = [(h, q) for h in range(NH) for q in range(4)]
            U = len(UNITS)
            for n in range(U + 3):
                if n < U:
                    h, q = UNITS[n]
                    if n == 0:
                        pe.wait_ge(u_copied, NPOOL)
                        pe.wait_ge(k_kept, NH)
                        pe.wait_ge(roped, S_UP - 1 - NH)
                    if n >= 3:
                        pe.wait_ge(p_max, n - 2)
                    nc.tensor.matmul(PS[:, n % 3, 0:(q + 1) * P], qkT[:, h, q * P:(q + 1) * P],
                                     qkT[:, NH + h, 0:(q + 1) * P], start=True, stop=True).then_inc(p_scored, 1)
                if 2 <= n < U + 2:
                    u = n - 2
                    h, q = UNITS[u]
                    pe.wait_ge(p_norm, u + 1)
                    if u >= 3:
                        pe.wait_ge(p_copied, u - 2)
                    for k in range(q + 1):
                        last = nc.tensor.transpose(PS[:, 3 + u % 3, k * P:(k + 1) * P], px[:, u % 3, k * P:(k + 1) * P],
                                                   ident)
                    last.then_inc(p_turned, 1)
                if n >= 3:
                    u = n - 3
                    h, q = UNITS[u]
                    pe.wait_ge(p_copied, u + 1)
                    if u == 0:
                        pe.wait_ge(vprompt_in, 16)
                    if u >= 2:
                        pe.wait_ge(p_low, u - 1)
                    for k in range(q + 1):
                        last = nc.tensor.matmul(PS[:, 6 + u % 2, 0:P], vprompt[:, k, h * HD:(h + 1) * HD],
                                                pxt[:, u % 3, k * P:(k + 1) * P], start=(k == 0), stop=(k == q))
                    last.then_inc(p_out, 1)

            pe.wait_ge(p_max, U)
            pe.wait_ge(p_copied, U)

            def k_turn(b, n):
                j = n % 2
                pe.wait_ge(k_in[n % 4], b * (4 * NPG) + 16 * (n // 4 + 1))
                if not (is_number(b, 0) and n < 2):
                    pe.wait_ge(kt_low, b * NPG + (n - 1))
                for h in range(NH):
                    last = nc.tensor.transpose(PS[:, 2 * j + h // 4, (h % 4) * P:(h % 4 + 1) * P],
                                               kpage[:, n % 4, h * HD:(h + 1) * HD], ident)
                last.then_inc(kt_turned, 1)

            def k_score(b, c):
                if c == 0:
                    pe.wait_ge(q_low, b + 1)
                    pe.wait_ge(pick_ready, b + 1)
                    pe.wait_ge(mask_ready, 1)
                if c < NCH:
                    pe.wait_ge(kt_low, b * NPG + (2 * c + 2))
                    w, mask = CHUNK, maskS[:, c * CHUNK:(c + 1) * CHUNK]
                    kh, kl = kth[:, c % 2], ktl[:, c % 2]
                else:
                    pe.wait_ge(kn_low, 1)
                    w, mask, kh, kl = NS, maskN[:, :], knh, knl
                if not (is_number(b, 0) and c == 0):
                    pe.wait_ge(s_copied, b * (NCH + 1) + c)
                for h in range(NH):
                    if h == NH - 1:
                        nc.tensor.matmul(PS[0:NS, 4, 0:w], pick[:, :], mask, start=False, stop=False)
                        nc.tensor.matmul(PS[0:NS, 4, 0:w], qhl[:, h * P:h * P + NS], kl[:, h, :],
                                         start=False, stop=False)
                    last = nc.tensor.matmul(PS[:, 4, 0:w], qhl[:, h * P:(h + 1) * P], kh[:, h, :],
                                            start=(h == 0), stop=(h == NH - 1))
                    if h < NH - 1:
                        nc.tensor.matmul(PS[0:NS, 4, 0:w], qhl[:, h * P:h * P + NS], kl[:, h, :],
                                         start=False, stop=False)
                last.then_inc(k_scored, 1)

            def turn_rows(waits, out, rows):
                if waits:
                    return nc.tensor.matmul(out, rows, ident[0:NS, 0:NS], start=True, stop=True)
                return nc.tensor.transpose(out, rows, ident[0:NS, 0:NS])

            def p_turn(b, g):
                if g == 0:
                    pe.wait_ge(s_exp, b)
                    pe.wait_ge(out_read, b)
                else:
                    pe.wait_ge(pt_low, b * 3 + (g - 3))
                n0, n1 = GROUPS[g]
                for n in range(n0, n1):
                    w = PAGE if n < NPG else NS
                    last = turn_rows(n == n0, PS[0:w, 5, (n - n0) * NS:(n - n0 + 1) * NS],
                                     prob[:, n * PAGE:n * PAGE + w])
                last.then_inc(pt_turned, 1)

            def pv(b, n):
                for g in range(3):
                    if n == GROUPS[g][0]:
                        pe.wait_ge(pt_low, b * 3 + (g - 2))
                if n == 0:
                    pe.wait_ge(out_read, b)
                if n == GROUPS[2][0]:
                    pe.wait_ge(ptn_low, b)
                if n < NPG:
                    pe.wait_ge(v_low[n % 2], b * (NPG // 2) + (n // 2 + 1 - NPG // 2))
                    vh, vl = value_halves(n, is_number(b, DB))
                    p = pt[:, n, :]
                else:
                    pe.wait_ge(vn_low, 1)
                    p, vh, vl = ptn[:, :], vnh, vnl
                for a in range(2):
                    cols = slice(a * 512, (a + 1) * 512)
                    if n == NPG:
                        nc.tensor.matmul(PS[0:NS, 6 + a, :], p[:, 0:NS], vl[:, cols], start=False, stop=False)
                    last = nc.tensor.matmul(PS[:, 6 + a, :], p, vh[:, cols], start=(n == 0), stop=(n == NPG))
                    if n < NPG:
                        last = nc.tensor.matmul(PS[0:NS, 6 + a, :], p[:, 0:NS], vl[:, cols], start=False, stop=False)
                last.then_inc(v_used if n < NPG else s_out, 1)

            def o_turn(b):
                pe.wait_ge(pt_low, b * 3)
                pe.wait_ge(ptn_low, b)
                pe.wait_ge(o_ready, b)
                for h in range(NH):
                    last = turn_rows(h == 0, PS[:, 5, h * NS:(h + 1) * NS], orow[:, h * HD:(h + 1) * HD])
                last.then_inc(o_turned, 1)

            def sequence(b, keys, values, ahead):
                for c in range(NCH + 1):
                    if keys and 0 < c < NCH:
                        k_turn(b, 2 * c)
                        k_turn(b, 2 * c + 1)
                    if values and c == 2:
                        p_turn(b, 1)
                    if c and keys:
                        k_score(b, c - 1)
                    if values and c == 1:
                        p_turn(b, 0)
                    if values and c >= 2:
                        pv(b, 2 * c - 4)
                        pv(b, 2 * c - 3)
                    if values and c == 3:
                        p_turn(b, 2)
                if ahead:
                    k_turn(b, NPG)
                if values:
                    pv(b, NPG - 2)
                    pv(b, NPG - 1)
                    pv(b, NPG)
                if ahead:
                    k_turn(b, NPG + 1)
                if keys:
                    k_score(b, NCH)
                if values:
                    o_turn(b)

            k_turn(0, 0)
            k_turn(0, 1)
            sequence(0, True, False, True)
            with pe.Fori(1, DB - 1) as b:
                sequence(b, True, True, True)
            sequence(DB - 1, True, True, False)
            sequence(DB, False, True, False)

            pe.wait_ge(low_ready, S_OUT)
            pe.wait_ge(o_ready, DB)
            for g in range(4):
                for m in range(2):
                    o = 2 * g + m
                    if o >= 2:
                        pe.wait_ge(psum_read, G_POOL + o - 1)
                    if o == 0:
                        pe.wait_ge(df_low, NPOOL)
                    for k in range(2):
                        a = (2 * g + k) * 256 + m * P
                        for w, d in ((wh[:, 0], DH), (wh[:, 0], DL), (pool_wl, DH)):
                            for n in range(2):
                                last = nc.tensor.matmul(pair(o)[:, n, :], w[:, a:a + P],
                                                        d[:, 2 * g + k, n * HALF:(n + 1) * HALF],
                                                        start=(k == 0 and w is not pool_wl and d is DH),
                                                        stop=(k == 1 and w is pool_wl))
                    if o == NPOOL - 1:
                        last.then_inc(slot_done, 1)
                    else:
                        last.then_inc(pool_done, 1)

            pe.wait_ge(psum_read, G_OUT)
            with pe.Fori(0, KT // 2) as i:
                mm(2 * i + S_OUT, 2 * i + G_OUT, 1, banks=0)
                mm(2 * i + (S_OUT + 1), 2 * i + (G_OUT + 1), 0, banks=1)
            pe.wait_ge(psum_read, G_FF)
            column_sums(1)
            spread_rstd(1)

            def feed_forward(i, first=False):
                read0 = READ_CHUNK * i + G_FF
                for j in range(2 * FT):
                    s = PER_CHUNK * i + (S_FF + j)
                    parity = (S_FF + j) % 2
                    pe.wait_ge(low_ready, s + 1)
                    if j < 2:
                        pe.wait_ge(psum_read, read0 + (j - 1))
                    elif j % 2 == 0:
                        pe.wait_ge(silu_done, FT * i + j // 2)
                    else:
                        pe.wait_ge(psum_read, read0 + (j - 1) // 2)
                    for k in range(KT):
                        if first and j == 0:
                            pe.wait_ge(*low_of(1, k))
                        for w, h in ((wh, HH), (wh, HL), (wl, HH)):
                            for n in range(2):
                                last = nc.tensor.matmul(pair(j)[:, n, :], w[:, parity, k * P:(k + 1) * P],
                                                        h[:, k, n * HALF:(n + 1) * HALF],
                                                        start=(k == 0 and w is wh and h is HH),
                                                        stop=(k == KT - 1 and w is wl))
                    last.then_inc(slot_done, 1)
                for j in range(FT):
                    s = PER_CHUNK * i + (S_FF + 2 * FT + j)
                    parity = (S_FF + j) % 2
                    pe.wait_ge(low_ready, s + 1)
                    for m in range(4):
                        o = 4 * j + m
                        if o == 0:
                            pe.wait_ge(silu_done, FT * i + FT)
                        else:
                            pe.wait_ge(psum_read, read0 + (FT + o - 1))
                        for k in range(FT):
                            if o == 0:
                                pe.wait_ge(hid_low, FT * i + (k + 1))
                            a = k * 512 + m * P
                            for w, h in ((wh, GH), (wh, GL), (wl, GH)):
                                for n in range(2):
                                    last = nc.tensor.matmul(pair(o)[:, n, :], w[:, parity, a:a + P],
                                                            h[:, k, n * HALF:(n + 1) * HALF],
                                                            start=(k == 0 and w is wh and h is GH),
                                                            stop=(k == FT - 1 and w is wl))
                        if m == 3:
                            last.then_inc(slot_done, 1)
                        else:
                            last.then_inc(down_done, 1)

            feed_forward(0, True)
            with pe.Fori(1, CHUNKS) as i:
                feed_forward(i)
            column_sums(2)
            spread_rstd(2)

            for f in range(KT):
                pe.wait_ge(xn_ready, 2 * KT + f + 1)
                if f >= 2:
                    pe.wait_ge(y_copied_act, f - 1)
                    pe.wait_ge(y_copied_dve, f - 1)
                for k in range(5):
                    last = nc.tensor.transpose(PS[0:ROWS[k], 2 * (f % 2) + k // 4, (k % 4) * P:(k % 4 + 1) * P],
                                               xn[:, f % 4, k * P:k * P + ROWS[k]], ident)
                last.then_inc(y_turned, 1)

        @block.scalar
        def _(act):
            def high(s, parity, wait=True):
                act.wait_ge(raw_in[parity], 16 * (s // 2 + 1))
                if wait:
                    act.wait_ge(slot_done, s - 1)
                nc.scalar.activation(wh[:, parity, :], raw[:, parity, :], ACT.Copy).then_inc(high_ready, 1)

            act.wait_ge(dve_seq, 2)
            for n in range(0, 20, 2):
                t, f = n // 4, 4 * (n % 4)
                if n % 4 == 0:
                    act.wait_ge(x_in[t], 16)
                    if t:
                        act.wait_ge(row_squared, t)
                    nc.scalar.activation(PS[0:ROWS[t], 0:4, :].rearrange("p a n -> p (a n)"), xin[0:ROWS[t], t, :],
                                         ACT.Square, accum_out=stats[0:ROWS[t], t:t + 1]).then_inc(row_squared, 1)
                act.wait_ge(x_turned, n + 1)
                nc.scalar.activation(XT[:, f:f + 4, t * P:t * P + ROWS[t]],
                                     PS[:, 4 + n % 4, :].rearrange("p (j t) -> p j t", j=4)[:, :, 0:ROWS[t]],
                                     ACT.Copy).then_inc(x_copied_act, 1)

            def square(m, f):
                if f >= 2:
                    act.wait_ge(sq_added, KT * (m - 1) + f - 1)
                nc.scalar.activation(sq[:, f % 2, :], XT[:, f, :], ACT.Square).then_inc(sq_ready, 1)

            def root(m):
                act.wait_ge(inv_ready, m + 1)
                nc.scalar.activation(stats[:, 0:5], stats[:, 0:5], ACT.Sqrt).then_inc(rstd_ready, 1)

            def norm_highs(m):
                for f in range(KT):
                    act.wait_ge(xn_ready, KT * m + f + 1)
                    nc.scalar.activation(HH[:, f, :], xn[:, f % 4, :], ACT.Copy).then_inc(norm_high, 1)

            root(0)
            high(0, 0, wait=False)
            high(1, 1, wait=False)
            act.wait_ge(x_copied_act, 10)
            act.wait_ge(x_copied_dve, 10)
            norm_highs(0)

            def rows_out(t):
                b, j = 4 + 2 * (t % 2), t % 2
                act.wait_ge(turned, t + 1)
                if t >= 2:
                    act.wait_ge(turn_out[j], 32 * (t // 2))
                nc.scalar.activation(stage[:, j, 0:4, :].rearrange("p a d -> p (a d)"), PS[:, b, :], ACT.Copy
                                     ).then_inc(act_seq, 1)
                nc.scalar.activation(stage[0:NS, j, 4, :], PS[0:NS, b + 1, 0:P], ACT.Copy).then_inc(turn_copied, 1)
                act.wait_ge(act_seq, t + 1)
                act.wait_ge(turn_copied, t + 1)
                dst_p, dst_s = row_outputs(TURNS[t])
                act.dma_start(dst_p, stage[:, j, 0:4, :]).then_inc(turn_out[j], 16)
                act.dma_start(dst_s, stage[0:NS, j, 4, :]).then_inc(turn_out[j], 16)

            for s in range(S_POOL):
                if s + 2 < S_POOL:
                    high(s + 2, s % 2)
                if s == S_WI:
                    rows_out(0)
                if S_QI < s < S_K:
                    h = s - 1 - S_QI
                    for n, blk in enumerate(BLOCKS):
                        o, w = BLK_OFF[blk], (blk + 1) * P
                        act.wait_ge(idx_scored, 3 * h + n + 1)
                        if h:
                            act.wait_ge(idx_added, 3 * (h - 1) + n + 1)
                        nc.scalar.activation(pr[:, o:o + w], PS[:, 4 + n, 0:w], ACT.Relu, scale=IDX_SCALE
                                             ).then_inc(idx_relu, 1)
                if S_QI <= s < S_K:
                    h = s - S_QI
                    act.wait_ge(roped, s)
                    nc.scalar.activation(
                        qis[:, :, h * DT:(h + 1) * DT],
                        T2[:, s % 2, 16 + SEQ:16 + NT].rearrange("p (b q) -> p b q", b=DB), ACT.Copy
                    ).then_inc(qis_copied, 1)
                if s == S_K - 1:
                    h = IH - 1
                    for n, blk in enumerate(BLOCKS):
                        o, w = BLK_OFF[blk], (blk + 1) * P
                        act.wait_ge(idx_scored, 3 * h + n + 1)
                        act.wait_ge(idx_added, 3 * (h - 1) + n + 1)
                        nc.scalar.activation(pr[:, o:o + w], PS[:, 4 + n, 0:w], ACT.Relu, scale=IDX_SCALE
                                             ).then_inc(idx_relu, 1)
                    for b in range(DB):
                        for c in range(5):
                            w = 512 if c < 4 else DT
                            n = 9 * b + 4 + c
                            m = 5 * b + c
                            act.wait_ge(is_scored, m + 1)
                            if m >= 3:
                                act.wait_ge(is_summed, m - 2)
                            nc.scalar.activation(irelu[:, m % 3, 0:w], PS[:, 5 + n % 3, 0:w], ACT.Relu,
                                                 scale=IDX_SCALE).then_inc(is_relu, 1)
                if S_K <= s < S_V:
                    act.wait_ge(roped, s)
                    nc.scalar.activation(qkT[:, NH + s - S_K, :], T2[:, s % 2, 16:16 + NT], ACT.Copy
                                         ).then_inc(k_kept, 1)
                if S_K < s <= S_Q:
                    rows_out(s - S_K)
                if s > S_UP:
                    act.wait_ge(d_ready, s - S_UP)
                    act.dma_start(d_keep[:, (s - 1 - S_UP) * NT:(s - S_UP) * NT], rtmp[:, :]).then_inc(d_kept, 16)
                if s > S_UP:
                    for f in ([s - 1 - S_UP] if s < S_POOL - 1 else [NPOOL - 2, NPOOL - 1]):
                        act.wait_ge(u_turned, f + 1)
                        if f >= 2:
                            act.wait_ge(u_out[f % 2], 16 * (DB + 1) * (f // 2))
                        nc.scalar.activation(upt[:, f % 2, :], PS[0:STATE, 4 + f % 2, 0:P], ACT.Copy
                                             ).then_inc(act_seq, 1)
                        nc.scalar.activation(ust[:, f % 2, :], PS[0:NS, 4 + f % 2, P:2 * P], ACT.Copy
                                             ).then_inc(u_copied, 1)
                        if f < NPOOL - 2:
                            store_last_rows(act, f)

            UNITS = [(h, q) for h in range(NH) for q in range(4)]
            U = len(UNITS)
            act.wait_ge(slot_done, S_POOL)
            act.wait_ge(low_ready, S_POOL)
            for n in range(U + 3):
                if n < U:
                    w = (UNITS[n][1] + 1) * P
                    act.wait_ge(p_max, n + 1)
                    nc.scalar.activation(px[:, n % 3, 0:w], px[:, n % 3, 0:w], ACT.Exp, bias=small[:, 32 + n:33 + n],
                                         accum_out=small[:, 64 + n:65 + n]).then_inc(p_exp, 1)
                if 2 <= n < U + 2:
                    u = n - 2
                    w = (UNITS[u][1] + 1) * P
                    act.wait_ge(p_turned, u + 1)
                    if u >= 3:
                        act.wait_ge(p_out, u - 2)
                    nc.scalar.activation(pxt[:, u % 3, 0:w], PS[:, 3 + u % 3, 0:w], ACT.Copy).then_inc(p_copied, 1)
                if n >= 3:
                    u = n - 3
                    h, q = UNITS[u]
                    act.wait_ge(p_out, u + 1)
                    nc.scalar.activation(HH[:, NPOOL + h, q * P:(q + 1) * P], PS[:, 6 + u % 2, 0:P], ACT.Copy
                                         ).then_inc(p_high, 1)

            def query_high(b):
                act.wait_ge(out_read, 1)
                if not is_number(b, 0):
                    act.wait_ge(k_scored, b * (NCH + 1))
                nc.scalar.activation(diagonal(qhl[:, 0:NH * (2 * NS + DT)]), qkT[:, 0:NH, tokens(b, SEQ)], ACT.Copy, scale=ATT_SCALE
                                     ).then_inc(q_high, 1)

            def key_high(b, n):
                c = n // 2
                act.wait_ge(kt_turned, b * NPG + (n + 1))
                if not (is_number(b, 0) and c < 2):
                    act.wait_ge(k_scored, b * (NCH + 1) + (c - 1 if c >= 2 else c - 2))
                nc.scalar.activation(kth[:, c % 2, :, (n % 2) * PAGE:(n % 2 + 1) * PAGE],
                                     PS[:, 2 * (n % 2):2 * (n % 2) + 2, :].rearrange("p a (h k) -> p (a h) k", h=4),
                                     ACT.Copy).then_inc(kt_high, 1)

            def value_high(b, n):
                act.wait_ge(v_in[n % 4], b * (4 * NPG) + (16 * (n // 4 + 1) - 4 * NPG))
                last = is_number(b, DB)
                ring = 4 if last else 2
                if n < 2:
                    act.wait_ge(out_read, b)
                elif n < ring:
                    act.wait_ge(k_scored, DB * (NCH + 1))
                else:
                    act.wait_ge(v_used, b * NPG + (n + 1 - ring - NPG))
                nc.scalar.activation(value_halves(n, last)[0], vpage[:, n % 4, :], ACT.Copy).then_inc(v_high, 1)

            def exponent(b):
                act.wait_ge(s_max, b)
                nc.scalar.activation(prob[:, :], prob[:, :], ACT.Exp, bias=small[0:NS, 129:130],
                                     accum_out=small[0:NS, 130:131]).then_inc(s_exp, 1)

            def prob_high(b, g):
                act.wait_ge(pt_turned, b * 3 + (g - 2))
                if g == 0:
                    act.wait_ge(out_read, b)
                n0, n1 = GROUPS[g][0], min(GROUPS[g][1], NPG)
                nc.scalar.activation(pt[:, n0:n1, 0:NS],
                                     PS[:, 5, 0:(n1 - n0) * NS].rearrange("p (n r) -> p n r", r=NS), ACT.Copy
                                     ).then_inc(pt_high, 1)
                if g == 2:
                    nc.scalar.activation(ptn[:, 0:NS], PS[0:NS, 5, (n1 - n0) * NS:(n1 - n0 + 1) * NS], ACT.Copy
                                         ).then_inc(ptn_high, 1)

            def sequence(b, keys, values, ahead):
                if keys:
                    query_high(b)
                for c in range(NCH + 1):
                    if values and c == 1:
                        exponent(b)
                    for n in (2 * c, 2 * c + 1):
                        if keys and 0 < c < NCH:
                            key_high(b, n)
                    if values and c in (1, 2):
                        prob_high(b, c - 1)
                    for n in (2 * c - 2, 2 * c - 1):
                        if values and c >= 1:
                            value_high(b, n)
                        if ahead and n == NPG - 2:
                            key_high(b, NPG)
                    if values and c == 3:
                        prob_high(b, 2)
                    if not keys and NCH // 2 <= c < NCH:
                        for f in (2 * c - NCH, 2 * c - NCH + 1):
                            if f == 0 or f == NPOOL // 2:
                                act.wait_ge(d_back, 16 * (1 + f // 4))
                            nc.scalar.activation(DH[:, f, :], dback[:, f, :], ACT.Copy).then_inc(df_high, 1)
                if not keys:
                    for i in range(2):
                        act.wait_ge(v_low[i], DB * NPG // 2)
                    high(S_POOL, 0)
                    high(S_OUT, 1)
                if values:
                    act.wait_ge(s_inv, 2 * b)
                    act.wait_ge(s_out, b)
                    nc.scalar.activation(orow[:, :], PS[NS:2 * NS, 6:8, :].rearrange("p a n -> p (a n)"), ACT.Copy,
                                         scale=small[NS:2 * NS, 131:132]).then_inc(low_out, 1)
                if ahead:
                    key_high(b, NPG + 1)
                if values:
                    act.wait_ge(o_turned, b)
                    cols = tokens(b, SEQ - DT)
                    nc.scalar.activation(HH[:, NPOOL:2 * NPOOL, cols], diagonal(turned_out), ACT.Copy
                                         ).then_inc(sy_high, 1)

            nc.scalar.activation(knh[:, :, :], qkT[:, NH:2 * NH, SEQ:NT], ACT.Copy).then_inc(kn_high, 1)
            act.wait_ge(vnew_in, 16)
            act.wait_ge(out_read, 1)
            nc.scalar.activation(vnh[:, :], vraw[:, :], ACT.Copy).then_inc(vn_high, 1)
            act.wait_ge(vn_low, 1)
            key_high(0, 0)
            key_high(0, 1)
            sequence(0, True, False, True)
            with act.Fori(1, DB - 1) as b:
                sequence(b, True, True, True)
            sequence(DB - 1, True, True, False)
            sequence(DB, False, True, False)

            act.wait_ge(df_low, NPOOL)
            for o in range(NPOOL):
                act.wait_ge(pool_done, o + 1) if o < NPOOL - 1 else act.wait_ge(slot_done, S_OUT)
                nc.scalar.activation(halves(HH[:, o, :]), pair(o), ACT.Copy, scale=gains[:, 3, o:o + 1]
                                     ).then_inc(pool_high, 1)

            high(S_OUT + 1, 0)
            for o in range(KT):
                high(S_OUT + 2 + o, (S_OUT + o) % 2)
                act.wait_ge(psum_read, G_OUT + o + 1)
                square(1, o)
            root(1)
            norm_highs(1)

            def ff_step(i, j, more, more_chunks=True):
                if j >= 2 * FT and not more_chunks:
                    for o in range(4 * (j - 2 * FT), 4 * (j - 2 * FT) + 3):
                        act.wait_ge(psum_read, G_FF + READ_CHUNK * i + FT + o + 1)
                        square(2, o)
                if more:
                    p = (S_FF + j) % 2
                    act.wait_ge(raw_in[p], 16 * (PER_CHUNK // 2) * i + 16 * ((S_FF + j + 2) // 2 + 1))
                    act.wait_ge(slot_done, PER_CHUNK * i + (S_FF + j + 1))
                    nc.scalar.activation(wh[:, p, :], raw[:, p, :], ACT.Copy).then_inc(high_ready, 1)
                if j >= 2 * FT:
                    if not more_chunks:
                        o = 4 * (j - 2 * FT) + 3
                        act.wait_ge(psum_read, G_FF + READ_CHUNK * i + FT + o + 1)
                        square(2, o)
                    return
                f = j // 2
                if j % 2 == 0:
                    act.wait_ge(slot_done, PER_CHUNK * i + (S_FF + j + 1))
                    act.wait_ge(psum_read, READ_CHUNK * i + G_FF + (f - 1 if f >= 2 else 0))
                    nc.scalar.activation(halves(sg[:, f % 2, :]), pair(j), ACT.Silu).then_inc(silu_done, 1)
                else:
                    act.wait_ge(psum_read, READ_CHUNK * i + (G_FF + f + 1))
                    nc.scalar.activation(GH[:, f, :], hid[:, f % 2, :], ACT.Copy).then_inc(hid_high, 1)

            with act.Fori(0, CHUNKS - 1) as i:
                for j in range(PER_CHUNK):
                    ff_step(i, j, True)
            for j in range(PER_CHUNK):
                ff_step(CHUNKS - 1, j, j + 2 < PER_CHUNK, False)

            root(2)
            for g in range(KT):
                act.wait_ge(y_turned, g + 1)
                nc.scalar.activation(yrow[:, 0:4, g * P:(g + 1) * P],
                                     PS[:, 2 * (g % 2), :].rearrange("p (a d) -> p a d", a=4), ACT.Copy
                                     ).then_inc(y_copied_act, 1)

            for t in range(2):
                act.wait_ge(turn_out[t], 32 * len(TURNS[t::2]))
                act.wait_ge(u_out[t], 16 * (DB + 1) * (NPOOL // 2))

        @block.vector
        def _(dve):
            link = Chain(dve, dve_seq)
            v = nc.vector
            link(v.memset(T2[:, :, 0:16], 0.0))
            link(v.memset(stats[:, :], 1.0))
            for n in range(1, 20, 2):
                t, f = n // 4, 4 * (n % 4)
                dve.wait_ge(x_turned, n + 1)
                v.tensor_copy(XT[:, f:f + 4, t * P:t * P + ROWS[t]],
                              PS[:, 4 + n % 4, :].rearrange("p (j t) -> p j t", j=4)[:, :, 0:ROWS[t]]
                              ).then_inc(x_copied_dve, 1)

            def add_square(m, f):
                dve.wait_ge(sq_ready, KT * (m - 1) + f + 1)
                if f == 0:
                    v.tensor_copy(ss[:, :], sq[:, 0, :]).then_inc(sq_added, 1)
                else:
                    dve.wait_ge(sq_added, KT * (m - 1) + f)
                    v.tensor_tensor(ss[:, :], ss[:, :], sq[:, f % 2, :], ALU.add).then_inc(sq_added, 1)

            def norm(m):
                if m == 0:
                    dve.wait_ge(row_squared, 5)
                    link(v.tensor_scalar(stats[:, 0:5], stats[:, 0:5], 1.0 / D, EPS, ALU.mult, ALU.add))
                else:
                    dve.wait_ge(col_summed, m)
                    link(v.tensor_scalar(stats[:, 0:4], PS[:, 4, 0:4], 1.0 / D, EPS, ALU.mult, ALU.add))
                    link(v.tensor_scalar(stats[0:NS, 4:5], PS[0:NS, 4, 4:5], 1.0 / D, EPS, ALU.mult, ALU.add))
                v.reciprocal(stats[:, 0:5], stats[:, 0:5]).then_inc(inv_ready, 1)
                dve.wait_ge(rstd_ready, m + 1)
                for t in range(5):
                    v.tensor_scalar(spread[:, t, :], ident, stats[:, t:t + 1], None, ALU.mult).then_inc(spread_ready, 1)
                if m == 0:
                    dve.wait_ge(x_copied_act, 10)
                    dve.wait_ge(x_copied_dve, 10)
                    dve.wait_ge(gains_ready, 1)
                dve.wait_ge(rstd_bcast, m + 1)

                def scaled(f):
                    if f >= 4:
                        if m < 2:
                            dve.wait_ge(*low_of(m, f - 4))
                        else:
                            dve.wait_ge(y_turned, f - 3)
                    v.scalar_tensor_tensor(out=xn[:, f % 4, :], in0=XT[:, f, :], scalar=gains[:, m, f:f + 1],
                                           in1=rstd, op0=ALU.mult, op1=ALU.mult).then_inc(xn_ready, 1)

                for f in range(2):
                    scaled(f)
                for f in range(KT):
                    if f + 2 < KT:
                        scaled(f + 2)
                    if m < 2 and by_dve(f):
                        dve.wait_ge(norm_high, KT * m + f + 1)
                        v.tensor_tensor(HL[:, f, :], xn[:, f % 4, :], HH[:, f, :].bitcast(F32), ALU.subtract
                                        ).then_inc(norm_low[1], 1)
                    if m == 2:
                        dve.wait_ge(y_turned, f + 1)
                        v.tensor_copy(yrow[0:NS, 4, f * P:(f + 1) * P], PS[0:NS, 2 * (f % 2) + 1, 0:P]
                                      ).then_inc(y_copied_dve, 1)

            dve.wait_ge(gains_turned, 1)
            v.tensor_copy(gains[:, :, :].rearrange("p n k -> p (n k)")[:, 0:3 * KT + NPOOL],
                          PS[:, 3, 0:3 * KT + NPOOL]).then_inc(gains_ready, 1)
            norm(0)
            dve.wait_ge(const_in, 16)

            cos, sin = cst[:, K_COS:K_COS + NT], cst[:, K_SIN:K_SIN + NT]

            link(v.memset(pscore[:, :], 0.0))
            for blk in BLOCKS:
                o = BLK_OFF[blk] + blk * P
                link(v.tensor_copy(pscore[:, o:o + P], cst[:, K_TRI:K_TRI + P]))

            def idx_add(h):
                for n, blk in enumerate(BLOCKS):
                    o, w = BLK_OFF[blk], (blk + 1) * P
                    dve.wait_ge(idx_relu, 3 * h + n + 1)
                    if h:
                        dve.wait_ge(idx_added, 3 * (h - 1) + n + 1)
                    v.scalar_tensor_tensor(out=pscore[:, o:o + w], in0=pr[:, o:o + w], scalar=wtok[:, blk, h:h + 1],
                                           in1=pscore[:, o:o + w], op0=ALU.mult, op1=ALU.add).then_inc(idx_added, 1)

            def sample_indexer():
                for b in range(DB):
                    for c in range(4):
                        n = 9 * b + c
                        dve.wait_ge(ik_turned, 4 * b + c + 1)
                        if b == 0 and c == 0:
                            dve.wait_ge(x_kept, 16)
                        if b >= 2:
                            dve.wait_ge(is_scored, 5 * (b - 1))
                        v.tensor_copy(ikT[:, b % 2, c * 512:(c + 1) * 512], PS[:, 5 + n % 3, :]).then_inc(ik_copied, 1)
                    v.tensor_copy(ikT[:, b % 2, PAST:NKEY], kiT[:, SEQ + b * DT:SEQ + (b + 1) * DT]
                                  ).then_inc(ik_new, 1)
                dve.wait_ge(is_summed, 5 * DB)
                v.tensor_copy(sscore[:, 0:PAST].rearrange("p (c n) -> p c n", c=4), PS[0:NS, 0:4, :])
                v.tensor_tensor(sscore[:, PAST:NKEY], PS[0:NS, 4, 0:DT], cst[0:NS, K_NEW:K_NEW + DT], ALU.add
                                ).then_inc(ss_copied, 1)
                dve.wait_ge(ss_copied, 1)

            def sample_round():
                link(v.max(small[0:NS, 0:8], sscore[:, :]))
                link(v.match_replace(sscore[:, :], small[0:NS, 0:8], sscore[:, :], TAKEN))

            def prompt_round():
                for n, blk in enumerate(BLOCKS):
                    o, w = BLK_OFF[blk], (blk + 1) * P
                    link(v.max(small[:, 8 + 8 * n:16 + 8 * n], pscore[:, o:o + w]))
                for n, blk in enumerate(BLOCKS):
                    o, w = BLK_OFF[blk], (blk + 1) * P
                    link(v.match_replace(pscore[:, o:o + w], small[:, 8 + 8 * n:16 + 8 * n], pscore[:, o:o + w],
                                         TAKEN))

            def pooled(f):
                g = f // 2
                e = T2[:, f % 2, :]
                if f:
                    dve.wait_ge(d_ready, f)
                v.tensor_copy(ES[:, :, 0:STATE], stateT[:, f, :].rearrange("p (b t) -> p b t", b=DB))
                link(v.tensor_copy(ES[:, :, STATE:STATE + DT], e[:, 16 + SEQ:16 + NT].rearrange("p (b t) -> p b t", b=DB)))
                cur_p, cur_s = e[:, 0:16 + SEQ], ES[:, :, :]
                for m in range(g + 1):
                    sh = 1 << m
                    o = (1 << (m + 1)) - 1
                    nxt_p, nxt_s = win[:, m % 2, :], wins[:, m % 2, :, :]
                    v.tensor_tensor(nxt_p[:, o:16 + SEQ], cur_p[:, o:16 + SEQ], cur_p[:, o - sh:16 + SEQ - sh], ALU.add)
                    link(v.tensor_tensor(nxt_s[:, :, o:STATE + DT], cur_s[:, :, o:STATE + DT],
                                         cur_s[:, :, o - sh:STATE + DT - sh], ALU.add))
                    cur_p, cur_s = nxt_p, nxt_s
                w = WINDOWS[g]
                link(v.tensor_tensor(cur_p[:, 16:16 + STATE], cur_p[:, 16:16 + STATE],
                                     cst[:, K_CNT + 16 * g:K_CNT + 16 * g + STATE], ALU.mult))
                if f:
                    dve.wait_ge(d_kept, 16 * f)
                dp = rtmp
                v.scalar_tensor_tensor(out=dp[:, 0:SEQ], in0=cur_p[:, 16:16 + SEQ], scalar=1.0 / w,
                                       in1=e[:, 16:16 + SEQ], op0=ALU.mult, op1=ALU.subtract)
                v.scalar_tensor_tensor(out=dp[:, SEQ:NT].rearrange("p (b t) -> p b t", b=DB),
                                       in0=cur_s[:, :, STATE:STATE + DT], scalar=1.0 / w,
                                       in1=ES[:, :, STATE:STATE + DT], op0=ALU.mult, op1=ALU.subtract
                                       ).then_inc(d_ready, 1)

            rounds = 0
            for s in range(S_POOL):
                dve.wait_ge(slot_done, s + 1)
                j = s % 2
                if s == S_KI:
                    dst = kiT[:, :]
                elif s >= S_UP or S_V <= s < S_Q or s == S_WI:
                    dst = None
                elif s >= S_Q:
                    dst = qkT[:, s - S_Q, :]
                else:
                    dst = T2[:, j, 16:16 + NT]
                if S_QI + 2 <= s < S_Q:
                    if s < S_K + 2:
                        dve.wait_ge(idx_scored, 3 * (min(s, S_K + 1) - 2 - S_QI + 1))
                        dve.wait_ge(qis_copied, min(s, S_K + 1) - 2 - S_QI + 1)
                    else:
                        dve.wait_ge(turned, s - S_K)
                        dve.wait_ge(k_kept, min(s - 1 - S_K, NH))
                if s == S_Q:
                    dve.wait_ge(is_summed, 5 * DB)
                if s == S_WI:
                    v.tensor_copy(halves(wiT[:, :]), pair(s, IH)).then_inc(psum_read, 1)
                elif dst is not None:
                    src = pair(s)
                    n_roped = s - NH if s >= S_Q else s if s else 1
                    if s:
                        dve.wait_ge(roped, n_roped - 1)
                    v.tensor_tensor(halves(rtmp[64:128, :]), src[0:64], halves(sin[0:64]), ALU.mult)
                    v.tensor_tensor(halves(rtmp[0:64, :]), src[64:128], halves(sin[64:128]), ALU.mult)
                    v.tensor_tensor(halves(dst), src, halves(cos), ALU.mult).then_inc(psum_read, 1)
                    dve.wait_ge(psum_read, s + 1)
                    v.tensor_tensor(dst, dst, rtmp[:, :], ALU.add).then_inc(roped, 1)
                elif s < S_Q:
                    v.tensor_copy(halves(T2[:, j, 16:16 + NT]), pair(s)).then_inc(psum_read, 1)
                else:
                    f = s - S_UP
                    if f >= 2:
                        dve.wait_ge(u_turned, f - 1)
                    else:
                        dve.wait_ge(turned, 2 * NH + 1)
                    v.tensor_copy(halves(T2[:, j, 16:16 + NT]), pair(s)).then_inc(psum_read, 1)
                    dve.wait_ge(psum_read, s + 1)
                    pooled(f)
                if s == S_UP - 1:
                    dve.wait_ge(state_turned, 1)
                    link(v.tensor_copy(stateT[:, :, :].rearrange("p (a f) r -> p a (f r)", a=2),
                                       PS[:, 6:8, 0:4 * DB * STATE]))
                if s == S_QI:
                    dve.wait_ge(wi_turned, 1)
                    v.memset(wrow[:, :], 0.0)
                    link(v.tensor_copy(wtok[:, 1:4, :], PS[:, 7, IH:4 * IH].rearrange("p (a h) -> p a h", a=3)))
                    v.tensor_tensor(wrow[:, :].rearrange("p (b x) -> p b x", b=DB)[:, :, 0:DT],
                                    PS[:, 7, 128:128 + NS].rearrange("p (b q) -> p b q", b=DB),
                                    cst[:, K_DIAG:K_DIAG + NS].rearrange("p (b q) -> p b q", b=DB), ALU.mult
                                    ).then_inc(wrow_ready, 1)
                if S_QI < s < S_K:
                    idx_add(s - 1 - S_QI)
                if s == S_K - 1:
                    idx_add(IH - 1)
                    sample_indexer()
                if S_K <= s < S_Q:
                    sample_round()
                    prompt_round()
                if S_Q <= s < S_UP:
                    sample_round()
                    sample_round()
            link(v.tensor_scalar(pscore[:, :], pscore[:, :], TAKEN, HIDE, ALU.not_equal, ALU.mult))
            UNITS = [(h, q) for h in range(NH) for q in range(4)]
            U = len(UNITS)
            dve.wait_ge(slot_done, S_POOL)
            dve.wait_ge(low_ready, S_POOL)
            for n in range(U + 4):
                if n < U:
                    h, q = UNITS[n]
                    w = (q + 1) * P
                    mask = pscore[:, BLK_OFF[q]:BLK_OFF[q] + w] if q else cst[:, K_TRI:K_TRI + P]
                    dve.wait_ge(p_scored, n + 1)
                    if n >= 3:
                        dve.wait_ge(p_turned, n - 2)
                    link(v.tensor_tensor_reduce(out=px[:, n % 3, 0:w], in0=PS[:, n % 3, 0:w], in1=mask,
                                                scale=ATT_SCALE, scalar=-3.0e38, op0=ALU.add, op1=ALU.max,
                                                accum_out=small[:, n:n + 1]))
                    v.tensor_scalar(small[:, 32 + n:33 + n], small[:, n:n + 1], -1.0, None, ALU.mult
                                    ).then_inc(p_max, 1)
                if 1 <= n <= U:
                    u = n - 1
                    w = (UNITS[u][1] + 1) * P
                    dve.wait_ge(p_exp, u + 1)
                    link(v.reciprocal(small[:, 96 + u:97 + u], small[:, 64 + u:65 + u]))
                    v.tensor_scalar(px[:, u % 3, 0:w], px[:, u % 3, 0:w], small[:, 96 + u:97 + u], None, ALU.mult
                                    ).then_inc(p_norm, 1)
                if n >= 4:
                    u = n - 4
                    h, q = UNITS[u]
                    dve.wait_ge(p_high, u + 1)
                    v.tensor_tensor(HL[:, NPOOL + h, q * P:(q + 1) * P], PS[:, 6 + u % 2, 0:P],
                                    HH[:, NPOOL + h, q * P:(q + 1) * P].bitcast(F32), ALU.subtract
                                    ).then_inc(p_low, 1)

            def query_low(b):
                dve.wait_ge(q_high, b + 1)
                cols = tokens(b, SEQ)
                v.scalar_tensor_tensor(out=diagonal(qhl[:, NS:]), in0=qkT[:, 0:NH, cols], scalar=ATT_SCALE,
                                       in1=diagonal(qhl[:, 0:NH * (2 * NS + DT)].bitcast(F32)), op0=ALU.mult, op1=ALU.subtract
                                       ).then_inc(q_low, 1)
                own = tokens(b, 0)
                v.tensor_copy(pick[:, :].rearrange("r (h q) -> r h q", h=NH),
                              cst[0:NS, own].rearrange("r (o q) -> r o q", o=1).broadcast_to([NS, NH, DT])
                              ).then_inc(pick_ready, 1)

            def key_low(b, n):
                c = n // 2
                dve.wait_ge(kt_high, b * NPG + (n + 1))
                place = (slice(None), c % 2, slice(None), slice((n % 2) * PAGE, (n % 2 + 1) * PAGE))
                v.tensor_tensor(ktl[place], PS[:, 2 * (n % 2):2 * (n % 2) + 2, :].rearrange(
                    "p a (h k) -> p (a h) k", h=4), kth[place].bitcast(F32), ALU.subtract).then_inc(kt_low, 1)

            def value_low(b, n):
                dve.wait_ge(v_high, b * NPG + (n + 1 - NPG))
                high, low = value_halves(n, is_number(b, DB))
                v.tensor_tensor(low, vpage[:, n % 4, :], high.bitcast(F32), ALU.subtract).then_inc(v_low[1], 1)

            def scores(b, c):
                dve.wait_ge(k_scored, b * (NCH + 1) + (c + 1))
                if not is_number(b, 0):
                    dve.wait_ge(pt_turned, b * 3 + (c // 3 - 2))
                w = CHUNK if c < NCH else NS
                place = prob[:, c * CHUNK:c * CHUNK + w]
                v.tensor_copy(place, PS[NS:2 * NS, 4, 0:w]).then_inc(s_low_copied, 1)
                dve.wait_ge(s_low_copied, b * (NCH + 1) + (c + 1))
                v.tensor_tensor(place, PS[0:NS, 4, 0:w], place, ALU.add).then_inc(s_copied, 1)
                dve.wait_ge(s_copied, b * (NCH + 1) + (c + 1))
                v.tensor_reduce(small[0:NS, c:c + 1], prob[:, c * CHUNK:c * CHUNK + w], AX.X, ALU.max
                                ).then_inc(part_max, 1)

            def maxima(b):
                dve.wait_ge(part_max, b * (NCH + 1))
                link(v.tensor_reduce(small[0:NS, 128:129], small[0:NS, 0:NCH + 1], AX.X, ALU.max))
                v.tensor_scalar(small[0:NS, 129:130], small[0:NS, 128:129], -1.0, None, ALU.mult).then_inc(s_max, 1)

            def prob_low(b, g):
                dve.wait_ge(pt_high, b * 3 + (g - 2))
                n0, n1 = GROUPS[g][0], min(GROUPS[g][1], NPG)
                if g == 2:
                    dve.wait_ge(ptn_high, b)
                v.tensor_tensor(pt[:, n0:n1, NS:2 * NS],
                                PS[:, 5, 0:(n1 - n0) * NS].rearrange("p (n r) -> p n r", r=NS),
                                pt[:, n0:n1, 0:NS].bitcast(F32), ALU.subtract).then_inc(pt_low, 1)
                if g == 2:
                    v.tensor_tensor(ptn[:, NS:2 * NS], PS[0:NS, 5, (n1 - n0) * NS:(n1 - n0 + 1) * NS],
                                    ptn[:, 0:NS].bitcast(F32), ALU.subtract).then_inc(ptn_low, 1)

            def sequence(b, keys, values, ahead):
                if values:
                    maxima(b)
                if keys:
                    query_low(b)
                for c in range(NCH + 1):
                    for n in (2 * c, 2 * c + 1):
                        if keys and 0 < c < NCH:
                            key_low(b, n)
                    if values and c in (1, 2):
                        prob_low(b, c - 1)
                    if keys and c:
                        scores(b, c - 1)
                    if ahead and c == NCH:
                        key_low(b, NPG)
                    if values and c:
                        value_low(b, 2 * c - 1)
                    if values and c == 3:
                        prob_low(b, 2)
                    if not keys and NCH // 2 <= c < NCH:
                        for f in (2 * c - NCH, 2 * c - NCH + 1):
                            dve.wait_ge(df_high, f + 1)
                            v.tensor_tensor(DL[:, f, :], dback[:, f, :], DH[:, f, :].bitcast(F32), ALU.subtract
                                            ).then_inc(df_low, 1)
                if values:
                    dve.wait_ge(s_exp, b)
                    v.reciprocal(small[NS:2 * NS, 131:132], small[0:NS, 130:131]).then_inc(s_inv, 1)
                    v.reciprocal(small[0:NS, 131:132], small[0:NS, 130:131]).then_inc(s_inv, 1)
                    dve.wait_ge(s_inv, 2 * b)
                    dve.wait_ge(low_out, b)
                    v.scalar_tensor_tensor(out=orow[:, :], in0=PS[0:NS, 6:8, :].rearrange("p a n -> p (a n)"),
                                           scalar=small[0:NS, 131:132], in1=orow[:, :], op0=ALU.mult, op1=ALU.add
                                           ).then_inc(o_ready, 1)
                if ahead:
                    key_low(b, NPG + 1)
                if keys:
                    scores(b, NCH)
                if values:
                    dve.wait_ge(sy_high, b)
                    cols = tokens(b, SEQ - DT)
                    v.tensor_tensor(HL[:, NPOOL:2 * NPOOL, cols], diagonal(turned_out),
                                    HH[:, NPOOL:2 * NPOOL, cols].bitcast(F32), ALU.subtract).then_inc(out_read, 1)

            dve.wait_ge(p_low, U)
            dve.wait_ge(d_kept, 16 * NPOOL)
            for t in range(2):
                dve.wait_ge(u_out[t], 16 * (DB + 1) * (NPOOL // 2))
            v.memset(qhl[:, :].bitcast(F32), 0.0).then_inc(out_read, 1)
            for t in range(2):
                dve.wait_ge(turn_out[t], 32 * len(TURNS[t::2]))
            v.tensor_scalar(maskS[:, :], sscore[:, :], TAKEN, HIDE, ALU.not_equal, ALU.mult).then_inc(bias_ready, 1)
            dve.wait_ge(bias_ready, 1)
            v.tensor_tensor(maskN[:, :].rearrange("r (b t) -> r b t", b=DB),
                            maskS[:, PAST:NKEY].bitcast(F32).rearrange("r (o t) -> r o t", o=1
                                                                      ).broadcast_to([NS, DB, DT]),
                            cst[0:NS, K_OTHER:K_OTHER + NS].rearrange("r (b t) -> r b t", b=DB), ALU.add
                            ).then_inc(mask_ready, 1)
            dve.wait_ge(kn_high, 1)
            v.tensor_tensor(knl[:, :, :], qkT[:, NH:2 * NH, SEQ:NT], knh[:, :, :].bitcast(F32), ALU.subtract
                            ).then_inc(kn_low, 1)
            dve.wait_ge(vn_high, 1)
            v.tensor_tensor(vnl[:, :], vraw[:, :], vnh[:, :].bitcast(F32), ALU.subtract).then_inc(vn_low, 1)
            key_low(0, 0)
            key_low(0, 1)
            sequence(0, True, False, True)
            before = link.n
            with dve.Fori(1, DB - 1) as b:
                link.more = b - 1
                sequence(b, True, True, True)
            link.more = 0
            assert link.n == before + 1
            link.n = before + DB - 2
            sequence(DB - 1, True, True, False)
            sequence(DB, False, True, False)

            for o in range(NPOOL):
                dve.wait_ge(pool_high, o + 1)
                v.scalar_tensor_tensor(out=halves(HL[:, o, :]), in0=pair(o), scalar=gains[:, 3, o:o + 1],
                                       in1=halves(HH[:, o, :].bitcast(F32)), op0=ALU.mult, op1=ALU.subtract
                                       ).then_inc(psum_read, 1)

            for o in range(KT):
                if o % 4 == 0:
                    dve.wait_ge(x_back[o // 4], 16)
                dve.wait_ge(slot_done, S_OUT + o + 1)
                v.tensor_tensor(halves(XT[:, o, :]), halves(XT[:, o, :]), pair(G_OUT + o), ALU.add
                                ).then_inc(psum_read, 1)
                if o:
                    add_square(1, o - 1)
            add_square(1, KT - 1)
            norm(1)

            def feed_forward(i, last=False):
                for f in range(FT):
                    dve.wait_ge(slot_done, PER_CHUNK * i + (S_FF + 2 * f + 2))
                    dve.wait_ge(silu_done, FT * i + (f + 1))
                    if f >= 2:
                        dve.wait_ge(hid_low, FT * i + (f - 1))
                    v.tensor_tensor(halves(hid[:, f % 2, :]), halves(sg[:, f % 2, :]), pair(1), ALU.mult
                                    ).then_inc(psum_read, 1)
                    dve.wait_ge(hid_high, FT * i + (f + 1))
                    v.tensor_tensor(GL[:, f, :], hid[:, f % 2, :], GH[:, f, :].bitcast(F32), ALU.subtract
                                    ).then_inc(hid_low, 1)
                for o in range(KT):
                    if o % 4 == 3:
                        dve.wait_ge(slot_done, PER_CHUNK * i + (S_FF + 2 * FT + o // 4 + 1))
                    else:
                        dve.wait_ge(down_done, 12 * i + (3 * (o // 4) + o % 4 + 1))
                    v.tensor_tensor(halves(XT[:, o, :]), halves(XT[:, o, :]), pair(o), ALU.add).then_inc(psum_read, 1)
                    if last and o:
                        add_square(2, o - 1)

            with dve.Fori(0, CHUNKS - 1) as i:
                feed_forward(i)
            feed_forward(CHUNKS - 1, True)
            add_square(2, KT - 1)
            norm(2)


_INS = ["x_prompt", "x_sample", "cache_k", "cache_v", "cache_idx_k", "state_pool", "page_table", "g_mix", "w_in",
        "w_pool", "s_pool", "w_out", "g_ffn", "w_gate", "w_up", "w_down", "g_final"]
_OUTS = [(1, SEQ, D), (DB, DT, D), (1, 1, SEQ, NH, HD), (1, 1, SEQ, NH, HD), (1, 1, SEQ, HD), (1, 1, STATE, POOL_W),
         (1, DB, DT, NH, HD), (1, DB, DT, NH, HD), (1, DB, DT, HD), (1, DB, STATE, POOL_W)]


def kernel(**inputs):
    import numpy as np
    import concourse.bacc as bacc
    from concourse.bass_utils import run_bass_kernel_spmd

    nc = bacc.Bacc("TRN2", target_bir_lowering=False, num_devices=1)
    arrays = {f"in_{n}": np.ascontiguousarray(inputs[n]) for n in _INS}
    arrays["in_const"] = constants()
    args = [nc.dram_tensor(n, a.shape, mybir.dt.from_np(a.dtype), kind="ExternalInput").ap()
            for n, a in arrays.items()]
    outs = [nc.dram_tensor(f"out_{i}", s, F32, kind="ExternalOutput").ap() for i, s in enumerate(_OUTS)]
    build(nc, *args, outs)
    r = run_bass_kernel_spmd(nc, [arrays], core_ids=[0])
    return tuple(r.results[0][f"out_{i}"] for i in range(len(_OUTS)))
```
